# Optimizing a Trainium2 kernel written in Bass

```python
import jax, jax.numpy as jnp
from jax import lax
import numpy as np
import math

D_MODEL = 1024
BATCH = 1
SEQ = 256
DEPTH = 2

N_MIXERS = 2
N_POOL_GROUPS = 4
POOL_GROUP = D_MODEL // N_POOL_GROUPS
POOL_WINDOWS = (2, 4, 8, 16)
N_HEADS = 16
QK_NOPE = 64
QK_ROPE = 32
V_HEAD = 64
Q_LORA = D_MODEL // 4
KV_LORA = D_MODEL // 8
ROPE_THETA = 10000.0
D_FF = 11 * D_MODEL // 4
Q_BLOCK = 128
EPS = 1e-6
N_MOD = 9
N_POOL_LAYERS = (DEPTH + 1) // 2
N_MLA_LAYERS = DEPTH // 2
ATTN_SCALE = (QK_NOPE + QK_ROPE) ** -0.5


def rmsnorm(x, g):
    xf = x.astype(jnp.float32)
    y = xf * lax.rsqrt(jnp.mean(xf * xf, axis=-1, keepdims=True) + EPS)
    return (y * g.astype(jnp.float32)).astype(x.dtype)

def swiglu(h, w_in, w_out):
    gate, up = jnp.split(h @ w_in, 2, axis=-1)
    return (jax.nn.silu(gate) * up) @ w_out

def centred_mean(x, window):
    s = x.shape[1]
    cs = lax.cumsum(x.astype(jnp.float32), axis=1)
    cs = jnp.pad(cs, ((0, 0), (1, 0), (0, 0)))
    t = jnp.arange(s)
    hi = jnp.clip(t + window // 2, 0, s)
    lo = jnp.clip(t - window // 2, 0, s)
    tot = jnp.take(cs, hi, axis=1) - jnp.take(cs, lo, axis=1)
    cnt = (hi - lo).astype(jnp.float32)[None, :, None]
    return (tot / cnt).astype(x.dtype)

def pool_mixer(h, w, b, scale):
    B, S, _ = h.shape
    hg = h.reshape(B, S, N_POOL_GROUPS, POOL_GROUP)
    pooled = jnp.stack([centred_mean(hg[:, :, g], POOL_WINDOWS[g]) for g in range(N_POOL_GROUPS)], axis=2)
    y = jnp.einsum('bsgc,gcd->bsgd', pooled - hg, w) + b
    return y.reshape(B, S, D_MODEL) * scale

def rope_tables(s, dtype):
    inv = 1.0 / (ROPE_THETA ** (jnp.arange(0, QK_ROPE, 2, dtype=jnp.float32) / QK_ROPE))
    ang = jnp.arange(s, dtype=jnp.float32)[:, None] * inv[None, :]
    return jnp.cos(ang).astype(dtype), jnp.sin(ang).astype(dtype)

def apply_rope(x, cos, sin):
    x1, x2 = jnp.split(x, 2, axis=-1)
    return jnp.concatenate([x1 * cos - x2 * sin, x2 * cos + x1 * sin], axis=-1)

def mla_mixer(h, w_in, q_norm, kv_norm, w_uq, w_uk, w_uv, w_o, cos, sin):
    B, S, _ = h.shape
    lat = h @ w_in
    c_q, c_kv, k_r = jnp.split(lat, [Q_LORA, Q_LORA + KV_LORA], axis=-1)
    c_q = rmsnorm(c_q, q_norm)
    c_kv = rmsnorm(c_kv, kv_norm)
    q = jnp.einsum('bsc,chd->bshd', c_q, w_uq)
    q_nope, q_rope = q[..., :QK_NOPE], q[..., QK_NOPE:]
    q_rope = apply_rope(q_rope, cos[:, None, :], sin[:, None, :]) * ATTN_SCALE
    k_rope = apply_rope(k_r, cos, sin)
    q_lat = jnp.einsum('bshn,chn->bshc', q_nope, w_uk) * ATTN_SCALE
    nb = S // Q_BLOCK
    qlb = q_lat.reshape(B, nb, Q_BLOCK, N_HEADS, KV_LORA).transpose(1, 0, 2, 3, 4)
    qrb = q_rope.reshape(B, nb, Q_BLOCK, N_HEADS, QK_ROPE).transpose(1, 0, 2, 3, 4)

    def block(args):
        ql, qr = args
        s = (jnp.einsum('bqhc,bkc->bhqk', ql, c_kv)
             + jnp.einsum('bqhr,bkr->bhqk', qr, k_rope))
        p = jax.nn.softmax(s.astype(jnp.float32), axis=-1).astype(c_kv.dtype)
        return jnp.einsum('bhqk,bkc->bqhc', p, c_kv)

    o_lat = lax.map(block, (qlb, qrb))
    o_lat = o_lat.transpose(1, 0, 2, 3, 4).reshape(B, S, N_HEADS, KV_LORA)
    o = jnp.einsum('bshc,chv->bshv', o_lat, w_uv)
    return o.reshape(B, S, N_HEADS * V_HEAD) @ w_o

def modulated_sublayer(x, mod, g_pre, g_post, fn, weight):
    shift, scale, gate = mod[:, 0], mod[:, 1], mod[:, 2]
    h = rmsnorm(x, g_pre) * (1.0 + scale) + shift
    y = rmsnorm(fn(h), g_post)
    return x + weight * (1.0 + gate) * y

def first_inputs(seed: int = 0) -> dict:
    key = jax.random.key(seed)
    ks = jax.random.split(key, 20)
    n = jax.random.normal
    f32 = jnp.float32
    return {
        "x": n(ks[0], (BATCH, SEQ, D_MODEL), f32),
        "c": n(ks[1], (BATCH, D_MODEL), f32),
        "ada_w": n(ks[2], (DEPTH, D_MODEL, N_MOD * D_MODEL), f32) * (0.5 * D_MODEL ** -0.5),
        "ada_b": n(ks[3], (DEPTH, N_MOD * D_MODEL), f32) * 0.01,
        "norm_g": 1.0 + 0.05 * n(ks[4], (DEPTH, 6, D_MODEL), f32),
        "ffn_w_in": n(ks[5], (DEPTH, 2, D_MODEL, 2 * D_FF), f32) * D_MODEL ** -0.5,
        "ffn_w_out": n(ks[6], (DEPTH, 2, D_FF, D_MODEL), f32) * D_FF ** -0.5,
        "pool_w": n(ks[7], (N_POOL_LAYERS, N_POOL_GROUPS, POOL_GROUP, POOL_GROUP), f32) * POOL_GROUP ** -0.5,
        "pool_b": n(ks[8], (N_POOL_LAYERS, N_POOL_GROUPS, POOL_GROUP), f32) * 0.01,
        "pool_scale": 1.0 + 0.05 * n(ks[9], (N_POOL_LAYERS, D_MODEL), f32),
        "mla_w_in": n(ks[10], (N_MLA_LAYERS, D_MODEL, Q_LORA + KV_LORA + QK_ROPE), f32) * D_MODEL ** -0.5,
        "mla_q_norm": 1.0 + 0.05 * n(ks[11], (N_MLA_LAYERS, Q_LORA), f32),
        "mla_kv_norm": 1.0 + 0.05 * n(ks[12], (N_MLA_LAYERS, KV_LORA), f32),
        "mla_w_uq": n(ks[13], (N_MLA_LAYERS, Q_LORA, N_HEADS, QK_NOPE + QK_ROPE), f32) * Q_LORA ** -0.5,
        "mla_w_uk": n(ks[14], (N_MLA_LAYERS, KV_LORA, N_HEADS, QK_NOPE), f32) * KV_LORA ** -0.5,
        "mla_w_uv": n(ks[15], (N_MLA_LAYERS, KV_LORA, N_HEADS, V_HEAD), f32) * KV_LORA ** -0.5,
        "mla_w_o": n(ks[16], (N_MLA_LAYERS, N_HEADS * V_HEAD, D_MODEL), f32) * (N_HEADS * V_HEAD) ** -0.5,
    }

def first_block(x, c, ada_w, ada_b, norm_g, ffn_w_in, ffn_w_out, pool_w, pool_b, pool_scale,
              mla_w_in, mla_q_norm, mla_kv_norm, mla_w_uq, mla_w_uk, mla_w_uv, mla_w_o):
    B = x.shape[0]
    cos, sin = rope_tables(x.shape[1], x.dtype)
    sc = jax.nn.silu(c)
    for i in range(DEPTH):
        mod = (sc @ ada_w[i] + ada_b[i]).reshape(B, N_MOD, D_MODEL)[:, :, None, :]
        g = norm_g[i]
        x = modulated_sublayer(x, mod[:, 0:3], g[0], g[1],
                               lambda h: swiglu(h, ffn_w_in[i, 0], ffn_w_out[i, 0]), 0.5)
        if i % N_MIXERS == 0:
            li = i // N_MIXERS
            mixer = lambda h: pool_mixer(h, pool_w[li], pool_b[li], pool_scale[li])
        else:
            li = i // N_MIXERS
            mixer = lambda h: mla_mixer(h, mla_w_in[li], mla_q_norm[li], mla_kv_norm[li],
                                        mla_w_uq[li], mla_w_uk[li], mla_w_uv[li], mla_w_o[li],
                                        cos, sin)
        x = modulated_sublayer(x, mod[:, 3:6], g[2], g[3], mixer, 1.0)
        x = modulated_sublayer(x, mod[:, 6:9], g[4], g[5],
                               lambda h: swiglu(h, ffn_w_in[i, 1], ffn_w_out[i, 1]), 0.5)
    return x


DEPTH_2 = 1

CONV_DIM = 512
CONV_WIDTH = 3
NSA_HEADS = 8
NSA_KV_GROUPS = 2
NSA_HPG = NSA_HEADS // NSA_KV_GROUPS
NSA_HEAD_DIM = 64
NSA_DIM = NSA_HEADS * NSA_HEAD_DIM
CMP_LEN = 32
CMP_STRIDE = 16
CMP_HIDDEN = 256
SLC_LEN = 64
SLC_TOPN = 8
SLC_FORCE_BONUS = 1e6
WINDOW = 512
NSA_QBLOCK = 64
GDN_HEADS = 4
GDN_HEAD_DIM = 128
GDN_DIM = GDN_HEADS * GDN_HEAD_DIM
GDN_CONV = 4
GDN_CHUNK = 64
N_BRANCH = 3
BRANCH_DIM = 512
IN_SPLITS = (3 * CONV_DIM, NSA_DIM, 6 * NSA_KV_GROUPS * NSA_HEAD_DIM, 3 * NSA_HEADS, 3 * GDN_DIM, GDN_DIM, GDN_HEADS, GDN_HEADS)
D_IN = 3 * CONV_DIM + NSA_DIM + 6 * NSA_KV_GROUPS * NSA_HEAD_DIM + 3 * NSA_HEADS + 4 * GDN_DIM + 2 * GDN_HEADS
MOE_GROUPS = 4
EXPERTS_PER_GROUP = 8
N_EXPERTS = MOE_GROUPS * EXPERTS_PER_GROUP
TOPK_IN_GROUP = 2
EXPERT_FF = 512
MOE_BLOCK = 256
RMS_EPS = 1e-6
NEG_INF = -1e30


def split_last(u, sizes):
    out, start = [], 0
    for n in sizes:
        out.append(u[..., start:start + n])
        start += n
    return out

def rms_norm(x, gain):
    xf = x.astype(jnp.float32)
    y = xf * lax.rsqrt(jnp.mean(xf * xf, axis=-1, keepdims=True) + RMS_EPS)
    return (y * gain.astype(jnp.float32)).astype(x.dtype)

def l2_norm(x):
    return x * lax.rsqrt(jnp.sum(x * x, axis=-1, keepdims=True) + RMS_EPS)

def causal_depthwise_conv(x, w):
    k, c = w.shape
    return lax.conv_general_dilated(x, w[:, None, :].astype(x.dtype), window_strides=(1,), padding=[(k - 1, 0)], dimension_numbers=('NWC', 'WIO', 'NWC'), feature_group_count=c)

def alibi_slopes(n):
    return 2.0 ** (-8.0 * jnp.arange(1, n + 1, dtype=jnp.float32) / n)

def short_conv_mixer(u_a, conv_w):
    b_gate, c_gate, x_in = split_last(u_a, (CONV_DIM, CONV_DIM, CONV_DIM))
    return b_gate * causal_depthwise_conv(c_gate * x_in, conv_w)

def nsa_compress(kv, pe, w1, w2):
    b, s, g, d = kv.shape
    n_cmp = (s - CMP_LEN) // CMP_STRIDE + 1
    idx = jnp.arange(n_cmp)[:, None] * CMP_STRIDE + jnp.arange(CMP_LEN)[None, :]
    blocks = kv[:, idx] + pe[:, None, :]
    flat = jnp.moveaxis(blocks, 3, 2).reshape(b, n_cmp, g, CMP_LEN * d)
    return jax.nn.gelu(flat @ w1) @ w2

def nsa_mixer(u_q, u_kv, u_g, qk_gain, cmp_pe, cmp_w1, cmp_w2):
    b, s, _ = u_q.shape
    g, hpg, d, qbl = NSA_KV_GROUPS, NSA_HPG, NSA_HEAD_DIM, NSA_QBLOCK
    f32 = jnp.float32
    scale = d ** -0.5
    q = rms_norm(u_q.reshape(b, s, g, hpg, d), qk_gain[0])
    kv = u_kv.reshape(b, s, 6, g, d)
    k_c = rms_norm(nsa_compress(kv[:, :, 0], cmp_pe[0], cmp_w1[0], cmp_w2[0]), qk_gain[1])
    v_c = nsa_compress(kv[:, :, 1], cmp_pe[1], cmp_w1[1], cmp_w2[1])
    n_cmp = k_c.shape[1]
    n_slc = s // SLC_LEN
    top_n = min(SLC_TOPN, n_slc)
    k_s = rms_norm(kv[:, :, 2], qk_gain[2]).reshape(b, n_slc, SLC_LEN, g, d).transpose(0, 3, 1, 2, 4)
    v_s = kv[:, :, 3].reshape(b, n_slc, SLC_LEN, g, d).transpose(0, 3, 1, 2, 4)
    pad = ((0, 0), (WINDOW, 0), (0, 0), (0, 0))
    k_w = jnp.pad(rms_norm(kv[:, :, 4], qk_gain[3]), pad)
    v_w = jnp.pad(kv[:, :, 5], pad)
    gates = jax.nn.sigmoid(u_g.astype(f32)).reshape(b, s, 3, g, hpg)
    slopes = alibi_slopes(NSA_HEADS).reshape(g, hpg)
    cmp_lo = jnp.arange(n_cmp) * CMP_STRIDE
    cmp_end = cmp_lo + CMP_LEN - 1
    slc_lo = jnp.arange(n_slc) * SLC_LEN
    overlap = ((cmp_lo[:, None] < slc_lo[None, :] + SLC_LEN) & (cmp_lo[:, None] + CMP_LEN > slc_lo[None, :])).astype(f32)
    n_qb = s // qbl
    q_blocks = jnp.moveaxis(q.reshape(b, n_qb, qbl, g, hpg, d), 1, 0)
    g_blocks = jnp.moveaxis(gates.reshape(b, n_qb, qbl, 3, g, hpg), 1, 0)
    bi = jnp.arange(b)[:, None, None, None]
    gi = jnp.arange(g)[None, :, None, None]
    j_idx = jnp.arange(n_slc)

    def query_block(args):
        qb, gb, blk = args
        q0 = blk * qbl
        t = q0 + jnp.arange(qbl)
        dist_c = (t[:, None] - cmp_end[None, :]).astype(f32)
        ok_c = dist_c >= 0
        s_c = jnp.einsum('bqghd,bcgd->bghqc', qb, k_c).astype(f32) * scale
        s_c = jnp.where(ok_c, s_c - slopes[:, :, None, None] * dist_c, NEG_INF)
        p_c = jax.nn.softmax(s_c, axis=-1) * jnp.any(ok_c, axis=-1)[:, None].astype(f32)
        o_c = jnp.einsum('bghqc,bcgd->bqghd', p_c.astype(v_c.dtype), v_c)
        imp = jnp.einsum('bghqc,cj->bgqj', p_c, overlap)
        jt = (t // SLC_LEN)[:, None]
        forced = (j_idx[None, :] == 0) | (j_idx[None, :] == jt) | (j_idx[None, :] == jt - 1)
        score = jnp.where(j_idx[None, :] <= jt, imp + jnp.where(forced, SLC_FORCE_BONUS, 0.0), NEG_INF)
        _, sel = lax.top_k(score, top_n)
        k_sel = k_s[bi, gi, sel].reshape(b, g, qbl, top_n * SLC_LEN, d)
        v_sel = v_s[bi, gi, sel].reshape(b, g, qbl, top_n * SLC_LEN, d)
        pos_s = (sel[..., None] * SLC_LEN + jnp.arange(SLC_LEN)).reshape(b, g, qbl, top_n * SLC_LEN)
        dist_s = (t[None, None, :, None] - pos_s).astype(f32)[:, :, None]
        s_s = jnp.einsum('bqghd,bgqkd->bghqk', qb, k_sel).astype(f32) * scale
        s_s = jnp.where(dist_s >= 0, s_s - slopes[None, :, :, None, None] * dist_s, NEG_INF)
        p_s = jax.nn.softmax(s_s, axis=-1)
        o_s = jnp.einsum('bghqk,bgqkd->bqghd', p_s.astype(v_sel.dtype), v_sel)
        k_wb = lax.dynamic_slice_in_dim(k_w, q0, WINDOW + qbl, axis=1)
        v_wb = lax.dynamic_slice_in_dim(v_w, q0, WINDOW + qbl, axis=1)
        pos_w = q0 - WINDOW + jnp.arange(WINDOW + qbl)
        dist_w = t[:, None] - pos_w[None, :]
        ok_w = (dist_w >= 0) & (dist_w < WINDOW) & (pos_w[None, :] >= 0)
        s_w = jnp.einsum('bqghd,bkgd->bghqk', qb, k_wb).astype(f32) * scale
        s_w = jnp.where(ok_w, s_w - slopes[:, :, None, None] * dist_w.astype(f32), NEG_INF)
        p_w = jax.nn.softmax(s_w, axis=-1)
        o_w = jnp.einsum('bghqk,bkgd->bqghd', p_w.astype(v_wb.dtype), v_wb)
        o = gb[:, :, 0, :, :, None] * o_c + gb[:, :, 1, :, :, None] * o_s + gb[:, :, 2, :, :, None] * o_w
        return o.reshape(b, qbl, NSA_DIM).astype(qb.dtype)

    out = lax.map(query_block, (q_blocks, g_blocks, jnp.arange(n_qb)))
    return jnp.moveaxis(out, 0, 1).reshape(b, s, NSA_DIM)

def chunk_gated_delta_rule(q, k, v, g, beta):
    b, s, h, dk = q.shape
    dv = v.shape[-1]
    c = GDN_CHUNK
    n = s // c

    def to_chunks(a):
        return jnp.moveaxis(a.reshape((b, n, c, h) + a.shape[3:]), 3, 1)

    q, k, v, beta = to_chunks(q), to_chunks(k), to_chunks(v), to_chunks(beta)
    gc = jnp.cumsum(to_chunks(g), axis=-1)
    tri = jnp.tril(jnp.ones((c, c), dtype=bool))
    decay = jnp.where(tri, jnp.exp(jnp.where(tri, gc[..., :, None] - gc[..., None, :], 0.0)), 0.0)
    k_beta = k * beta[..., None]
    m = jnp.einsum('bhncd,bhnsd->bhncs', k_beta, k) * decay
    t_inv = lax.linalg.triangular_solve(m, jnp.broadcast_to(jnp.eye(c, dtype=m.dtype), m.shape), left_side=True, lower=True, unit_diagonal=True)
    u = t_inv @ (v * beta[..., None])
    w = t_inv @ (k_beta * jnp.exp(gc)[..., None])
    attn = jnp.einsum('bhncd,bhnsd->bhncs', q, k) * decay
    q_dec = q * jnp.exp(gc)[..., None]
    g_last = gc[..., -1:]
    k_dec = k * jnp.exp(g_last - gc)[..., None]
    chunk_decay = jnp.exp(g_last[..., 0])

    def step(state, xs):
        q_i, k_i, u_i, w_i, a_i, d_i = xs
        v_new = u_i - jnp.einsum('bhcd,bhde->bhce', w_i, state)
        o_i = jnp.einsum('bhcd,bhde->bhce', q_i, state) + jnp.einsum('bhcs,bhse->bhce', a_i, v_new)
        state = state * d_i[..., None, None] + jnp.einsum('bhcd,bhce->bhde', k_i, v_new)
        return state, o_i

    xs = tuple(jnp.moveaxis(a, 2, 0) for a in (q_dec, k_dec, u, w, attn, chunk_decay))
    _, o = lax.scan(step, jnp.zeros((b, h, dk, dv), q.dtype), xs)
    return o.transpose(1, 0, 3, 2, 4).reshape(b, s, h, dv)

def gated_deltanet_mixer(u_qkv, u_z, u_b, u_a, conv_w, a_log, dt_bias, out_gain):
    b, s, _ = u_qkv.shape
    f32 = jnp.float32
    qkv = jax.nn.silu(causal_depthwise_conv(u_qkv, conv_w)).astype(f32).reshape(b, s, 3, GDN_HEADS, GDN_HEAD_DIM)
    q = l2_norm(qkv[:, :, 0]) * GDN_HEAD_DIM ** -0.5
    k = l2_norm(qkv[:, :, 1])
    v = qkv[:, :, 2]
    beta = jax.nn.sigmoid(u_b.astype(f32))
    g = -jnp.exp(a_log.astype(f32)) * jax.nn.softplus(u_a.astype(f32) + dt_bias.astype(f32))
    o = chunk_gated_delta_rule(q, k, v, g, beta)
    o = rms_norm(o, out_gain) * jax.nn.silu(u_z.astype(f32).reshape(b, s, GDN_HEADS, GDN_HEAD_DIM))
    return o.reshape(b, s, GDN_DIM).astype(u_qkv.dtype)

def hybrid_mixer(h, w_in, conv_a_w, nsa_qk_gain, cmp_pe, cmp_w1, cmp_w2, gdn_conv_w, gdn_a_log, gdn_dt_bias, gdn_out_gain, w_branch, w_gate, b_gate, w_out):
    b, s, dm = h.shape
    u = h @ w_in
    u_a, u_nq, u_nkv, u_ng, u_gqkv, u_gz, u_gb, u_ga = split_last(u, IN_SPLITS)
    y_a = short_conv_mixer(u_a, conv_a_w)
    y_n = nsa_mixer(u_nq, u_nkv, u_ng, nsa_qk_gain, cmp_pe, cmp_w1, cmp_w2)
    y_g = gated_deltanet_mixer(u_gqkv, u_gz, u_gb, u_ga, gdn_conv_w, gdn_a_log, gdn_dt_bias, gdn_out_gain)
    branches = jnp.einsum('bsrc,rcd->bsrd', jnp.stack([y_a, y_n, y_g], axis=2), w_branch)
    gates = jax.nn.sigmoid((h @ w_gate + b_gate).astype(jnp.float32)).reshape(b, s, N_BRANCH, dm)
    merged = jnp.sum(gates * branches, axis=2).astype(h.dtype)
    return merged @ w_out

def hier_moe(h, w_rg, b_rg, w_re, b_re, w_eg, w_eu, w_ed):
    b, s, dm = h.shape
    n_tok = b * s
    n_asg = n_tok * TOPK_IN_GROUP
    xt = h.reshape(n_tok, dm)
    lg = (xt @ w_rg + b_rg).astype(jnp.float32)
    grp = jnp.argmax(lg, axis=-1)
    p_grp = jnp.take_along_axis(jax.nn.softmax(lg, axis=-1), grp[:, None], axis=-1)
    le = (xt @ w_re + b_re).astype(jnp.float32).reshape(n_tok, MOE_GROUPS, EXPERTS_PER_GROUP)
    le = jnp.take_along_axis(le, grp[:, None, None], axis=1)[:, 0]
    top_p, top_i = lax.top_k(jax.nn.softmax(le, axis=-1), TOPK_IN_GROUP)
    gate = top_p / jnp.sum(top_p, axis=-1, keepdims=True) * p_grp
    expert = (grp[:, None] * EXPERTS_PER_GROUP + top_i).reshape(n_asg)
    token = jnp.arange(n_asg) // TOPK_IN_GROUP
    order = jnp.argsort(expert)
    e_s, tok_s, gate_s = expert[order], token[order], gate.reshape(n_asg)[order]
    counts = jnp.bincount(expert, length=N_EXPERTS)
    n_blk = (counts + MOE_BLOCK - 1) // MOE_BLOCK
    start = jnp.cumsum(counts) - counts
    pad_start = (jnp.cumsum(n_blk) - n_blk) * MOE_BLOCK
    dest = pad_start[e_s] + jnp.arange(n_asg) - start[e_s]
    total_blk = n_asg // MOE_BLOCK + N_EXPERTS
    buf = jnp.zeros((total_blk * MOE_BLOCK, dm), h.dtype).at[dest].set(xt[tok_s])
    blk_expert = jnp.repeat(jnp.arange(N_EXPERTS), n_blk, total_repeat_length=total_blk)

    def expert_block(args):
        xb, e = args
        return (jax.nn.silu(xb @ w_eg[e]) * (xb @ w_eu[e])) @ w_ed[e]

    yb = lax.map(expert_block, (buf.reshape(total_blk, MOE_BLOCK, dm), blk_expert))
    y = yb.reshape(total_blk * MOE_BLOCK, dm)[dest] * gate_s[:, None].astype(h.dtype)
    return jax.ops.segment_sum(y, tok_s, num_segments=n_tok).reshape(b, s, dm)

def second_inputs(seed: int = 0) -> dict:
    key = jax.random.key(seed)
    ks = jax.random.split(key, 24)
    f32 = jnp.float32

    def nrm(k, shape, scale):
        return jax.random.normal(k, shape, f32) * scale

    out_scale = (2 * DEPTH_2) ** -0.5
    dt = jnp.exp(jax.random.uniform(ks[10], (DEPTH_2, GDN_HEADS), f32, math.log(1e-3), math.log(1e-1)))
    return {
        'x': nrm(ks[0], (BATCH, SEQ, D_MODEL), 1.0),
        'norm_mix': 1.0 + nrm(ks[1], (DEPTH_2, D_MODEL), 0.02),
        'w_in': nrm(ks[2], (DEPTH_2, D_MODEL, D_IN), D_MODEL ** -0.5),
        'conv_a_w': nrm(ks[3], (DEPTH_2, CONV_WIDTH, CONV_DIM), CONV_WIDTH ** -0.5),
        'nsa_qk_gain': 1.0 + nrm(ks[4], (DEPTH_2, 4, NSA_HEAD_DIM), 0.02),
        'cmp_pe': nrm(ks[5], (DEPTH_2, 2, CMP_LEN, NSA_HEAD_DIM), 0.02),
        'cmp_w1': nrm(ks[6], (DEPTH_2, 2, CMP_LEN * NSA_HEAD_DIM, CMP_HIDDEN), (CMP_LEN * NSA_HEAD_DIM) ** -0.5),
        'cmp_w2': nrm(ks[7], (DEPTH_2, 2, CMP_HIDDEN, NSA_HEAD_DIM), CMP_HIDDEN ** -0.5),
        'gdn_conv_w': nrm(ks[8], (DEPTH_2, GDN_CONV, 3 * GDN_DIM), GDN_CONV ** -0.5),
        'gdn_a_log': jnp.log(jax.random.uniform(ks[9], (DEPTH_2, GDN_HEADS), f32, 1.0, 16.0)),
        'gdn_dt_bias': dt + jnp.log(-jnp.expm1(-dt)),
        'gdn_out_gain': 1.0 + nrm(ks[11], (DEPTH_2, GDN_HEAD_DIM), 0.02),
        'w_branch': nrm(ks[12], (DEPTH_2, N_BRANCH, BRANCH_DIM, D_MODEL), BRANCH_DIM ** -0.5),
        'w_gate': nrm(ks[13], (DEPTH_2, D_MODEL, N_BRANCH * D_MODEL), D_MODEL ** -0.5),
        'b_gate': nrm(ks[14], (DEPTH_2, N_BRANCH * D_MODEL), 0.01),
        'w_out': nrm(ks[15], (DEPTH_2, D_MODEL, D_MODEL), D_MODEL ** -0.5 * out_scale),
        'norm_ffn': 1.0 + nrm(ks[16], (DEPTH_2, D_MODEL), 0.02),
        'w_router_group': nrm(ks[17], (DEPTH_2, D_MODEL, MOE_GROUPS), D_MODEL ** -0.5),
        'b_router_group': nrm(ks[18], (DEPTH_2, MOE_GROUPS), 0.01),
        'w_router_expert': nrm(ks[19], (DEPTH_2, D_MODEL, N_EXPERTS), D_MODEL ** -0.5),
        'b_router_expert': nrm(ks[20], (DEPTH_2, N_EXPERTS), 0.01),
        'w_expert_gate': nrm(ks[21], (DEPTH_2, N_EXPERTS, D_MODEL, EXPERT_FF), D_MODEL ** -0.5),
        'w_expert_up': nrm(ks[22], (DEPTH_2, N_EXPERTS, D_MODEL, EXPERT_FF), D_MODEL ** -0.5),
        'w_expert_down': nrm(ks[23], (DEPTH_2, N_EXPERTS, EXPERT_FF, D_MODEL), EXPERT_FF ** -0.5 * out_scale),
    }

def second_block(x, norm_mix, w_in, conv_a_w, nsa_qk_gain, cmp_pe, cmp_w1, cmp_w2, gdn_conv_w, gdn_a_log, gdn_dt_bias, gdn_out_gain, w_branch, w_gate, b_gate, w_out, norm_ffn, w_router_group, b_router_group, w_router_expert, b_router_expert, w_expert_gate, w_expert_up, w_expert_down):
    for l in range(DEPTH_2):
        h = rms_norm(x, norm_mix[l])
        x = x + hybrid_mixer(h, w_in[l], conv_a_w[l], nsa_qk_gain[l], cmp_pe[l], cmp_w1[l], cmp_w2[l], gdn_conv_w[l], gdn_a_log[l], gdn_dt_bias[l], gdn_out_gain[l], w_branch[l], w_gate[l], b_gate[l], w_out[l])
        h = rms_norm(x, norm_ffn[l])
        x = x + hier_moe(h, w_router_group[l], b_router_group[l], w_router_expert[l], b_router_expert[l], w_expert_gate[l], w_expert_up[l], w_expert_down[l])
    return x


def setup_inputs(seed=0):
    out = dict(first_inputs(seed))
    for name, value in second_inputs(seed + 1).items():
        if name != "x":
            out[name + "_2"] = value
    return out


def reference(
    x, c, ada_w, ada_b, norm_g, ffn_w_in, ffn_w_out, pool_w, pool_b, pool_scale, mla_w_in,
    mla_q_norm, mla_kv_norm, mla_w_uq, mla_w_uk, mla_w_uv, mla_w_o, norm_mix_2, w_in_2,
    conv_a_w_2, nsa_qk_gain_2, cmp_pe_2, cmp_w1_2, cmp_w2_2, gdn_conv_w_2, gdn_a_log_2,
    gdn_dt_bias_2, gdn_out_gain_2, w_branch_2, w_gate_2, b_gate_2, w_out_2, norm_ffn_2,
    w_router_group_2, b_router_group_2, w_router_expert_2, b_router_expert_2, w_expert_gate_2,
    w_expert_up_2, w_expert_down_2,
):
    x = first_block(
        x, c, ada_w, ada_b, norm_g, ffn_w_in, ffn_w_out, pool_w, pool_b, pool_scale, mla_w_in,
        mla_q_norm, mla_kv_norm, mla_w_uq, mla_w_uk, mla_w_uv, mla_w_o,
    )
    return second_block(
        x, norm_mix_2, w_in_2, conv_a_w_2, nsa_qk_gain_2, cmp_pe_2, cmp_w1_2, cmp_w2_2,
        gdn_conv_w_2, gdn_a_log_2, gdn_dt_bias_2, gdn_out_gain_2, w_branch_2, w_gate_2,
        b_gate_2, w_out_2, norm_ffn_2, w_router_group_2, b_router_group_2, w_router_expert_2,
        b_router_expert_2, w_expert_gate_2, w_expert_up_2, w_expert_down_2,
    )


_drawn_inputs = setup_inputs


def setup_inputs(seed=0):
    import zlib

    import numpy as np

    out = dict(_drawn_inputs(seed))
    spreads = {}
    factors = {'pool_b': 3.349,
     'mla_q_norm': 4.126,
     'norm_mix_2': 5.455,
     'nsa_qk_gain_2': 57.127,
     'cmp_pe_2': 64.0,
     'gdn_a_log_2': 3.159,
     'gdn_out_gain_2': 64.0,
     'b_gate_2': 24.499,
     'norm_ffn_2': 19.041,
     'b_router_group_2': 26.766,
     'b_router_expert_2': 57.524,
     'cmp_w1_2': 3.42,
     'cmp_w2_2': 3.11}
    for name, (base, spread) in spreads.items():
        noise = np.random.default_rng([zlib.crc32(name.encode()), seed]).standard_normal(out[name].shape)
        drawn = base * np.exp(spread * noise) if base else spread * noise
        out[name] = __import__('jax').numpy.asarray(drawn.astype(out[name].dtype))
    for name, factor in factors.items():
        out[name] = (out[name] * factor).astype(out[name].dtype)
    return out
```

```python
from contextlib import ExitStack

import concourse.bass as bass
from concourse import mybir

F32 = mybir.dt.float32
ALU = mybir.AluOpType
ACT = mybir.ActivationFunctionType
AX = mybir.AxisListType

P = 128
S = 256
D = 1024
KT = D // P
TT = S // P
SLOT = KT * P
CHUNK = 3 * SLOT
RING = 6
EPS = 1e-6
DEPTH = 2
NF = 2816 // P
HEADS = 16
MLA_SCALE = (64 + 32) ** -0.5
NSA_T = 4
NCMP = 15
GH = 4
NU = GH * TT
E = 32
FE = 4

STAGES = [("ada0", 24), ("ffn0", NF), ("pool", 1), ("ffn1", NF), ("ada1", 24), ("ffn2", NF),
          ("mla", 7), ("ffn3", NF), ("hyb", 14), ("cmp", 3), ("msk", 1), ("mrg", 12), ("out", 3),
          ("moe", E * FE)]
BASE = {}
_at = 0
for _n, _c in STAGES:
    BASE[_n] = _at
    _at += _c
NCHUNK = _at

COLS = {}
NCOL = 0
for _n, _c in [("c", 8), ("ada_b", 144), ("norm_g", 96), ("pool_b", 8), ("pool_scale", 8),
               ("norm_mix", 8), ("norm_ffn", 8), ("b_gate", 24), ("q_norm", 2), ("kv_norm", 1),
               ("conv_a", 12), ("conv_g", 48), ("qk_gain", 4), ("out_gain", 1), ("pe", 32),
               ("b_rt", 36), ("a_log", 4), ("dt", 4)]:
    COLS[_n] = (NCOL, NCOL + _c)
    NCOL += _c

M_ND, M_LOW, M_UPP = 0, 512, 512 + 7 * P
M_STRICT, M_TRIL, M_HALF, M_TRI, M_OK = 2304, 2432, 2560, 2688, 2816


def build(nc, stream, cols_d, ident_d, x_d, out_d):
    ctx = ExitStack()
    with ctx:
        def sb(name, shape):
            return ctx.enter_context(nc.sbuf_tensor(name, shape, F32))

        names = {}

        def sem(name):
            if name not in names:
                names[name] = ctx.enter_context(nc.semaphore(name))
            return names[name]

        ring = sb("ring", [P, RING, CHUNK])
        X = sb("X", [P, KT, S])
        H = sb("H", [P, KT, S])
        mem = sb("mem", [P, 26, 1024])
        cols = sb("cols", [P, NCOL])
        cst = sb("cst", [P, 2 * P])
        mod = sb("mod", [P, DEPTH, 72])
        modA = sb("modA", [P, DEPTH, 3, KT])
        modC = sb("modC", [P, DEPTH, 3, KT])
        silc = sb("silc", [P, KT])
        rstd = sb("rstd", [P, S])
        act = sb("act", [P, 2, S])
        sg = sb("sg", [P, 2, S])
        eps = sb("eps", [P, 1])
        st = sb("st", [P, 512])
        psA = ctx.enter_context(nc.psum_tensor("psA", [P, 4, 512], F32))
        psG = ctx.enter_context(nc.psum_tensor("psG", [P, 2, 512], F32))
        psS = ctx.enter_context(nc.psum_tensor("psS", [P, 2, 512], F32))
        ident, ones = cst[:, 0:P], cst[:, P:2 * P]

        def blk(i, n=1):
            return mem[:, i:i + n, :].rearrange("p a b -> p (a b)")

        def tiles(i, n=1, w=S):
            return blk(i, n).rearrange("p (t s) -> p t s", s=w)

        def col(name, i, n=1):
            a = COLS[name][0] + i
            return cols[:, a:a + n]

        def chunk(n, a=0, b=CHUNK):
            return ring[:, n % RING, a:b]

        Y, SQ = tiles(0, 2), tiles(2, 2)
        chunk_used, h_ready, x_ready = sem("chunk_used"), sem("h_ready"), sem("x_ready")
        full = [sem(f"chunk_full{j}") for j in range(RING)]

        def arrived(eng, n, i=0):
            if isinstance(i, int):
                eng.wait_ge(full[(n + i) % RING], 16 * ((n + i) // RING + 1))
            else:
                eng.wait_ge(full[n % RING], i * 16 // RING + 16 * (n // RING + 1))

        class Chain:

            def __init__(self, eng, name):
                self.eng, self.name, self.n = eng, name, {}

            def link(self, ins, name=None):
                name = name or self.name
                self.n[name] = self.n.get(name, 0) + 1
                ins.then_inc(sem(name), 1)
                self.eng.wait_ge(sem(name), self.n[name])

        def pre_cols(n):
            if n < 6:
                i, s = divmod(n, 3)
                return (lambda k: modA[:, i, s, k:k + 1]), (lambda k: mod[:, i, 24 * s + k:24 * s + k + 1])
            name = "norm_mix" if n == 6 else "norm_ffn"
            return (lambda k: col(name, k)), None

        block = ctx.enter_context(nc.Block())

        @block.sync
        def _(sp):
            sp.dma_start(cols[:, :], cols_d).then_inc(sem("cols_in"), 16)
            sp.dma_start(cst[:, :], ident_d).then_inc(sem("cst_in"), 16)
            for j in range(RING):
                sp.dma_start(ring[:, j, :], stream[j, :, :]).then_inc(full[j], 16)
                if j == 2:
                    sp.dma_start(X[:, :, :], x_d).then_inc(sem("x_in"), 16)
            whole = NCHUNK // RING * RING
            with sp.Fori(1, NCHUNK // RING) as r:
                i = r * RING
                for j in range(RING):
                    sp.wait_ge(chunk_used, i + (j + 1 - RING))
                    sp.dma_start(ring[:, j, :], stream[bass.ds(i + j, 1), :, :].rearrange("o p n -> (o p) n")).then_inc(full[j], 16)
            for n in range(whole, NCHUNK):
                sp.wait_ge(chunk_used, n + 1 - RING)
                sp.dma_start(ring[:, n % RING, :], stream[n, :, :]).then_inc(full[n % RING], 16)
            sp.wait_ge(x_ready, 9)
            sp.dma_start(out_d, X[:, :, :]).then_inc(sem("out_written"), 16)
            sp.wait_ge(sem("out_written"), 16)

        LAT, CQN, QN, QR, ROT, KRM = tiles(4), tiles(5), tiles(6, 2), tiles(8), tiles(9), tiles(10)
        KVTOK = blk(11)[:, 0:S].rearrange("p (t c) -> p t c", t=TT)
        QL = blk(11)[:, 512:1024].rearrange("p (b s) -> p b s", b=2)
        PB, PTB = tiles(12, 1, 512), tiles(13, 1, 512)
        OL = blk(14)[:, 0:512].rearrange("p (b s) -> p b s", b=2)
        MO = tiles(15, 2)
        UA, UQ, UK, UKV, UG, UZ = tiles(4, 3), tiles(7), tiles(8), tiles(9), tiles(10, 3), tiles(13)
        YN, YG = tiles(14), tiles(15)
        YA = tiles(5)
        KG = blk(16).rearrange("p (y g s) -> p y g s", y=2, g=2)
        VG = blk(17).rearrange("p (y t g c) -> p y t g c", y=2, t=TT, g=2)
        BL = [blk(18)[:, 512 * y:512 * y + 480].rearrange("p (l g c) -> p l g c", l=16, g=2) for y in range(2)]
        HID = blk(19)[:, 0:120].rearrange("p (y m g c) -> p y m g c", y=2, m=2, g=2)
        KGC = blk(19)[:, 128:128 + 2 * NCMP].rearrange("p (g c) -> p g c", g=2)
        VGC = blk(19)[0:NCMP, 256:512].rearrange("p (g c) -> p g c", g=2)
        KT_W = blk(19)[:, 512:768]
        NPB, NPTB = tiles(20, 1, 512), tiles(21, 1, 512)
        VTC = tiles(22)
        GT = st[:, 0:64].rearrange("p (t c) -> p t c", t=TT)
        GATE = st[:, 64:64 + 48].rearrange("p (t c) -> p t c", t=TT)
        NMAX = st[:, 120:124].rearrange("p (b t) -> p b t", b=2)
        SUM = st[:, 124:128].rearrange("p (b t) -> p b t", b=2)
        FAC = st[:, 128:132].rearrange("p (b t) -> p b t", b=2)
        BETA, GG, GC, EGC, KD, BG, GX = (st[:, 136 + 8 * i:144 + 8 * i] for i in range(7))
        AL = st[:, 200:204]
        RL = st[:, 208:216]

        def unit_col(t, h, n):
            return t[:, n * GH + h:n * GH + h + 1]

        def units(b):
            return blk(b).rearrange("p (u s) -> p u s", u=NU)

        CV = tiles(16, 3)
        KBG, KDEC, VB, DEC, ER, L_, LT = (units(i) for i in (19, 20, 21, 22, 23, 24, 25))
        TM, TMT, XM, XMT, P1, Q1 = (units(i) for i in (7, 8, 9, 10, 11, 12))
        AT_, ATT, WT, UU = units(4), units(6), units(0), units(1)
        SST = blk(2)[:, 0:512].rearrange("p (h s) -> p h s", h=GH)
        VNEW = blk(2)[:, 512:1024].rearrange("p (h s) -> p h s", h=GH)
        OT = blk(3).rearrange("p (h n s) -> p h n s", h=GH, n=2)
        QT, KTT, VT = CV[:, 0:4], CV[:, 4:8], CV[:, 8:12]
        GB = blk(16, 8)

        msk = BASE["msk"]

        def mask(a, n=P):
            return chunk(msk, a, a + n)

        NSA_UNITS = [(t, y, g) for t in range(NSA_T) for y in range(3) for g in range(2)]

        @block.tensor
        def _(pe):
            def mm(out, lhsT, rhs, start, stop):
                return nc.tensor.matmul(out, lhsT, rhs, start=start, stop=stop, skip_group_check=True)

            pe.wait_ge(sem("cst_in"), 16)

            def ada(layer):
                c0 = BASE[f"ada{layer}"]
                pe.wait_ge(sem("silc_ready"), 1)
                with pe.Fori(0, 24, RING) as i:
                    for j in range(RING):
                        arrived(pe, c0 + j, i)
                        for m in range(3):
                            for k in range(KT):
                                last = mm(psS[:, 0, bass.ds(i * 3 + (3 * j + m), 1)],
                                          chunk(c0 + j, m * SLOT + k * P, m * SLOT + k * P + P),
                                          silc[:, k:k + 1], start=(k == 0), stop=(k == KT - 1))
                        last.then_inc(chunk_used, 1)

            def pre_norm(n):
                pe.wait_ge(sem("pre_sq_act"), n + 1)
                pe.wait_ge(sem("pre_sq_dve"), n + 1)
                for k in range(KT):
                    last = mm(psS[:, 0, 0:S], ones, SQ[:, k, :], start=(k == 0), stop=(k == KT - 1))
                last.then_inc(sem("pre_sum"), 1)

            def post_norm(n):
                for k in range(KT):
                    if k % 2 == 0:
                        pe.wait_ge(sem("post_sq"), 4 * n + k // 2 + 1)
                    last = mm(psS[:, 0, 0:S], ones, SQ[:, k, :], start=(k == 0), stop=(k == KT - 1))
                last.then_inc(sem("post_sum"), 1)

            def ffn(c0, t0, nf, norm):
                def gate_up(i, f):
                    c, t = c0 + f, t0 + f
                    arrived(pe, c, i)
                    if t >= 2:
                        pe.wait_ge(sem("act_ready"), i + (t - 1))
                    for u in range(2):
                        for k in range(KT):
                            if isinstance(i, int) and f == 0 and u == 0:
                                pe.wait_ge(h_ready, 8 * norm + k + 1)
                            last = mm(psG[:, t % 2, u * S:(u + 1) * S],
                                      chunk(c, u * SLOT + k * P, u * SLOT + k * P + P), H[:, k, :],
                                      start=(u == 0 and k == 0), stop=(u == 1 and k == KT - 1),)
                    last.then_inc(sem("gu_ready"), 1)

                def down(i, f, first=False, final=False):
                    c, t = c0 + f, t0 + f
                    pe.wait_ge(sem("act_ready"), i + (t + 1))
                    for m in range(KT):
                        last = mm(psA[:, m // 2, (m % 2) * S:(m % 2 + 1) * S],
                                  chunk(c, 2 * SLOT + m * P, 2 * SLOT + m * P + P), act[:, t % 2, :],
                                  start=(first and m % 2 == 0), stop=final)
                    last.then_inc(chunk_used, 1)

                gate_up(0, 0)
                gate_up(0, 1)
                down(0, 0, first=True)
                whole = (nf - 2) // RING
                with pe.Fori(0, whole * RING, RING) as i:
                    for j in range(RING):
                        gate_up(i, 2 + j)
                        down(i, 1 + j)
                for f in range(2 + whole * RING, nf):
                    gate_up(0, f)
                    down(0, f - 1)
                down(0, nf - 1, final=True)

            def pool():
                c = BASE["pool"]
                arrived(pe, c)
                pe.wait_ge(sem("pooled"), 1)
                for m in range(KT):
                    g, dt = divmod(m, 2)
                    for k in range(2):
                        a = (g * 4 + dt * 2 + k) * P
                        last = mm(psA[:, m // 2, (m % 2) * S:(m % 2 + 1) * S], chunk(c, a, a + P),
                                  SQ[:, 2 * g + k, :], start=(m % 2 == 0 and k == 0),
                                  stop=(k == 1))
                last.then_inc(chunk_used, 1)

            def attention(n, p, prep, scores, blocks, product, after):
                for u in range(-1, n + 1):
                    if u + 1 < n:
                        prep(u + 1)
                        if u >= 1:
                            pe.wait_ge(sem(p + "exp"), 2 * u)
                        scores(u + 1).then_inc(sem(p + "score"), 1)
                    if 0 <= u - 1:
                        pe.wait_ge(sem(p + "pt"), u)
                        product(u - 1).then_inc(sem(p + "pv"), 1)
                        after(u - 1)
                    if 0 <= u < n:
                        pe.wait_ge(sem(p + "p"), u + 1)
                        if u >= 2:
                            pe.wait_ge(sem(p + "pt"), u - 1)
                        blocks(u).then_inc(sem(p + "tr"), 1)

            def mla():
                c = BASE["mla"]
                for m in range(4):
                    cc, s = c + m // 3, m % 3
                    arrived(pe, cc)
                    for k in range(KT):
                        if m == 0:
                            pe.wait_ge(h_ready, 8 * 4 + k + 1)
                        last = mm(psA[:, m, 0:S], chunk(cc, s * SLOT + k * P, s * SLOT + k * P + P),
                                  H[:, k, :], start=(k == 0), stop=(k == KT - 1))
                    if m == 2:
                        last.then_inc(chunk_used, 1)
                last.then_inc(sem("mla_lat"), 1)
                pe.wait_ge(sem("mla_sq"), 1)
                for k in range(2):
                    mm(psS[:, 0, 0:S], ones, ROT[:, k, :], start=(k == 0), stop=(k == 1))
                mm(psS[:, 1, 0:S], ones, ROT[:, 2, :], start=True, stop=True).then_inc(sem("mla_sum"), 1)
                pe.wait_ge(sem("mla_cqn"), 1)
                for m in range(12):
                    b = m % 4
                    if m % 4 == 0 and m:
                        pe.wait_ge(sem("mla_q"), m // 4)
                    for k in range(2):
                        j = 2 * m + k
                        cc, a = (c + 1, SLOT + j * P) if j < 16 else (c + 2, (j - 16) * P)
                        if j in (0, 16):
                            arrived(pe, cc)
                        last = mm(psA[:, b, 0:S], chunk(cc, a, a + P), CQN[:, k, :],
                                  start=(k == 0), stop=(k == 1))
                    if m == 7:
                        last.then_inc(chunk_used, 1)
                    if m == 11:
                        last.then_inc(sem("mla_qps"), 1)
                    if m in (3,):
                        last.then_inc(sem("mla_qps"), 1)
                    if m == 7:
                        pass
                arrived(pe, c + 3)
                pe.wait_ge(sem("mla_q"), 3)
                rot = chunk(c + 3, 2 * SLOT + 512, 2 * SLOT + 640)
                for m in range(4):
                    mm(psA[:, m // 2, (m % 2) * S:(m % 2 + 1) * S], rot, QR[:, m, :],
                       start=(m % 2 == 0), stop=True)
                mm(psG[:, 0, 0:S], rot, LAT[:, 3, :], start=True, stop=True)
                for t in range(TT):
                    last = nc.tensor.transpose(psG[:, 1, t * P:(t + 1) * P], CQN[:, 2, t * P:(t + 1) * P], ident)
                last.then_inc(sem("mla_rot"), 1)
                pe.wait_ge(sem("mla_ready"), 1)

                def prep(h):
                    if h >= 1:
                        pe.wait_ge(sem("mla_ql"), h)
                    a = SLOT + h * P
                    ins = mm(psS[:, 0, 0:S], chunk(c + 2, a, a + P), QN[:, h // 2, :], start=True, stop=True)
                    ins.then_inc(sem("mla_qlps"), 1)

                def scores(h):
                    pe.wait_ge(sem("mla_ql"), h + 1)
                    for t in range(TT):
                        mm(psA[:, h % 2, t * S:(t + 1) * S], QL[:, h % 2, t * P:(t + 1) * P],
                           CQN[:, 2, :], start=(t == 0), stop=False)
                        last = mm(psA[:, h % 2, t * S:(t + 1) * S], QR[:, h // 4, t * P:(t + 1) * P],
                                  KRM[:, h % 4, :], start=False, stop=True)
                    return last

                def blocks(h):
                    for kt in range(TT):
                        for t in range(TT):
                            last = nc.tensor.transpose(
                                psA[:, 2 + h % 2, kt * S + t * P:kt * S + (t + 1) * P],
                                PB[:, h % 2, t * S + kt * P:t * S + (kt + 1) * P], ident)
                    return last

                def product(h):
                    if h >= 2:
                        pe.wait_ge(sem("mla_ol"), h - 1)
                    for kt in range(TT):
                        last = mm(psG[:, h % 2, 0:S], KVTOK[:, kt, :], PTB[:, h % 2, kt * S:(kt + 1) * S],
                                  start=(kt == 0), stop=(kt == 1))
                    return last

                def up(h):
                    if h < 0:
                        return
                    pe.wait_ge(sem("mla_ol"), h + 1)
                    if h % 2 == 0 and h:
                        pe.wait_ge(sem("mla_o"), h // 2)
                    last = mm(psS[:, 1, 0:S], chunk(c + 3, h * P, h * P + P), OL[:, h % 2, :],
                              start=(h % 2 == 0), stop=(h % 2 == 1))
                    last.then_inc(sem("mla_up"), 1)

                attention(HEADS, "mla_", prep, scores, blocks, product, lambda h: up(h - 1))
                up(HEADS - 1)
                pe.wait_ge(sem("mla_up"), HEADS)
                pe.sem_inc(chunk_used, 2)
                pe.wait_ge(sem("mla_o"), HEADS // 2)
                for m in range(KT):
                    cc, s = c + 4 + m // 3, m % 3
                    arrived(pe, cc)
                    for k in range(KT):
                        last = mm(psA[:, m // 2, (m % 2) * S:(m % 2 + 1) * S],
                                  chunk(cc, s * SLOT + k * P, s * SLOT + k * P + P), MO[:, k, :],
                                  start=(m % 2 == 0 and k == 0), stop=(k == KT - 1))
                    if s == 2 or m == KT - 1:
                        last.then_inc(chunk_used, 1)

            def hybrid_in():
                c = BASE["hyb"]
                for m in range(40):
                    cc, s, j = c + m // 3, m % 3, m // 2
                    arrived(pe, cc)
                    if m % 2 == 0 and j >= 2:
                        pe.wait_ge(sem("u_out"), j - 1)
                    for k in range(KT):
                        if m == 0:
                            pe.wait_ge(h_ready, 8 * 6 + k + 1)
                        last = mm(psG[:, j % 2, (m % 2) * S:(m % 2 + 1) * S],
                                  chunk(cc, s * SLOT + k * P, s * SLOT + k * P + P), H[:, k, :],
                                  start=(m % 2 == 0 and k == 0), stop=(k == KT - 1))
                    if m % 2 == 1:
                        last.then_inc(sem("u_ps"), 1)
                    elif s == 2:
                        last.then_inc(chunk_used, 1)
                    if m % 2 == 1 and s == 2:
                        pe.wait_ge(sem("u_ps"), j + 1)
                        pe.sem_inc(chunk_used, 1)
                for t in range(TT):
                    for k in range(KT):
                        a = SLOT + k * 32
                        last = mm(psS[:, 0, t * 32:(t + 1) * 32], H[:, k, t * P:(t + 1) * P],
                                  chunk(c + 13, a, a + 32), start=(k == 0), stop=(k == KT - 1))
                last.then_inc(chunk_used, 1)

            def nsa():
                c = BASE["cmp"]
                pe.wait_ge(sem("blocks_ready"), 4)
                for y in range(2):
                    for m in range(2):
                        for l in range(16):
                            s = y * 4 + l // 4
                            cc, a = c + s // 3, (s % 3) * SLOT + (l % 4) * S + m * P
                            if m == 0 and l % 4 == 0:
                                arrived(pe, cc)
                            last = mm(psA[:, y * 2 + m, 0:2 * NCMP], chunk(cc, a, a + P),
                                      BL[y][:, l, :, :].rearrange("p g c -> p (g c)"),
                                      start=(l == 0), stop=(l == 15))
                last.then_inc(sem("cmp_hid"), 1)
                pe.wait_ge(sem("hid_ready"), 1)
                w2 = 2 * SLOT
                arrived(pe, c + 2)
                for g in range(2):
                    for k in range(2):
                        a = w2 + (k * 2 + g) * P
                        mm(psG[:, 0, g * NCMP:(g + 1) * NCMP], chunk(c + 2, a, a + P), HID[:, 0, k, g, :],
                           start=(k == 0), stop=(k == 1))
                for g in range(2):
                    for k in range(2):
                        a = w2 + (4 + k * 2 + g) * P
                        last = mm(psG[0:NCMP, 1, g * P:(g + 1) * P], HID[:, 1, k, g, :], chunk(c + 2, a, a + P),
                                  start=(k == 0), stop=(k == 1))
                last.then_inc(sem("cmp_out"), 1)
                arrived(pe, msk)
                half = mask(M_HALF)
                pe.wait_ge(sem("nsa_sq"), 1)
                for t in range(NSA_T):
                    mm(psA[:, t // 2, (t % 2) * S:(t % 2 + 1) * S], half, SQ[:, t, :],
                       start=(t % 2 == 0), stop=True)
                for y in range(2):
                    mm(psA[:, 2, y * S:(y + 1) * S], half, SQ[:, 4 + y, :],
                       start=(y == 0), stop=True)
                pe.wait_ge(sem("nsa_sqc"), 1)
                mm(psA[:, 3, 0:2 * NCMP], half, SQ[:, 6, 0:2 * NCMP], start=True,
                   stop=True).then_inc(sem("nsa_sum"), 1)
                for y in range(2):
                    for t in range(TT):
                        last = nc.tensor.transpose(psS[:, 1, (y * TT + t) * P:(y * TT + t + 1) * P],
                                                   UKV[:, 2 * y + 1, t * P:(t + 1) * P], ident)
                last.then_inc(sem("nsa_v"), 1)
                pe.wait_ge(sem("nsa_ready"), 1)
                pe.sem_inc(chunk_used, 3)

                def key(y, g):
                    return KGC[:, g, :] if y == 0 else KG[:, y - 1, g, :]

                def scores(u):
                    t, y, g = NSA_UNITS[u]
                    w = NCMP if y == 0 else S
                    for i in range(TT):
                        last = mm(psA[:, u % 2, i * S:i * S + w], UQ[:, t, i * P:(i + 1) * P], key(y, g),
                                  start=(i == 0), stop=True)
                    return last

                def blocks(u):
                    t, y, g = NSA_UNITS[u]
                    if y == 0:
                        for i in range(TT):
                            last = nc.tensor.transpose(psA[0:NCMP, 2 + u % 2, i * P:(i + 1) * P],
                                                       NPB[:, u % 2, i * S:i * S + NCMP], ident)
                        return last
                    for kt in range(TT):
                        for i in range(TT):
                            last = nc.tensor.transpose(
                                psA[:, 2 + u % 2, kt * S + i * P:kt * S + (i + 1) * P],
                                NPB[:, u % 2, i * S + kt * P:i * S + (kt + 1) * P], ident)
                    return last

                def product(u):
                    t, y, g = NSA_UNITS[u]
                    first, final = (y == 0 and g == 0), (y == 2 and g == 1)
                    if first and t >= 2:
                        pe.wait_ge(sem("nsa_o"), t - 1)
                    if y == 0:
                        return mm(psG[:, t % 2, 0:S], VGC[:, g, :], NPTB[0:NCMP, u % 2, 0:S],
                                  start=first, stop=False)
                    for kt in range(TT):
                        last = mm(psG[:, t % 2, 0:S], VG[:, y - 1, kt, g, :],
                                  NPTB[:, u % 2, kt * S:(kt + 1) * S], start=False, stop=(final and kt == 1))
                    return last

                attention(len(NSA_UNITS), "nsa_", lambda u: None, scores, blocks, product, lambda u: None)

            def gdn():
                pe.wait_ge(sem("gdn_sq"), 1)
                pe.wait_ge(sem("nsa_o"), NSA_T)
                for b in range(4):
                    last = mm(psA[:, b, :], ones, SQ[:, 2 * b:2 * b + 2, :].rearrange("p a s -> p (a s)"),
                              start=True, stop=True)
                last.then_inc(sem("gdn_sum"), 1)
                pe.wait_ge(sem("gdn_g"), 1)
                mm(psS[:, 0, 0:NU], mask(M_TRI), GG, start=True, stop=True).then_inc(sem("gdn_gc"), 1)
                pe.wait_ge(sem("gdn_gu"), 1)
                for b in range(2):
                    last = mm(psG[:, b, :], ones, DEC[:, 4 * b:4 * b + 4, :].rearrange("p u s -> p (u s)"),
                              start=True, stop=True)
                last.then_inc(sem("gdn_row"), 1)
                pe.wait_ge(sem("gdn_qk"), 1)
                for u in range(NU):
                    h, n = divmod(u, 2)
                    nc.tensor.transpose(psA[:, u // 4, (u % 4) * P:(u % 4 + 1) * P],
                                        KTT[:, h, n * P:(n + 1) * P], ident)
                for u in range(NU):
                    h, n = divmod(u, 2)
                    last = nc.tensor.transpose(psA[:, 2 + u // 4, (u % 4) * P:(u % 4 + 1) * P],
                                               VT[:, h, n * P:(n + 1) * P], ident)
                last.then_inc(sem("gdn_kv"), 1)
                pe.wait_ge(sem("gdn_kvtok"), 1)
                for u in range(NU):
                    h, n = divmod(u, 2)
                    k = KTT[:, h, n * P:(n + 1) * P]
                    mm(psA[:, u // 4, (u % 4) * P:(u % 4 + 1) * P], k, k, start=(u % 4 == 0),
                       stop=True)
                    last = mm(psA[:, 2 + u // 4, (u % 4) * P:(u % 4 + 1) * P], QT[:, h, n * P:(n + 1) * P], k,
                              start=(u % 4 == 0), stop=True)
                last.then_inc(sem("gdn_gram"), 1)
                pe.wait_ge(sem("gdn_l"), 1)
                for u in range(NU):
                    nc.tensor.transpose(psA[:, u // 4, (u % 4) * P:(u % 4 + 1) * P], L_[:, u, :], ident)
                    last = nc.tensor.transpose(psA[:, 2 + u // 4, (u % 4) * P:(u % 4 + 1) * P],
                                               AT_[:, u, :], ident)
                last.then_inc(sem("gdn_lt"), 1)

                def each(ps, b0, lhs, rhs):
                    for u in range(NU):
                        last = mm(ps[:, b0 + u // 4, (u % 4) * P:(u % 4 + 1) * P], lhs[:, u, :], rhs[:, u, :],
                                  start=(u % 4 == 0), stop=True)
                    return last

                pe.wait_ge(sem("gdn_att"), 1)
                for lev in range(1, 7):
                    pe.wait_ge(sem("gdn_x"), lev + 1)
                    pe.wait_ge(sem("gdn_t"), lev)
                    each(psA, 0, XMT, TM)
                    each(psA, 2, XM, TMT).then_inc(sem("gdn_p1"), 1)
                    pe.wait_ge(sem("gdn_p1out"), lev)
                    each(psG, 0, TMT, P1)
                    each(psS, 0, TM, Q1).then_inc(sem("gdn_r"), 1)
                pe.wait_ge(sem("gdn_t"), 7)
                each(psA, 0, KBG, TMT)
                each(psA, 2, TMT, VB).then_inc(sem("gdn_wu"), 1)
                pe.wait_ge(sem("gdn_wuout"), 1)
                for h in range(GH):
                    mm(psG[:, 0, h * P:(h + 1) * P], KDEC[:, 2 * h, :], UU[:, 2 * h, :],
                       start=(h == 0), stop=True)
                    last = mm(psS[:, 0, h * P:(h + 1) * P], UU[:, 2 * h, :], ATT[:, 2 * h, :],
                              start=(h == 0), stop=True)
                last.then_inc(sem("gdn_s1"), 1)
                pe.wait_ge(sem("gdn_state"), 1)
                for h in range(GH):
                    last = mm(psG[:, 1, h * P:(h + 1) * P], WT[:, 2 * h + 1, :], SST[:, h, :],
                              start=(h == 0), stop=True)
                last.then_inc(sem("gdn_ws"), 1)
                pe.wait_ge(sem("gdn_vnew"), 1)
                for h in range(GH):
                    mm(psS[:, 1, h * P:(h + 1) * P], SST[:, h, :], ER[:, 2 * h + 1, :],
                       start=(h == 0), stop=False)
                    last = mm(psS[:, 1, h * P:(h + 1) * P], VNEW[:, h, :], ATT[:, 2 * h + 1, :],
                              start=False, stop=True)
                last.then_inc(sem("gdn_o1"), 1)
                pe.wait_ge(sem("gdn_osq"), 1)
                for b in range(2):
                    last = mm(psA[:, b, :], ones, blk(0)[:, b * 512:(b + 1) * 512], start=True, stop=True)
                last.then_inc(chunk_used, 1)

            def merge():
                c = BASE["mrg"]
                pe.wait_ge(sem("yg_ready"), 1)
                branch = [YA, YN, YG]
                for j in range(24):
                    m, r = divmod(j, 3)
                    cc, s = c + j // 2, j % 2
                    arrived(pe, cc)
                    if j >= 2:
                        pe.wait_ge(sem("mrg_out"), j - 1)
                    for k in range(KT):
                        mm(psG[:, j % 2, 0:S], chunk(cc, s * SLOT + k * P, s * SLOT + k * P + P), H[:, k, :],
                           start=(k == 0), stop=(k == KT - 1))
                    for k in range(4):
                        a = 2 * SLOT + (s * 4 + k) * P
                        last = mm(psG[:, j % 2, S:2 * S], chunk(cc, a, a + P), branch[r][:, k, :],
                                  start=False, stop=(k == 3))
                    last.then_inc(sem("mrg_ps"), 1)
                    if s == 1:
                        pe.wait_ge(sem("mrg_ps"), j + 1)
                        pe.sem_inc(chunk_used, 1)
                c = BASE["out"]
                for m in range(KT):
                    cc, s = c + m // 3, m % 3
                    arrived(pe, cc)
                    for k in range(KT):
                        if m == 0 and k == 0:
                            pe.wait_ge(sem("merged"), KT)
                        last = mm(psA[:, m // 2, (m % 2) * S:(m % 2 + 1) * S],
                                  chunk(cc, s * SLOT + k * P, s * SLOT + k * P + P), Y[:, k, :],
                                  start=(m % 2 == 0 and k == 0), stop=(k == KT - 1))
                    if s == 2:
                        last.then_inc(chunk_used, 1)
                last.then_inc(sem("hyb_acc"), 1)

            def router():
                c = BASE["out"] + 2
                for t in range(TT):
                    for k in range(KT):
                        pe.wait_ge(h_ready, 8 * 7 + k + 1)
                        a = 2 * SLOT + k * 36
                        last = mm(psS[:, 1, t * 36:(t + 1) * 36], H[:, k, t * P:(t + 1) * P],
                                  chunk(c, a, a + 36), start=(k == 0), stop=(k == KT - 1))
                last.then_inc(chunk_used, 1)
                pe.wait_ge(sem("rt_gate"), 1)
                for t in range(TT):
                    last = nc.tensor.transpose(psS[0:E, 0, t * P:(t + 1) * P], blk(24)[:, t * E:(t + 1) * E], ident)
                last.then_inc(sem("rt_tr"), 1)
                pe.wait_ge(sem("rt_gt"), 1)
                for j in range(E // 2):
                    if j >= 2:
                        pe.wait_ge(sem("rt_bc"), j - 1)
                    for i in range(2):
                        e = 2 * j + i
                        last = mm(psG[:, j % 2, i * S:(i + 1) * S],
                                  ident[0:E, e:e + 1].to_broadcast([E, P]), blk(25)[0:E, 0:S],
                                  start=(i == 0), stop=True)
                    last.then_inc(sem("rt_ps"), 1)
                pe.wait_ge(sem("rt_bc"), E // 2)

            ada(0)
            pre_norm(0)
            ffn(BASE["ffn0"], 0, NF, 0)
            post_norm(0)
            pre_norm(1)
            pool()
            post_norm(1)
            pre_norm(2)
            ffn(BASE["ffn1"], NF, NF, 2)
            post_norm(2)
            pe.wait_ge(sem("root_ready"), 6)
            ada(1)
            pre_norm(3)
            ffn(BASE["ffn2"], 2 * NF, NF, 3)
            post_norm(3)
            pre_norm(4)
            mla()
            post_norm(4)
            pre_norm(5)
            ffn(BASE["ffn3"], 3 * NF, NF, 5)
            post_norm(5)
            pre_norm(6)
            hybrid_in()
            nsa()
            gdn()
            merge()
            pre_norm(7)
            router()
            ffn(BASE["moe"], 4 * NF, E * FE, 7)

        @block.scalar
        def _(ac):
            A = nc.scalar.activation
            ch = Chain(ac, "act_step")

            def root(dst, ps, scale):
                A(dst, ps, ACT.Sqrt, bias=eps[:, 0:1], scale=scale).then_inc(sem("root_ready"), 1)

            def pre_norm(n):
                ac.wait_ge(x_ready, n + 1)
                A(SQ[:, 0:4, :], X[:, 0:4, :], ACT.Square).then_inc(sem("pre_sq_act"), 1)
                ac.wait_ge(sem("pre_sum"), n + 1)
                root(rstd[:, :], psS[:, 0, 0:S], 1.0 / D)

            def post_norm(n):
                for b in range(4):
                    ac.wait_ge(sem("y_ready"), 4 * n + b + 1)
                    A(SQ[:, 2 * b:2 * b + 2, :], Y[:, 2 * b:2 * b + 2, :], ACT.Square).then_inc(sem("post_sq"), 1)
                ac.wait_ge(sem("post_sum"), n + 1)
                root(rstd[:, :], psS[:, 0, 0:S], 1.0 / D)

            def ffn(t0, nf):
                def one(i, t):
                    ac.wait_ge(sem("gu_ready"), i + (t + 1))
                    if t >= 2:
                        ac.wait_ge(sem("act_ready"), i + (t - 1))
                    A(sg[:, t % 2, :], psG[:, t % 2, 0:S], ACT.Silu).then_inc(sem("silu_ready"), 1)
                one(0, t0)
                one(0, t0 + 1)
                with ac.Fori(0, nf - 2, 2) as i:
                    one(i, t0 + 2)
                    one(i, t0 + 3)

            def attention(n, p, src, dst, width, copy, extra):
                for u in range(-1, n + 1):
                    if u + 1 < n:
                        v = u + 1
                        ac.wait_ge(sem(p + "max"), v + 1)
                        if v >= 2:
                            ac.wait_ge(sem(p + "tr"), v - 1)
                        for t in range(TT):
                            w = width(v)
                            A(dst(v)[:, t * S:t * S + w], src(v)[:, t * S:t * S + w], ACT.Exp,
                              bias=NMAX[:, v % 2, t:t + 1],
                              accum_out=SUM[:, v % 2, t:t + 1]).then_inc(sem(p + "exp"), 1)
                    if 0 <= u < n:
                        ac.wait_ge(sem(p + "tr"), u + 1)
                        if u >= 2:
                            ac.wait_ge(sem(p + "pv"), u - 1)
                        copy(u).then_inc(sem(p + "pt"), 1)
                    extra(u)

            def mla():
                ac.wait_ge(sem("mla_lat"), 1)
                for m in range(4):
                    A(LAT[:, m, :], psA[:, m, 0:S], ACT.Copy)
                for m in range(3):
                    last = A(ROT[:, m, :], psA[:, m, 0:S], ACT.Square)
                last.then_inc(sem("mla_sq"), 1)
                ac.wait_ge(sem("mla_sum"), 1)
                root(rstd[:, :], psS[:, 0, 0:S], 1.0 / 256)
                root(CQN[:, 3, :], psS[:, 1, 0:S], 1.0 / 128)
                for g in range(3):
                    if g < 2:
                        ac.wait_ge(sem("mla_qps"), 1) if g == 0 else ac.wait_ge(chunk_used, BASE["mla"] + 2)
                    else:
                        ac.wait_ge(sem("mla_qps"), 2)
                    for b in range(4):
                        if g < 2:
                            last = A(QN[:, 4 * g + b, :], psA[:, b, 0:S], ACT.Copy)
                        else:
                            last = A(QR[:, b, :], psA[:, b, 0:S], ACT.Copy)
                    last.then_inc(sem("mla_q"), 1)

                def extra(u):
                    if u + 2 < HEADS:
                        query(u + 2)
                    if u >= 1:
                        h = u - 1
                        ac.wait_ge(sem("mla_pv"), h + 1)
                        if h >= 2:
                            ac.wait_ge(sem("mla_up"), h - 1)
                        A(OL[:, h % 2, :], psG[:, h % 2, 0:S], ACT.Copy).then_inc(sem("mla_ol"), 1)

                def query(h):
                    ac.wait_ge(sem("mla_qlps"), h + 1)
                    if h >= 2:
                        ac.wait_ge(sem("mla_score"), h - 1)
                    A(QL[:, h % 2, :], psS[:, 0, 0:S], ACT.Copy, scale=MLA_SCALE).then_inc(sem("mla_ql"), 1)

                query(0)
                attention(HEADS, "mla_", lambda u: psA[:, u % 2, :], lambda u: PB[:, u % 2, :], lambda u: S,
                          lambda u: A(PTB[:, u % 2, :], psA[:, 2 + u % 2, :], ACT.Copy), extra)

            def hybrid_in():
                dst = [UA[:, 2 * j:2 * j + 2] for j in range(6)] + [UQ[:, 0:2], UQ[:, 2:4]]
                dst += [UK[:, 0:2], UK[:, 2:4], UKV[:, 0:2], UKV[:, 2:4]]
                dst += [UG[:, 2 * j:2 * j + 2] for j in range(6)] + [UZ[:, 0:2], UZ[:, 2:4]]
                for j in range(20):
                    ac.wait_ge(sem("u_ps"), j + 1)
                    src = psG[:, j % 2, :].rearrange("p (a s) -> p a s", a=2)
                    if j in (8, 9):
                        A(dst[j][0:64], src[0:64], ACT.Copy)
                        A(dst[j][64:P, :, 0:S - 1], src[64:P, :, 1:S], ACT.Copy).then_inc(sem("u_out"), 1)
                    else:
                        A(dst[j], src, ACT.Silu if j >= 18 else ACT.Copy).then_inc(sem("u_out"), 1)
                ac.wait_ge(chunk_used, BASE["hyb"] + 14)
                ch.link(A(GT, psS[:, 0, 0:64].rearrange("p (t c) -> p t c", t=2), ACT.Copy), "gt_out")
                A(GATE, GT[:, :, 0:24], ACT.Sigmoid).then_inc(sem("gate_sig"), 1)
                beta = BETA.rearrange("p (t h) -> p t h", t=2)
                A(beta, GT[:, :, 24:28], ACT.Sigmoid).then_inc(sem("beta_ready"), 1)

            def nsa():
                A(SQ[:, 0:4, :], UQ, ACT.Square)
                ch.link(A(SQ[:, 4:6, :], UKV[:, 0:3:2, :], ACT.Square), "nsa_sq")
                ac.wait_ge(sem("cmp_hid"), 1)
                A(HID.rearrange("p y m g c -> p (y m) (g c)"), psA[:, :, 0:2 * NCMP],
                  ACT.Gelu_apprx_tanh).then_inc(sem("hid_ready"), 1)
                ac.wait_ge(sem("cmp_out"), 1)
                A(SQ[:, 6, 0:2 * NCMP], psG[:, 0, 0:2 * NCMP], ACT.Square).then_inc(sem("nsa_sqc"), 1)

                ac.wait_ge(sem("nsa_sum"), 1)
                root(SQ[:, 0:6, :].rearrange("p (b a) s -> p b (a s)", a=2), psA[:, 0:3, :], 1.0 / 64)
                root(SQ[:, 6, 0:2 * NCMP], psA[:, 3, 0:2 * NCMP], 1.0 / 64)

                def copy(u):
                    if NSA_UNITS[u][1] == 0:
                        return A(NPTB[0:NCMP, u % 2, 0:S], psA[0:NCMP, 2 + u % 2, 0:S], ACT.Copy)
                    return A(NPTB[:, u % 2, :], psA[:, 2 + u % 2, :], ACT.Copy)

                def extra(u):
                    if u >= 1 and u % 6 == 0:
                        ac.wait_ge(sem("nsa_pv"), u)
                        t = u // 6 - 1
                        A(YN[:, t, :], psG[:, t % 2, 0:S], ACT.Copy).then_inc(sem("nsa_o"), 1)

                attention(len(NSA_UNITS), "nsa_", lambda u: NPB[:, u % 2, :], lambda u: NPB[:, u % 2, :],
                          lambda u: NCMP if NSA_UNITS[u][1] == 0 else S, copy, extra)

            def gdn():
                ac.wait_ge(sem("gdn_z"), 1)
                A(AL, col("a_log", 0, 4), ACT.Exp)
                ch.link(A(EGC, GX, ACT.Abs))
                ch.link(A(EGC, EGC, ACT.Exp, scale=-1.0))
                A(EGC, EGC, ACT.Ln, bias=ones[:, 0:1]).then_inc(sem("gdn_ln"), 1)
                ac.wait_ge(sem("gdn_conv"), 1)
                ch.link(A(blk(16, 3), blk(16, 3), ACT.Silu), "gdn_cv")
                A(blk(2, 2), blk(16, 2), ACT.Square).then_inc(sem("gdn_sq"), 1)
                ac.wait_ge(sem("gdn_sum"), 1)
                root(blk(2, 2).rearrange("p (b n) -> p b n", b=4), psA[:, :, :], 1.0)
                ac.wait_ge(sem("gdn_diff"), 1)
                A(ER.rearrange("p u s -> p (u s)").rearrange("p (b n) -> p b n", b=2), psG[:, :, :],
                  ACT.Exp).then_inc(sem("gdn_er"), 1)
                A(blk(22), blk(22), ACT.Exp, scale=-1.0)
                A(EGC, GC, ACT.Exp)
                A(KD, GX, ACT.Exp).then_inc(sem("gdn_exps"), 1)
                ac.wait_ge(sem("gdn_lt"), 1)
                A(blk(25).rearrange("p (b n) -> p b n", b=2), psA[:, 0:2, :], ACT.Copy).then_inc(sem("gdn_ltout"), 1)
                A(blk(6).rearrange("p (b n) -> p b n", b=2), psA[:, 2:4, :], ACT.Copy).then_inc(sem("gdn_att"), 1)
                for lev in range(1, 7):
                    ac.wait_ge(sem("gdn_p1"), lev)
                    A(blk(11).rearrange("p (b n) -> p b n", b=2), psA[:, 0:2, :], ACT.Copy)
                    A(blk(12).rearrange("p (b n) -> p b n", b=2), psA[:, 2:4, :], ACT.Copy)\
                        .then_inc(sem("gdn_p1out"), 1)
                ac.wait_ge(sem("gdn_wu"), 1)
                A(blk(0).rearrange("p (b n) -> p b n", b=2), psA[:, 0:2, :], ACT.Copy)
                A(blk(1).rearrange("p (b n) -> p b n", b=2), psA[:, 2:4, :], ACT.Copy).then_inc(sem("gdn_wuout"), 1)
                ac.wait_ge(sem("gdn_o1"), 1)
                A(OT[:, :, 0, :], psS[:, 0, :].rearrange("p (h s) -> p h s", h=GH), ACT.Copy)
                ch.link(A(OT[:, :, 1, :], psS[:, 1, :].rearrange("p (h s) -> p h s", h=GH), ACT.Copy))
                A(blk(0), blk(3), ACT.Square).then_inc(sem("gdn_osq"), 1)
                ac.wait_ge(chunk_used, msk + 1)
                root(blk(0).rearrange("p (b n) -> p b n", b=2), psA[:, 0:2, :], 1.0 / P)

            def merge():
                for j in range(24):
                    m, r = divmod(j, 3)
                    ac.wait_ge(sem("mrg_ps"), j + 1)
                    if j >= 2:
                        ac.wait_ge(sem("mrg_out"), j - 1)
                    A(sg[:, j % 2, :], psG[:, j % 2, 0:S], ACT.Sigmoid,
                      bias=col("b_gate", 8 * r + m)).then_inc(sem("mrg_sig"), 1)

            def router():
                ac.wait_ge(sem("rt_max"), 1)
                A(blk(24)[:, 256:264], blk(24)[:, 256:264], ACT.Exp)
                A(blk(24)[:, 128:192], blk(24)[:, 128:192], ACT.Exp).then_inc(sem("rt_exp"), 1)
                for j in range(E // 2):
                    ac.wait_ge(sem("rt_ps"), j + 1)
                    A(GB[:, j * 512:(j + 1) * 512], psG[:, j % 2, :], ACT.Copy).then_inc(sem("rt_bc"), 1)

            ac.wait_ge(sem("cols_in"), 16)
            A(silc[:, :], col("c", 0, 8), ACT.Silu).then_inc(sem("silc_ready"), 1)
            pre_norm(0)
            ffn(0, NF)
            post_norm(0)
            pre_norm(1)
            post_norm(1)
            pre_norm(2)
            ffn(NF, NF)
            post_norm(2)
            pre_norm(3)
            ffn(2 * NF, NF)
            post_norm(3)
            pre_norm(4)
            mla()
            post_norm(4)
            pre_norm(5)
            ffn(3 * NF, NF)
            post_norm(5)
            pre_norm(6)
            hybrid_in()
            nsa()
            gdn()
            merge()
            pre_norm(7)
            router()
            ffn(4 * NF, E * FE)

        @block.vector
        def _(ve):
            V = nc.vector
            ch = Chain(ve, "dve_step")
            link = ch.link

            def ada(layer):
                ve.wait_ge(chunk_used, BASE[f"ada{layer}"] + 24)
                link(V.tensor_tensor(mod[:, layer, :], psS[:, 0, 0:72], col("ada_b", 72 * layer, 72), ALU.add))
                m = mod[:, layer, :].rearrange("p (s q k) -> p s q k", s=3, q=3)
                g = col("norm_g", 48 * layer, 48).rearrange("p (s q k) -> p s q k", s=3, q=2)
                V.scalar_tensor_tensor(modA[:, layer], m[:, :, 1, :], 1.0, g[:, :, 0, :], ALU.add, ALU.mult)
                link(V.scalar_tensor_tensor(modC[:, layer], m[:, :, 2, :], 1.0, g[:, :, 1, :], ALU.add, ALU.mult))
                link(V.tensor_scalar(modC[:, layer, 0:3:2], modC[:, layer, 0:3:2], 0.5, None, ALU.mult))

            roots = Chain(ve, "root_used")

            def root(dst):
                n = roots.n.get("root_used", 0) + 1
                ve.wait_ge(sem("root_ready"), n)
                roots.link(V.reciprocal(dst, dst))

            def pre_norm(n):
                V.tensor_tensor(SQ[:, 4:8, :], X[:, 4:8, :], X[:, 4:8, :], ALU.mult).then_inc(sem("pre_sq_dve"), 1)
                root(rstd[:, :])
                scale, shift = pre_cols(n)
                for b in range(2):
                    link(V.tensor_tensor(H[:, 4 * b:4 * b + 4, :], X[:, 4 * b:4 * b + 4, :],
                                         rstd[:, None, :].to_broadcast([P, 4, S]), ALU.mult))
                    for k in range(4 * b, 4 * b + 4):
                        if shift is None:
                            ins = V.tensor_scalar(H[:, k, :], H[:, k, :], scale(k), None, ALU.mult)
                        else:
                            ins = V.tensor_scalar(H[:, k, :], H[:, k, :], scale(k), shift(k), ALU.mult, ALU.add)
                        ins.then_inc(h_ready, 1)

            def post_norm(n, done, layer, s, from_acc=True):
                if from_acc:
                    ve.wait_ge(chunk_used, done)
                    for b in range(4):
                        V.tensor_copy(Y[:, 2 * b:2 * b + 2, :], psA[:, b, :].rearrange("p (a s) -> p a s", a=2))\
                            .then_inc(sem("y_ready"), 1)
                root(rstd[:, :])
                for k in range(KT):
                    last = V.scalar_tensor_tensor(Y[:, k, :], Y[:, k, :], modC[:, layer, s, k:k + 1], rstd[:, :],
                                                  ALU.mult, ALU.mult)
                link(last)
                link(V.tensor_tensor(X[:, :, :], X[:, :, :], Y, ALU.add), "x_ready")

            def ffn(t0, nf, gated=False):
                def one(i, t, f=0, e=None):
                    ve.wait_ge(sem("silu_ready"), i + (t + 1))
                    if not gated:
                        V.tensor_tensor(act[:, t % 2, :], sg[:, t % 2, :], psG[:, t % 2, S:2 * S],
                                        ALU.mult).then_inc(sem("act_ready"), 1)
                        return
                    gate = GB[:, bass.ds(e * S, S)]
                    V.tensor_tensor(sg[:, t % 2, :], sg[:, t % 2, :], gate, ALU.mult)\
                        .then_inc(sem("gated"), 1)
                    ve.wait_ge(sem("gated"), i + (f + 1))
                    V.tensor_tensor(act[:, t % 2, :], sg[:, t % 2, :], psG[:, t % 2, S:2 * S],
                                    ALU.mult).then_inc(sem("act_ready"), 1)
                if gated:
                    with ve.Fori(0, E) as e:
                        for j in range(FE):
                            one(e * FE, t0 + j, j, e)
                else:
                    with ve.Fori(0, nf, 2) as i:
                        one(i, t0)
                        one(i, t0 + 1)

            def pool():
                c = BASE["pool"]
                arrived(ve, c)
                w = S + 16
                pa = blk(4, 3)[:, 0:8 * w].rearrange("p (k s) -> p k s", s=w)
                pb = blk(7, 3)[:, 0:8 * w].rearrange("p (k s) -> p k s", s=w)
                V.memset(blk(4, 3)[:, 0:8 * w], 0.0)
                link(V.memset(blk(7, 3)[:, 0:8 * w], 0.0))
                link(V.tensor_copy(pa[:, :, 8:8 + S], H[:, :, :]))
                link(V.tensor_tensor(pb[:, :, 1:w], pa[:, :, 0:w - 1], pa[:, :, 1:w], ALU.add))
                link(V.tensor_tensor(pa[:, 2:8, 1:w - 1], pb[:, 2:8, 0:w - 2], pb[:, 2:8, 2:w], ALU.add))
                link(V.tensor_tensor(pb[:, 4:8, 2:w - 2], pa[:, 4:8, 0:w - 4], pa[:, 4:8, 4:w], ALU.add))
                link(V.tensor_tensor(pa[:, 6:8, 4:w - 4], pb[:, 6:8, 0:w - 8], pb[:, 6:8, 8:w], ALU.add))
                for g in range(4):
                    src = (pb, pa, pb, pa)[g]
                    inv = chunk(c, 2048 + g * S, 2048 + (g + 1) * S)
                    last = V.tensor_tensor(SQ[:, 2 * g:2 * g + 2, :], src[:, 2 * g:2 * g + 2, 8:8 + S],
                                           inv[:, None, :].to_broadcast([P, 2, S]), ALU.mult)
                link(last)
                link(V.tensor_tensor(SQ[:, :, :], SQ[:, :, :], H[:, :, :], ALU.subtract), "pooled")
                ve.wait_ge(chunk_used, c + 1)
                for m in range(KT):
                    last = V.tensor_scalar(Y[:, m, :], psA[:, m // 2, (m % 2) * S:(m % 2 + 1) * S],
                                           col("pool_b", m), col("pool_scale", m), ALU.add, ALU.mult)
                    if m % 2 == 1:
                        last.then_inc(sem("y_ready"), 1)

            def attention(n, p, first, finish):
                for u in range(-1, n):
                    if u + 1 < n:
                        v = u + 1
                        ve.wait_ge(sem(p + "score"), v + 1)
                        first(v)
                    if u >= 0:
                        ve.wait_ge(sem(p + "exp"), 2 * u + 2)
                        finish(u)

            def negate_max(src, u, name):
                link(V.tensor_reduce(FAC[:, u % 2, :], src, AX.X, ALU.max))
                link(V.tensor_scalar(NMAX[:, u % 2, :], FAC[:, u % 2, :], -1.0, None, ALU.mult), name)

            def mla():
                c = BASE["mla"]
                root(rstd[:, :])
                for k in range(2):
                    V.scalar_tensor_tensor(CQN[:, k, :], LAT[:, k, :], col("q_norm", k), rstd[:, :],
                                           ALU.mult, ALU.mult)
                root(CQN[:, 3, :])
                link(V.scalar_tensor_tensor(CQN[:, 2, :], LAT[:, 2, :], col("kv_norm", 0), CQN[:, 3, :],
                                            ALU.mult, ALU.mult), "mla_cqn")
                ve.wait_ge(sem("mla_rot"), 1)
                arrived(ve, c + 3)
                cos = chunk(c + 3, 2 * SLOT, 2 * SLOT + S)
                sin = chunk(c + 3, 2 * SLOT + S, 2 * SLOT + 2 * S)
                link(V.tensor_tensor(ROT, psA[:, 0:2, :].rearrange("p b (a s) -> p (b a) s", a=2),
                                     sin[:, None, :].to_broadcast([P, 4, S]), ALU.mult))
                link(V.tensor_tensor(QR, QR, cos[:, None, :].to_broadcast([P, 4, S]), ALU.mult))
                link(V.tensor_tensor(QR, QR, ROT, ALU.add))
                link(V.tensor_scalar(QR, QR, MLA_SCALE, None, ALU.mult))
                link(V.tensor_tensor(ROT[:, 0, :], psG[:, 0, 0:S], sin, ALU.mult))
                link(V.tensor_tensor(LAT[:, 3, :], LAT[:, 3, :], cos, ALU.mult))
                link(V.tensor_tensor(LAT[:, 3, :], LAT[:, 3, :], ROT[:, 0, :], ALU.add))
                link(V.memset(KRM, 0.0))
                for j in range(4):
                    V.tensor_copy(KRM[32 * j:32 * j + 32, j, :], LAT[32 * j:32 * j + 32, 3, :])
                link(V.tensor_copy(KVTOK, psG[:, 1, 0:S].rearrange("p (t c) -> p t c", t=2)), "mla_ready")

                def first(u):
                    negate_max(psA[:, u % 2, :].rearrange("p (t s) -> p t s", t=2), u, "mla_max")

                def finish(u):
                    link(V.reciprocal(FAC[:, u % 2, :], SUM[:, u % 2, :]))
                    for t in range(TT):
                        last = V.tensor_scalar(PB[:, u % 2, t * S:(t + 1) * S], PB[:, u % 2, t * S:(t + 1) * S],
                                               FAC[:, u % 2, t:t + 1], None, ALU.mult)
                    last.then_inc(sem("mla_p"), 1)
                    if u % 2 == 1 and u >= 3:
                        out(u - 2)

                def out(h):
                    ve.wait_ge(sem("mla_up"), h + 1)
                    V.tensor_copy(MO[:, h // 2, :], psS[:, 1, 0:S]).then_inc(sem("mla_o"), 1)

                attention(HEADS, "mla_", first, finish)
                out(HEADS - 1)

            def small():
                ve.wait_ge(sem("u_out"), 6)
                link(V.tensor_tensor(UA[:, 4:8, :], UA[:, 4:8, :], UA[:, 8:12, :], ALU.mult))
                for j in (2, 1, 0):
                    d = 2 - j
                    for k in range(4):
                        w = col("conv_a", 4 * j + k)
                        if d == 0:
                            last = V.tensor_scalar(UA[:, 8 + k, :], UA[:, 4 + k, :], w, None, ALU.mult)
                        else:
                            last = V.scalar_tensor_tensor(UA[:, 8 + k, d:S], UA[:, 4 + k, 0:S - d], w,
                                                          UA[:, 8 + k, d:S], ALU.mult, ALU.add)
                    link(last)
                link(V.tensor_tensor(YA, UA[:, 0:4, :], UA[:, 8:12, :], ALU.mult))
                ve.wait_ge(sem("u_out"), 10)
                for y in range(2):
                    pe_ = col("pe", 16 * y, 16)
                    for g in range(2):
                        base = UK[:, 2 * y + g, :]
                        src = base.copy()
                        src = windows(base)
                        V.tensor_tensor(BL[y][:, :, g, :], src, pe_[:, :, None].to_broadcast([P, 16, NCMP]),
                                        ALU.add).then_inc(sem("blocks_ready"), 1)

            def windows(base):
                a = list(base.ap)
                return bass.AP(tensor=base.tensor, offset=base.offset, ap=[list(a[0]), [2, 16], [16, NCMP]])

            def nsa():
                ve.wait_ge(sem("cmp_out"), 1)
                arrived(ve, msk)
                V.tensor_copy(VGC, psG[0:NCMP, 1, 0:2 * P].rearrange("p (g c) -> p g c", g=2))
                root(SQ[:, 0:6, :])
                root(SQ[:, 6, 0:2 * NCMP])
                link(V.scalar_tensor_tensor(UQ, UQ, col("qk_gain", 0), SQ[:, 0:4, :], ALU.mult, ALU.mult))
                V.tensor_scalar(UQ, UQ, 64 ** -0.5, None, ALU.mult)
                V.memset(KG, 0.0)
                for y in range(2):
                    last = V.scalar_tensor_tensor(UKV[:, 2 * y, :], UKV[:, 2 * y, :], col("qk_gain", 2 + y),
                                                  SQ[:, 4 + y, :], ALU.mult, ALU.mult)
                link(last)
                for y in range(2):
                    for g in range(2):
                        V.tensor_copy(KG[64 * g:64 * g + 64, y, g, :], UKV[64 * g:64 * g + 64, 2 * y, :])
                V.scalar_tensor_tensor(KGC, psG[:, 0, 0:2 * NCMP].rearrange("p (g c) -> p g c", g=2),
                                       col("qk_gain", 1),
                                       SQ[:, 6, 0:2 * NCMP].rearrange("p (g c) -> p g c", g=2),
                                       ALU.mult, ALU.mult)
                ve.wait_ge(sem("nsa_v"), 1)
                link(V.memset(VG, 0.0))
                for y in range(2):
                    for g in range(2):
                        V.tensor_copy(VG[:, y, :, g, 64 * g:64 * g + 64],
                                      psS[:, 1, y * S:(y + 1) * S].rearrange("p (t c) -> p t c", t=2)
                                      [:, :, 64 * g:64 * g + 64])
                ve.wait_ge(sem("gate_sig"), 1)
                for t in range(TT):
                    last = V.tensor_scalar(GATE[:, t, 0:8], GATE[:, t, 0:8], mask(M_OK + t, 1), None, ALU.mult)
                link(last, "nsa_ready")

                def first(u):
                    t, y, g = NSA_UNITS[u]
                    w = NCMP if y == 0 else S
                    slope = 2.0 ** (-(g * 4 + t + 1))
                    v3 = lambda a: a.rearrange("p (t s) -> p t s", t=2)[:, :, 0:w]
                    nd = mask(M_OK + 2, 2 * NCMP).rearrange("p (t s) -> p t s", t=2) if y == 0 else \
                        v3(mask(M_ND, 512))
                    if u >= 2:
                        ve.wait_ge(sem("nsa_tr"), u - 1)
                    link(V.scalar_tensor_tensor(v3(NPB[:, u % 2, :]), nd, slope, v3(psA[:, u % 2, :]),
                                                ALU.mult, ALU.add))
                    negate_max(v3(NPB[:, u % 2, :]), u, "nsa_max")

                def finish(u):
                    t, y, g = NSA_UNITS[u]
                    w = NCMP if y == 0 else S
                    link(V.reciprocal(FAC[:, u % 2, :], SUM[:, u % 2, :]))
                    link(V.tensor_tensor(FAC[:, u % 2, :], FAC[:, u % 2, :], GATE[:, :, y * 8 + g * 4 + t], ALU.mult))
                    for i in range(TT):
                        last = V.tensor_scalar(NPB[:, u % 2, i * S:i * S + w], NPB[:, u % 2, i * S:i * S + w],
                                               FAC[:, u % 2, i:i + 1], None, ALU.mult)
                    last.then_inc(sem("nsa_p"), 1)

                attention(len(NSA_UNITS), "nsa_", first, finish)

            def gdn():
                ve.wait_ge(sem("nsa_o"), NSA_T)
                z3 = GX.rearrange("p (t h) -> p t h", t=2)
                dt3 = col("dt", 0, 4)[:, None, :].to_broadcast([P, 2, 4])
                link(V.tensor_tensor(z3, GT[:, :, 28:32], dt3, ALU.add), "gdn_z")
                link(V.tensor_scalar(GG, GX, 0.0, None, ALU.max))
                for j in (3, 2, 1, 0):
                    d = 3 - j
                    for k in range(12):
                        w = col("conv_g", 12 * j + k)
                        if d == 0:
                            last = V.tensor_scalar(CV[:, k, :], UG[:, k, :], w, None, ALU.mult)
                        else:
                            last = V.scalar_tensor_tensor(CV[:, k, d:S], UG[:, k, 0:S - d], w, CV[:, k, d:S],
                                                          ALU.mult, ALU.add)
                    link(last, "gdn_conv" if j == 0 else None)
                ve.wait_ge(sem("gdn_ln"), 1)
                link(V.tensor_tensor(GG, GG, EGC, ALU.add))
                g3 = GG.rearrange("p (t h) -> p t h", t=2)
                link(V.tensor_tensor(g3, g3, AL[:, None, :].to_broadcast([P, 2, 4]), ALU.mult))
                link(V.tensor_scalar(GG, GG, -1.0, None, ALU.mult), "gdn_g")
                for u in range(NU):
                    h, n = divmod(u, 2)
                    last = V.tensor_scalar(DEC[:, u, :], mask(M_TRI), unit_col(GG, h, n), None, ALU.mult)
                link(last, "gdn_gu")
                ve.wait_ge(sem("gdn_gc"), 1)
                link(V.tensor_copy(GC, psS[:, 0, 0:NU]))
                root(blk(2, 2))
                V.scalar_tensor_tensor(blk(16), blk(16), P ** -0.5, blk(2), ALU.mult, ALU.mult)
                link(V.tensor_tensor(blk(17), blk(17), blk(3), ALU.mult), "gdn_qk")
                ve.wait_ge(sem("gdn_row"), 1)
                row = psG[:, :, :].rearrange("p b (u s) -> p (b u) s", u=4)
                for u in range(NU):
                    h, n = divmod(u, 2)
                    V.tensor_scalar(DEC[:, u, :], row[:, u, :], unit_col(GC, h, n), 0.0, ALU.subtract, ALU.max)
                rl = RL.rearrange("p (n h) -> p h n", n=2)
                link(V.tensor_copy(rl, row[:, :, P - 1:P].rearrange("p (h n) o -> p h (n o)", n=2)))
                link(V.tensor_tensor(GX, RL, GC, ALU.subtract), "gdn_diff")
                ve.wait_ge(sem("gdn_exps"), 1)
                ve.wait_ge(sem("beta_ready"), 1)
                link(V.tensor_tensor(DEC, DEC, mask(M_TRIL)[:, None, :].to_broadcast([P, NU, P]), ALU.mult))
                link(V.tensor_tensor(BG, BETA, EGC, ALU.mult))
                ve.wait_ge(sem("gdn_kv"), 1)
                for u in range(NU):
                    h, n = divmod(u, 2)
                    k = psA[:, u // 4, (u % 4) * P:(u % 4 + 1) * P]
                    v = psA[:, 2 + u // 4, (u % 4) * P:(u % 4 + 1) * P]
                    V.tensor_scalar(KBG[:, u, :], k, unit_col(BG, h, n), None, ALU.mult)
                    V.tensor_scalar(KDEC[:, u, :], k, unit_col(KD, h, n), None, ALU.mult)
                    last = V.tensor_scalar(VB[:, u, :], v, unit_col(BETA, h, n), None, ALU.mult)
                link(last, "gdn_kvtok")
                ve.wait_ge(sem("gdn_gram"), 1)
                for u in range(NU):
                    h, n = divmod(u, 2)
                    V.scalar_tensor_tensor(L_[:, u, :], psA[:, u // 4, (u % 4) * P:(u % 4 + 1) * P],
                                           unit_col(BETA, h, n), DEC[:, u, :], ALU.mult, ALU.mult)
                link(V.tensor_tensor(AT_, psA[:, 2:4, :].rearrange("p b (u s) -> p (b u) s", u=4), DEC, ALU.mult))
                link(V.tensor_tensor(L_, L_, mask(M_STRICT)[:, None, :].to_broadcast([P, NU, P]), ALU.mult), "gdn_l")
                ve.wait_ge(sem("gdn_er"), 1)
                rl2 = GX.rearrange("p (n h) -> p h n", n=2)
                link(V.tensor_copy(rl2, ER[:, :, P - 1:P].rearrange("p (h n) o -> p h (n o)", n=2)))
                link(V.tensor_tensor(ER, ER, blk(16).rearrange("p (u s) -> p u s", u=NU), ALU.mult))
                idb = ident[:, None, :].to_broadcast([P, NU, P])
                ve.wait_ge(sem("gdn_x"), 1)
                V.tensor_tensor(TM, idb, XM, ALU.subtract)
                link(V.tensor_tensor(TMT, idb, XMT, ALU.subtract), "gdn_t")
                for lev in range(1, 7):
                    ve.wait_ge(sem("gdn_r"), lev)
                    V.tensor_tensor(TM, TM, psG[:, :, :].rearrange("p b (u s) -> p (b u) s", u=4), ALU.subtract)
                    link(V.tensor_tensor(TMT, TMT, psS[:, :, :].rearrange("p b (u s) -> p (b u) s", u=4),
                                         ALU.subtract), "gdn_t")
                ve.wait_ge(sem("gdn_s1"), 1)
                link(V.tensor_copy(SST, psG[:, 0, :].rearrange("p (h s) -> p h s", h=GH)), "gdn_state")
                ve.wait_ge(sem("gdn_ws"), 1)
                link(V.tensor_tensor(VNEW, UU[:, 1:NU:2, :], psG[:, 1, :].rearrange("p (h s) -> p h s", h=GH),
                                     ALU.subtract), "gdn_vnew")
                root(blk(0))
                link(V.scalar_tensor_tensor(blk(3), blk(3), col("out_gain", 0), blk(0), ALU.mult, ALU.mult))
                link(V.tensor_tensor(blk(15), blk(3), blk(13), ALU.mult), "yg_ready")

            def merge():
                for j in range(24):
                    m, r = divmod(j, 3)
                    ve.wait_ge(sem("mrg_sig"), j + 1)
                    ps = psG[:, j % 2, S:2 * S]
                    if r == 0:
                        link(V.tensor_tensor(Y[:, m, :], sg[:, j % 2, :], ps, ALU.mult), "mrg_out")
                    else:
                        link(V.tensor_tensor(act[:, 0, :], sg[:, j % 2, :], ps, ALU.mult), "mrg_out")
                        link(V.tensor_tensor(Y[:, m, :], Y[:, m, :], act[:, 0, :], ALU.add),
                             "merged" if r == 2 else None)
                ve.wait_ge(sem("hyb_acc"), 1)
                add_acc()

            def add_acc():
                for b in range(4):
                    last = V.tensor_tensor(X[:, 2 * b:2 * b + 2, :], X[:, 2 * b:2 * b + 2, :],
                                           psA[:, b, :].rearrange("p (a s) -> p a s", a=2), ALU.add)
                link(last, "x_ready")

            def router():
                w = blk(24)
                LG = w[:, 192:192 + 72]
                lg3 = w[:, 192:264]
                G3 = w[:, 0:64].rearrange("p (t e) -> p t e", t=2)
                LE = w[:, 128:192].rearrange("p (t e) -> p t e", t=2)
                EXL = w[:, 256:264].rearrange("p (t e) -> p t e", t=2)
                LGT = w[:, 264:336].rearrange("p (t e) -> p t e", t=2)
                OH = w[:, 336:344].rearrange("p (t e) -> p t e", t=2)
                T1 = w[:, 384:448].rearrange("p (t e) -> p t e", t=2)
                O1 = w[:, 448:512].rearrange("p (t e) -> p t e", t=2)
                O2 = w[:, 512:576].rearrange("p (t e) -> p t e", t=2)
                W4 = w[:, 576:580]
                W32 = w[:, 584:616]
                Z = w[:, 640:656].rearrange("p (i t o) -> p i t o", i=8, t=2)
                for i in range(32):
                    V.memset(W32[:, i:i + 1], float(32 - i))
                for i in range(4):
                    V.memset(W4[:, i:i + 1], float(4 - i))
                ve.wait_ge(chunk_used, BASE["out"] + 3)
                rt = psS[:, 1, 0:72].rearrange("p (t c) -> p t c", t=2)
                b36 = col("b_rt", 0, 36)[:, None, :].to_broadcast([P, 2, 36])
                link(V.tensor_tensor(LGT, rt, b36, ALU.add))

                def first_max(src, weights, out, best, n):
                    link(V.tensor_reduce(Z[:, best], src, AX.X, ALU.max))
                    link(V.tensor_tensor(out, src, Z[:, best].to_broadcast([P, 2, n]), ALU.is_equal))
                    link(V.tensor_tensor(out, out, weights[:, None, :].to_broadcast([P, 2, n]), ALU.mult))
                    link(V.tensor_reduce(Z[:, 7], out, AX.X, ALU.max))
                    link(V.tensor_tensor(out, out, Z[:, 7].to_broadcast([P, 2, n]), ALU.is_equal))

                first_max(LGT[:, :, 0:4], W4, OH, 0, 4)
                link(V.tensor_tensor(EXL, LGT[:, :, 0:4], Z[:, 0].to_broadcast([P, 2, 4]), ALU.subtract))
                for t in range(2):
                    o4 = OH[:, t, :][:, :, None].to_broadcast([P, 4, 8])
                    le = LGT[:, t, 4:36].rearrange("p (g e) -> p g e", g=4)
                    link(V.tensor_tensor(LE[:, t, :].rearrange("p (g e) -> p g e", g=4), le, o4, ALU.mult))
                    link(V.tensor_scalar(OH[:, t, :], OH[:, t, :], 1.0, 1e30, ALU.subtract, ALU.mult))
                    link(V.tensor_tensor(LE[:, t, :].rearrange("p (g e) -> p g e", g=4),
                                         LE[:, t, :].rearrange("p (g e) -> p g e", g=4), o4, ALU.add))
                link(V.tensor_reduce(Z[:, 1], LE, AX.X, ALU.max))
                link(V.tensor_tensor(LE, LE, Z[:, 1].to_broadcast([P, 2, 32]), ALU.subtract), "rt_max")
                ve.wait_ge(sem("rt_exp"), 1)
                link(V.tensor_reduce(Z[:, 2], EXL, AX.X, ALU.add))
                first_max(LE, W32, O1, 3, 32)
                link(V.scalar_tensor_tensor(T1, O1, -2.0, LE, ALU.mult, ALU.add))
                first_max(T1, W32, O2, 4, 32)
                link(V.tensor_tensor(Z[:, 5], Z[:, 3], Z[:, 4], ALU.add))
                link(V.tensor_tensor(Z[:, 5], Z[:, 5], Z[:, 2], ALU.mult))
                link(V.reciprocal(Z[:, 5], Z[:, 5]))
                link(V.tensor_tensor(Z[:, 3], Z[:, 3], Z[:, 5], ALU.mult))
                link(V.tensor_tensor(Z[:, 4], Z[:, 4], Z[:, 5], ALU.mult))
                link(V.tensor_tensor(O1, O1, Z[:, 3].to_broadcast([P, 2, 32]), ALU.mult))
                link(V.tensor_tensor(O2, O2, Z[:, 4].to_broadcast([P, 2, 32]), ALU.mult))
                link(V.tensor_tensor(G3, O1, O2, ALU.add), "rt_gate")
                ve.wait_ge(sem("rt_tr"), 1)
                link(V.tensor_copy(blk(25)[0:E, 0:S], psS[0:E, 0, 0:S]), "rt_gt")
                ve.wait_ge(sem("rt_bc"), E // 2)

            ve.wait_ge(sem("x_in"), 16)
            V.memset(eps[:, :], EPS)
            ve.wait_ge(sem("cols_in"), 16)
            ada(0)
            link(V.memset(st[:, :], 0.0), "x_ready")
            pre_norm(0)
            ffn(0, NF)
            post_norm(0, BASE["ffn0"] + NF, 0, 0)
            pre_norm(1)
            ve.wait_ge(h_ready, 16)
            pool()
            post_norm(1, 0, 0, 1, from_acc=False)
            pre_norm(2)
            ffn(NF, NF)
            post_norm(2, BASE["ffn1"] + NF, 0, 2)
            ada(1)
            pre_norm(3)
            ffn(2 * NF, NF)
            post_norm(3, BASE["ffn2"] + NF, 1, 0)
            pre_norm(4)
            mla()
            post_norm(4, BASE["mla"] + 7, 1, 1)
            pre_norm(5)
            ffn(3 * NF, NF)
            post_norm(5, BASE["ffn3"] + NF, 1, 2)
            pre_norm(6)
            small()
            nsa()
            gdn()
            merge()
            pre_norm(7)
            router()
            ffn(4 * NF, E * FE, gated=True)
            ve.wait_ge(chunk_used, NCHUNK)
            add_acc()

        @block.gpsimd
        def _(po):
            for lev in range(7):
                if lev == 0:
                    po.wait_ge(sem("gdn_ltout"), 1)
                    po.wait_ge(sem("gdn_l"), 1)
                    arrived(po, msk)
                else:
                    if lev == 1:
                        po.wait_ge(sem("gdn_t"), 1)
                    else:
                        po.wait_ge(sem("gdn_p1"), lev - 1)
                low = mask(M_LOW + lev * P)[:, None, :].to_broadcast([P, NU, P])
                upp = mask(M_UPP + lev * P)[:, None, :].to_broadcast([P, NU, P])
                nc.gpsimd.tensor_tensor(XM, L_, low, ALU.mult)
                nc.gpsimd.tensor_tensor(XMT, LT, upp, ALU.mult).then_inc(sem("gdn_x"), 1)


def _slots(w):
    import numpy as np
    k, m = w.shape
    w = w.reshape(k // P, P, m // P, P).transpose(2, 1, 0, 3)
    return [np.ascontiguousarray(w[i]).reshape(P, -1) for i in range(m // P)]


def _pack_stream(a):
    import numpy as np
    out = np.zeros((NCHUNK, P, CHUNK), np.float32)

    def put(name, parts, at=0):
        c, w = BASE[name], at
        for p in parts:
            n = p.shape[1]
            while n:
                q, o = divmod(w, CHUNK)
                k = min(n, CHUNK - o)
                out[c + q, :p.shape[0], o:o + k] = p[:, p.shape[1] - n:p.shape[1] - n + k]
                w, n = w + k, n - k

    for i in range(DEPTH):
        put(f"ada{i}", _slots(a["ada_w"][i]))
    for j in range(4):
        w_in, w_out = a["ffn_w_in"][j // 2, j % 2], a["ffn_w_out"][j // 2, j % 2]
        up = w_in.reshape(KT, P, 2, NF, P)
        o = out[BASE[f"ffn{j}"]:BASE[f"ffn{j}"] + NF].reshape(NF, P, 3, SLOT)
        o[:, :, 0:2] = up.transpose(3, 1, 2, 0, 4).reshape(NF, P, 2, SLOT)
        o[:, :, 2] = w_out.reshape(NF, P, SLOT)
    pw = a["pool_w"][0].reshape(4, 2, P, 2, P).transpose(2, 0, 3, 1, 4).reshape(P, 2048)
    t = np.arange(S)
    inv = np.stack([1.0 / (np.clip(t + w // 2, 0, S) - np.clip(t - w // 2, 0, S)) for w in (2, 4, 8, 16)])
    put("pool", [pw, np.broadcast_to(inv.astype(np.float32).reshape(1, -1), (P, 1024))])

    w = a["mla_w_in"][0]
    w = np.concatenate([w[:, :384]] + [w[:, 384:416]] * 4, axis=1)
    uq = a["mla_w_uq"][0]
    uq = np.concatenate([uq[:, :, :64].reshape(256, 1024), uq[:, :, 64:].reshape(256, 512)], axis=1)
    uq = uq.reshape(2, P, 12, P).transpose(1, 2, 0, 3).reshape(P, 24 * P)
    uk = np.zeros((P, HEADS, P), np.float32)
    uv = np.zeros((P, HEADS, P), np.float32)
    for h in range(HEADS):
        b = 64 * (h % 2)
        uk[b:b + 64, h, :] = a["mla_w_uk"][0][:, h, :].T
        uv[:, h, b:b + 64] = a["mla_w_uv"][0][:, h, :]
    ang = np.arange(S, dtype=np.float32)[None, :] * \
        (1.0 / (np.float32(10000.0) ** (np.arange(0, 32, 2, dtype=np.float32) / 32)))[:, None].astype(np.float32)
    cos = np.tile(np.cos(ang).astype(np.float32), (8, 1))
    sin = np.tile(np.sin(ang).astype(np.float32), (8, 1))
    rot = np.zeros((P, P), np.float32)
    for p in range(P):
        if p % 32 < 16:
            rot[p + 16, p] = -1.0
        else:
            rot[p - 16, p] = 1.0
    put("mla", _slots(w) + [uq, uk.reshape(P, -1), uv.reshape(P, -1), cos, sin, rot])
    put("mla", _slots(a["mla_w_o"][0]), 4 * CHUNK)

    w = a["w_in_2"][0]
    ua, uq_, ukv, ung, ugq, uz, ub, uaa = np.split(w, np.cumsum([1536, 512, 768, 24, 1536, 512, 4]), axis=1)
    uq_ = uq_.reshape(D, 2, 4, 64).transpose(0, 2, 1, 3).reshape(D, 512)
    kv = ukv.reshape(D, 6, 2, 64)
    dup = [kv[:, y, g] for y in (0, 1) for g in (0, 1) for _ in (0, 1)]
    rest = [kv[:, y].reshape(D, P) for y in range(2, 6)]
    big = np.concatenate([ua, uq_] + dup + rest + [ugq, uz], axis=1)
    small = np.concatenate([ung, ub, uaa], axis=1).reshape(KT, P, 32).transpose(1, 0, 2).reshape(P, 256)
    put("hyb", _slots(big) + [small])

    w1 = a["cmp_w1_2"][0].reshape(2, 16, P, 256).transpose(0, 2, 1, 3).reshape(2, P, 4096)
    w2 = np.zeros((2, P, 2, 2, P), np.float32)
    for g in range(2):
        w2[:, :, :, g, 64 * g:64 * g + 64] = a["cmp_w2_2"][0].reshape(2, 2, P, 64).transpose(0, 2, 1, 3)
    put("cmp", [w1[0], w1[1], w2[0].reshape(P, 512), w2[1].reshape(P, 512)])

    m = np.zeros((P, CHUNK), np.float32)
    q = np.arange(P)
    for i in range(TT):
        dist = (q + P * i)[:, None] - np.arange(S)[None, :]
        m[:, i * S:(i + 1) * S] = np.where(dist >= 0, -dist, -1e33)
        dc = (q + P * i)[:, None] - (np.arange(NCMP) * 16 + 31)[None, :]
        m[:, M_OK + 2 + i * NCMP:M_OK + 2 + (i + 1) * NCMP] = np.where(dc >= 0, -dc, -1e33)
        m[:, M_OK + i] = (dc >= 0).any(axis=1)
    for lev in range(7):
        b = 1 << lev
        low = (q[:, None] // (2 * b) == q[None, :] // (2 * b)) & (q[:, None] // b % 2 == 1) & (q[None, :] // b % 2 == 0)
        m[:, M_LOW + lev * P:M_LOW + (lev + 1) * P] = low
        m[:, M_UPP + lev * P:M_UPP + (lev + 1) * P] = low.T
    m[:, M_STRICT:M_STRICT + P] = q[:, None] > q[None, :]
    m[:, M_TRIL:M_TRIL + P] = q[:, None] >= q[None, :]
    m[:, M_HALF:M_HALF + P] = q[:, None] // 64 == q[None, :] // 64
    m[:, M_TRI:M_TRI + P] = q[:, None] <= q[None, :]
    put("msk", [m])

    gate = a["w_gate_2"][0].reshape(KT, P, 3, KT, P)
    br = a["w_branch_2"][0].reshape(3, 512, D).copy()
    br[1] = br[1].reshape(2, 4, 64, D).transpose(1, 0, 2, 3).reshape(512, D)
    br = br.reshape(3, 4, P, KT, P)
    for j in range(24):
        mt, r = divmod(j, 3)
        c, s = BASE["mrg"] + j // 2, j % 2
        out[c, :, s * SLOT:(s + 1) * SLOT] = gate[:, :, r, mt].transpose(1, 0, 2).reshape(P, SLOT)
        out[c, :, 2 * SLOT + s * 512:2 * SLOT + s * 512 + 512] = br[r, :, :, mt].transpose(1, 0, 2).reshape(P, 512)
    wr = np.concatenate([a["w_router_group_2"][0], a["w_router_expert_2"][0]], axis=1)
    put("out", _slots(a["w_out_2"][0]) + [wr.reshape(KT, P, 36).transpose(1, 0, 2).reshape(P, 288)])
    o = out[BASE["moe"]:].reshape(E, FE, P, 3, SLOT)
    for s, name in enumerate(("w_expert_gate_2", "w_expert_up_2")):
        o[:, :, :, s] = a[name][0].reshape(E, KT, P, FE, P).transpose(0, 3, 2, 1, 4).reshape(E, FE, P, SLOT)
    o[:, :, :, 2] = a["w_expert_down_2"][0].reshape(E, FE, P, SLOT)
    return out


def _pack_cols(a):
    import numpy as np
    out = np.zeros((P, NCOL), np.float32)

    def put(name, v):
        i, j = COLS[name]
        out[:, i:j] = v

    def by_channel(v):
        return v.reshape(-1, P).T

    put("c", by_channel(a["c"]))
    put("ada_b", by_channel(a["ada_b"]))
    put("norm_g", by_channel(a["norm_g"]))
    for name, key in (("pool_b", "pool_b"), ("pool_scale", "pool_scale"), ("norm_mix", "norm_mix_2"),
                      ("norm_ffn", "norm_ffn_2"), ("b_gate", "b_gate_2"), ("q_norm", "mla_q_norm"),
                      ("kv_norm", "mla_kv_norm"), ("conv_a", "conv_a_w_2"), ("conv_g", "gdn_conv_w_2"),
                      ("out_gain", "gdn_out_gain_2")):
        put(name, by_channel(a[key]))
    put("qk_gain", np.concatenate([a["nsa_qk_gain_2"][0].T] * 2, axis=0))
    put("pe", a["cmp_pe_2"][0].reshape(2, 16, P).transpose(2, 0, 1).reshape(P, 32))
    put("b_rt", np.concatenate([a["b_router_group_2"][0], a["b_router_expert_2"][0]])[None, :])
    put("a_log", a["gdn_a_log_2"][0][None, :])
    put("dt", a["gdn_dt_bias_2"][0][None, :])
    return out


def kernel(**inputs):
    import numpy as np
    import concourse.bacc as bacc
    from concourse.bass_utils import run_bass_kernel_spmd as run

    a = {k: np.asarray(v) for k, v in inputs.items()}
    arrays = {
        "stream": _pack_stream(a),
        "cols_in": _pack_cols(a),
        "consts": np.concatenate([np.eye(P, dtype=np.float32), np.ones((P, P), np.float32)], axis=1),
        "x_in": np.ascontiguousarray(a["x"][0].T.reshape(KT, P, S).transpose(1, 0, 2)),
    }
    nc = bacc.Bacc("TRN2", target_bir_lowering=False, num_devices=1)
    args = [nc.dram_tensor(n, v.shape, F32, kind="ExternalInput").ap() for n, v in arrays.items()]
    out = nc.dram_tensor("x_out", (P, KT, S), F32, kind="ExternalOutput").ap()
    build(nc, *args, out)
    r = run(nc, [arrays], core_ids=[0])
    y = np.asarray(r.results[0]["x_out"])
    return np.ascontiguousarray(y.transpose(1, 0, 2).reshape(D, S).T)[None]
```

```python
from contextlib import ExitStack

import concourse.bass as bass
from concourse import mybir

F32 = mybir.dt.float32
ALU = mybir.AluOpType
ACT = mybir.ActivationFunctionType
AX = mybir.AxisListType

P = 128
S = 256
D = 1024
KT = D // P
TT = S // P
SLOT = KT * P
CHUNK = 3 * SLOT
RING = 6
EPS = 1e-6
DEPTH = 2
NF = 2816 // P
HEADS = 16
MLA_SCALE = (64 + 32) ** -0.5
NSA_T = 4
NCMP = 15
GH = 4
NU = GH * TT
E = 32
FE = 4
NP = E // 2
CAP = 64

ADA = [6, 18, 18, 6]
STAGES = [("ada", ADA[0]), ("ffn0", NF + ADA[1]), ("pool", 1), ("ffn1", NF + ADA[2]), ("ffn2", NF + ADA[3]),
          ("mla", 7), ("ffn3", NF), ("hyb", 14), ("cmp", 3), ("msk", 1), ("mrg", 12), ("out", 3),
          ("moe", E * FE)]
BASE = {}


def ffn_pos(f, na):
    return f + min(max(f - 1, 0), na)


_at = 0
for _n, _c in STAGES:
    BASE[_n] = _at
    _at += _c
NCHUNK = _at

COLS = {}
NCOL = 0
for _n, _c in [("c", 8), ("ada_b", 144), ("norm_g", 96), ("pool_b", 8), ("pool_scale", 8),
               ("norm_mix", 8), ("norm_ffn", 8), ("b_gate", 24), ("q_norm", 2), ("kv_norm", 1),
               ("conv_a", 12), ("conv_g", 48), ("qk_gain", 4), ("out_gain", 1), ("pe", 32),
               ("b_rt", 36), ("a_log", 4), ("dt", 4)]:
    COLS[_n] = (NCOL, NCOL + _c)
    NCOL += _c

M_ND, M_LOW, M_UPP = 0, 512, 512 + 7 * P
M_STRICT, M_TRIL, M_HALF, M_TRI, M_OK = 2304, 2432, 2560, 2688, 2816


def build(nc, stream, cols_d, ident_d, x_d, out_d):
    ctx = ExitStack()
    with ctx:
        def sb(name, shape):
            return ctx.enter_context(nc.sbuf_tensor(name, shape, F32))

        names = {}

        def sem(name):
            if name not in names:
                names[name] = ctx.enter_context(nc.semaphore(name))
            return names[name]

        ring = sb("ring", [P, RING, CHUNK])
        X = sb("X", [P, KT, S])
        H = sb("H", [P, KT, S])
        mem = sb("mem", [P, 26, 1024])
        cols = sb("cols", [P, NCOL])
        cst = sb("cst", [P, 3 * P + CAP])
        most = ctx.enter_context(nc.sbuf_tensor("most", [1, 1], mybir.dt.int32))
        mod = sb("mod", [P, DEPTH, 72])
        modA = sb("modA", [P, DEPTH, 3, KT])
        modC = sb("modC", [P, DEPTH, 3, KT])
        silc = sb("silc", [P, KT])
        rstd = sb("rstd", [P, S])
        act = sb("act", [P, 2, S])
        sg = sb("sg", [P, 2, S])
        eps = sb("eps", [P, 1])
        st = sb("st", [P, 512])
        psA = ctx.enter_context(nc.psum_tensor("psA", [P, 4, 512], F32))
        psG = ctx.enter_context(nc.psum_tensor("psG", [P, 2, 512], F32))
        psS = ctx.enter_context(nc.psum_tensor("psS", [P, 2, 512], F32))
        ident, ones, before = cst[:, 0:P], cst[:, P:2 * P], cst[:, 2 * P:3 * P]
        iota = cst[:, 3 * P:3 * P + CAP]

        def blk(i, n=1):
            return mem[:, i:i + n, :].rearrange("p a b -> p (a b)")

        def tiles(i, n=1, w=S):
            return blk(i, n).rearrange("p (t s) -> p t s", s=w)

        def col(name, i, n=1):
            a = COLS[name][0] + i
            return cols[:, a:a + n]

        def chunk(n, a=0, b=CHUNK):
            return ring[:, n % RING, a:b]

        Y, SQ = tiles(0, 2), tiles(2, 2)
        ADP = blk(24)[:, 0:6 * P].rearrange("p (b m n) -> p b m n", b=2, m=3)
        chunk_used, h_ready, x_ready = sem("chunk_used"), sem("h_ready"), sem("x_ready")
        full = [sem(f"chunk_full{j}") for j in range(RING)]

        def arrived(eng, n, i=0):
            if isinstance(i, int):
                eng.wait_ge(full[(n + i) % RING], 16 * ((n + i) // RING + 1))
            else:
                eng.wait_ge(full[n % RING], i * 16 // RING + 16 * (n // RING + 1))

        class Chain:

            def __init__(self, eng, name):
                self.eng, self.name, self.n = eng, name, {}

            def link(self, ins, name=None):
                name = name or self.name
                self.n[name] = self.n.get(name, 0) + 1
                ins.then_inc(sem(name), 1)
                self.eng.wait_ge(sem(name), self.n[name])

        def pre_cols(n):
            if n < 6:
                i, s = divmod(n, 3)
                return (lambda k: modA[:, i, s, k:k + 1]), (lambda k: mod[:, i, 24 * s + k:24 * s + k + 1])
            name = "norm_mix" if n == 6 else "norm_ffn"
            return (lambda k: col(name, k)), None

        block = ctx.enter_context(nc.Block())

        @block.sync
        def _(sp):
            sp.dma_start(cols[:, :], cols_d).then_inc(sem("cols_in"), 16)
            sp.dma_start(cst[:, :], ident_d).then_inc(sem("cst_in"), 16)
            for j in range(RING):
                sp.dma_start(ring[:, j, :], stream[j, :, :]).then_inc(full[j], 16)
                if j == 2:
                    sp.dma_start(X[:, :, :], x_d).then_inc(sem("x_in"), 16)
            whole = NCHUNK // RING * RING
            with sp.Fori(1, NCHUNK // RING) as r:
                i = r * RING
                for j in range(RING):
                    sp.wait_ge(chunk_used, i + (j + 1 - RING))
                    sp.dma_start(ring[:, j, :], stream[bass.ds(i + j, 1), :, :].rearrange("o p n -> (o p) n")).then_inc(full[j], 16)
            for n in range(whole, NCHUNK):
                sp.wait_ge(chunk_used, n + 1 - RING)
                sp.dma_start(ring[:, n % RING, :], stream[n, :, :]).then_inc(full[n % RING], 16)
            sp.wait_ge(x_ready, 9)
            sp.dma_start(out_d, X[:, :, :]).then_inc(sem("out_written"), 16)
            sp.wait_ge(sem("out_written"), 16)

        LAT, CQN, QN, QR, ROT, KRM = tiles(4), tiles(5), tiles(6, 2), tiles(8), tiles(9), tiles(10)
        KVTOK = blk(11)[:, 0:S].rearrange("p (t c) -> p t c", t=TT)
        QL = blk(11)[:, 512:1024].rearrange("p (b s) -> p b s", b=2)
        PB, PTB = tiles(12, 1, 512), tiles(13, 1, 512)
        OL = blk(14)[:, 0:512].rearrange("p (b s) -> p b s", b=2)
        MO = tiles(15, 2)
        UA, UQ, UK, UKV, UG, UZ = tiles(4, 3), tiles(7), tiles(8), tiles(9), tiles(10, 3), tiles(13)
        YN, YG = tiles(14), tiles(15)
        YA = tiles(5)
        KG = blk(16).rearrange("p (y g s) -> p y g s", y=2, g=2)
        VG = blk(17).rearrange("p (y t g c) -> p y t g c", y=2, t=TT, g=2)
        BL = [blk(18)[:, 512 * y:512 * y + 480].rearrange("p (l g c) -> p l g c", l=16, g=2) for y in range(2)]
        HID = blk(19)[:, 0:120].rearrange("p (y m g c) -> p y m g c", y=2, m=2, g=2)
        KGC = blk(19)[:, 128:128 + 2 * NCMP].rearrange("p (g c) -> p g c", g=2)
        VGC = blk(19)[0:NCMP, 256:512].rearrange("p (g c) -> p g c", g=2)
        KT_W = blk(19)[:, 512:768]
        NPB, NPTB = tiles(20, 1, 512), tiles(21, 1, 512)
        VTC = tiles(22)
        GT = st[:, 0:64].rearrange("p (t c) -> p t c", t=TT)
        GATE = st[:, 64:64 + 48].rearrange("p (t c) -> p t c", t=TT)
        NMAX = st[:, 120:124].rearrange("p (b t) -> p b t", b=2)
        SUM = st[:, 124:128].rearrange("p (b t) -> p b t", b=2)
        FAC = st[:, 128:132].rearrange("p (b t) -> p b t", b=2)
        BETA, GG, GC, EGC, KD, BG, GX = (st[:, 136 + 8 * i:144 + 8 * i] for i in range(7))
        AL = st[:, 200:204]
        RL = st[:, 208:216]

        def unit_col(t, h, n):
            return t[:, n * GH + h:n * GH + h + 1]

        def units(b):
            return blk(b).rearrange("p (u s) -> p u s", u=NU)

        CV = tiles(16, 3)
        KBG, KDEC, VB, DEC, ER, L_, LT = (units(i) for i in (19, 20, 21, 22, 23, 24, 25))
        TM, TMT, XM, XMT, P1, Q1 = (units(i) for i in (7, 8, 9, 10, 11, 12))
        AT_, ATT, WT, UU = units(4), units(6), units(0), units(1)
        SST = blk(2)[:, 0:512].rearrange("p (h s) -> p h s", h=GH)
        VNEW = blk(2)[:, 512:1024].rearrange("p (h s) -> p h s", h=GH)
        OT = blk(3).rearrange("p (h n s) -> p h n s", h=GH, n=2)
        QT, KTT, VT = CV[:, 0:4], CV[:, 4:8], CV[:, 8:12]
        ASG = blk(22)[:, 0:64].rearrange("p (t e) -> p t e", t=TT)
        POS = blk(22)[:, 64:128].rearrange("p (t e) -> p t e", t=TT)
        SEL, SELG, SELGT = blk(4, 4), blk(8, 4), blk(12, 4)
        HTOK, XE, YS = tiles(16, 2, D), tiles(18, 1, P), blk(20)
        HT = blk(19)[:, 0:512].rearrange("p (f s) -> p f s", f=FE)
        HACT, HSIL = blk(21)[:, 0:512], blk(21)[:, 512:1024]
        GB = blk(4, 8)
        HD = tiles(12, 2)

        msk = BASE["msk"]

        def mask(a, n=P):
            return chunk(msk, a, a + n)

        NSA_UNITS = [(t, y, g) for t in range(NSA_T) for y in range(3) for g in range(2)]

        @block.tensor
        def _(pe):
            def mm(out, lhsT, rhs, start, stop):
                return nc.tensor.matmul(out, lhsT, rhs, start=start, stop=stop, skip_group_check=True)

            pe.wait_ge(sem("cst_in"), 16)

            def ada(n, t, i=0):
                pe.wait_ge(sem("ada_prod"), i + (n + t + 1))
                for m in range(3):
                    at = psS[:, 1, 3 * t + m:3 * t + m + 1] if isinstance(i, int) else \
                        psS[:, 1, bass.ds(i * 3 + (3 * t + m), 1)]
                    last = mm(at, ADP[:, (n + t) % 2, m, :], ones[:, 0:1], start=True, stop=True)
                last.then_inc(chunk_used, 1)

            def pre_norm(n):
                pe.wait_ge(sem("pre_sq_act"), n + 1)
                pe.wait_ge(sem("pre_sq_dve"), n + 1)
                for k in range(KT):
                    last = mm(psS[:, 0, 0:S], ones, SQ[:, k, :], start=(k == 0), stop=(k == KT - 1))
                last.then_inc(sem("pre_sum"), 1)

            def post_norm(n):
                for k in range(KT):
                    if k % 2 == 0:
                        pe.wait_ge(sem("post_sq"), 4 * n + k // 2 + 1)
                    last = mm(psS[:, 0, 0:S], ones, SQ[:, k, :], start=(k == 0), stop=(k == KT - 1))
                last.then_inc(sem("post_sum"), 1)

            def ffn(c0, t0, nf, norm, na=0, n=0):
                def gate_up(i, f, shift=0):
                    c, t = c0 + f + shift, t0 + f
                    arrived(pe, c, i if isinstance(i, int) or not looped else i * 2)
                    if t >= 2:
                        pe.wait_ge(sem("act_ready"), i + (t - 1))
                    for u in range(2):
                        for k in range(KT):
                            if isinstance(i, int) and f == 0 and u == 0:
                                pe.wait_ge(h_ready, 8 * norm + k + 1)
                            last = mm(psG[:, t % 2, u * S:(u + 1) * S],
                                      chunk(c, u * SLOT + k * P, u * SLOT + k * P + P), H[:, k, :],
                                      start=(u == 0 and k == 0), stop=(u == 1 and k == KT - 1),)
                    last.then_inc(sem("gu_ready"), 1)

                def down(i, f, shift=0, first=False, final=False):
                    c, t = c0 + f + shift, t0 + f
                    pe.wait_ge(sem("act_ready"), i + (t + 1))
                    for m in range(KT):
                        last = mm(psA[:, m // 2, (m % 2) * S:(m % 2 + 1) * S],
                                  chunk(c, 2 * SLOT + m * P, 2 * SLOT + m * P + P), act[:, t % 2, :],
                                  start=(first and m % 2 == 0), stop=final)
                    last.then_inc(chunk_used, 1)

                looped = False
                gate_up(0, 0)
                gate_up(0, 1)
                down(0, 0, first=True)
                whole = (nf - 2) // RING * RING
                looped = True
                if na:
                    with pe.Fori(0, na, RING) as i:
                        for j in range(RING):
                            gate_up(i, 2 + j, j + 1)
                            down(i, 1 + j, j)
                            ada(n, j, i)
                looped = False
                if na < whole:
                    with pe.Fori(na, whole, RING) as i:
                        for j in range(RING):
                            gate_up(i, 2 + j, na)
                            down(i, 1 + j, na)
                for f in range(2 + whole, nf):
                    gate_up(0, f, na)
                    down(0, f - 1, na)
                down(0, nf - 1, na, final=True)

            def pool():
                c = BASE["pool"]
                arrived(pe, c)
                pe.wait_ge(sem("pooled"), 1)
                for m in range(KT):
                    g, dt = divmod(m, 2)
                    for k in range(2):
                        a = (g * 4 + dt * 2 + k) * P
                        last = mm(psA[:, m // 2, (m % 2) * S:(m % 2 + 1) * S], chunk(c, a, a + P),
                                  SQ[:, 2 * g + k, :], start=(m % 2 == 0 and k == 0),
                                  stop=(k == 1))
                last.then_inc(chunk_used, 1)

            def attention(n, p, prep, scores, blocks, product, after):
                for u in range(-1, n + 1):
                    if u + 1 < n:
                        prep(u + 1)
                        if u >= 1:
                            pe.wait_ge(sem(p + "exp"), 2 * u)
                        scores(u + 1).then_inc(sem(p + "score"), 1)
                    if 0 <= u - 1:
                        pe.wait_ge(sem(p + "pt"), u)
                        product(u - 1).then_inc(sem(p + "pv"), 1)
                        after(u - 1)
                    if 0 <= u < n:
                        pe.wait_ge(sem(p + "p"), u + 1)
                        if u >= 2:
                            pe.wait_ge(sem(p + "pt"), u - 1)
                        blocks(u).then_inc(sem(p + "tr"), 1)

            def mla():
                c = BASE["mla"]
                for m in range(4):
                    cc, s = c + m // 3, m % 3
                    arrived(pe, cc)
                    for k in range(KT):
                        if m == 0:
                            pe.wait_ge(h_ready, 8 * 4 + k + 1)
                        last = mm(psA[:, m, 0:S], chunk(cc, s * SLOT + k * P, s * SLOT + k * P + P),
                                  H[:, k, :], start=(k == 0), stop=(k == KT - 1))
                    if m == 2:
                        last.then_inc(chunk_used, 1)
                last.then_inc(sem("mla_lat"), 1)
                pe.wait_ge(sem("mla_sq"), 1)
                for k in range(2):
                    mm(psS[:, 0, 0:S], ones, ROT[:, k, :], start=(k == 0), stop=(k == 1))
                mm(psS[:, 1, 0:S], ones, ROT[:, 2, :], start=True, stop=True).then_inc(sem("mla_sum"), 1)
                pe.wait_ge(sem("mla_cqn"), 1)
                for m in range(12):
                    b = m % 4
                    if m % 4 == 0 and m:
                        pe.wait_ge(sem("mla_q"), m // 4)
                    for k in range(2):
                        j = 2 * m + k
                        cc, a = (c + 1, SLOT + j * P) if j < 16 else (c + 2, (j - 16) * P)
                        if j in (0, 16):
                            arrived(pe, cc)
                        last = mm(psA[:, b, 0:S], chunk(cc, a, a + P), CQN[:, k, :],
                                  start=(k == 0), stop=(k == 1))
                    if m == 7:
                        last.then_inc(chunk_used, 1)
                    if m == 11:
                        last.then_inc(sem("mla_qps"), 1)
                    if m in (3,):
                        last.then_inc(sem("mla_qps"), 1)
                    if m == 7:
                        pass
                arrived(pe, c + 3)
                pe.wait_ge(sem("mla_q"), 3)
                rot = chunk(c + 3, 2 * SLOT + 512, 2 * SLOT + 640)
                for m in range(4):
                    mm(psA[:, m // 2, (m % 2) * S:(m % 2 + 1) * S], rot, QR[:, m, :],
                       start=(m % 2 == 0), stop=True)
                mm(psG[:, 0, 0:S], rot, LAT[:, 3, :], start=True, stop=True)
                for t in range(TT):
                    last = nc.tensor.transpose(psG[:, 1, t * P:(t + 1) * P], CQN[:, 2, t * P:(t + 1) * P], ident)
                last.then_inc(sem("mla_rot"), 1)
                pe.wait_ge(sem("mla_ready"), 1)

                def prep(h):
                    if h >= 1:
                        pe.wait_ge(sem("mla_ql"), h)
                    a = SLOT + h * P
                    ins = mm(psS[:, 0, 0:S], chunk(c + 2, a, a + P), QN[:, h // 2, :], start=True, stop=True)
                    ins.then_inc(sem("mla_qlps"), 1)

                def scores(h):
                    pe.wait_ge(sem("mla_ql"), h + 1)
                    for t in range(TT):
                        mm(psA[:, h % 2, t * S:(t + 1) * S], QL[:, h % 2, t * P:(t + 1) * P],
                           CQN[:, 2, :], start=(t == 0), stop=False)
                        last = mm(psA[:, h % 2, t * S:(t + 1) * S], QR[:, h // 4, t * P:(t + 1) * P],
                                  KRM[:, h % 4, :], start=False, stop=True)
                    return last

                def blocks(h):
                    for kt in range(TT):
                        for t in range(TT):
                            last = nc.tensor.transpose(
                                psA[:, 2 + h % 2, kt * S + t * P:kt * S + (t + 1) * P],
                                PB[:, h % 2, t * S + kt * P:t * S + (kt + 1) * P], ident)
                    return last

                def product(h):
                    if h >= 2:
                        pe.wait_ge(sem("mla_ol"), h - 1)
                    for kt in range(TT):
                        last = mm(psG[:, h % 2, 0:S], KVTOK[:, kt, :], PTB[:, h % 2, kt * S:(kt + 1) * S],
                                  start=(kt == 0), stop=(kt == 1))
                    return last

                def up(h):
                    if h < 0:
                        return
                    pe.wait_ge(sem("mla_ol"), h + 1)
                    if h % 2 == 0 and h:
                        pe.wait_ge(sem("mla_o"), h // 2)
                    last = mm(psS[:, 1, 0:S], chunk(c + 3, h * P, h * P + P), OL[:, h % 2, :],
                              start=(h % 2 == 0), stop=(h % 2 == 1))
                    last.then_inc(sem("mla_up"), 1)

                attention(HEADS, "mla_", prep, scores, blocks, product, lambda h: up(h - 1))
                up(HEADS - 1)
                pe.wait_ge(sem("mla_up"), HEADS)
                pe.sem_inc(chunk_used, 2)
                pe.wait_ge(sem("mla_o"), HEADS // 2)
                for m in range(KT):
                    cc, s = c + 4 + m // 3, m % 3
                    arrived(pe, cc)
                    for k in range(KT):
                        last = mm(psA[:, m // 2, (m % 2) * S:(m % 2 + 1) * S],
                                  chunk(cc, s * SLOT + k * P, s * SLOT + k * P + P), MO[:, k, :],
                                  start=(m % 2 == 0 and k == 0), stop=(k == KT - 1))
                    if s == 2 or m == KT - 1:
                        last.then_inc(chunk_used, 1)

            def hybrid_in():
                c = BASE["hyb"]
                for m in range(40):
                    cc, s, j = c + m // 3, m % 3, m // 2
                    arrived(pe, cc)
                    if m % 2 == 0 and j >= 2:
                        pe.wait_ge(sem("u_out"), j - 1)
                    for k in range(KT):
                        if m == 0:
                            pe.wait_ge(h_ready, 8 * 6 + k + 1)
                        last = mm(psG[:, j % 2, (m % 2) * S:(m % 2 + 1) * S],
                                  chunk(cc, s * SLOT + k * P, s * SLOT + k * P + P), H[:, k, :],
                                  start=(m % 2 == 0 and k == 0), stop=(k == KT - 1))
                    if m % 2 == 1:
                        last.then_inc(sem("u_ps"), 1)
                    elif s == 2:
                        last.then_inc(chunk_used, 1)
                    if m % 2 == 1 and s == 2:
                        pe.wait_ge(sem("u_ps"), j + 1)
                        pe.sem_inc(chunk_used, 1)
                for t in range(TT):
                    for k in range(KT):
                        a = SLOT + k * 32
                        last = mm(psS[:, 0, t * 32:(t + 1) * 32], H[:, k, t * P:(t + 1) * P],
                                  chunk(c + 13, a, a + 32), start=(k == 0), stop=(k == KT - 1))
                last.then_inc(chunk_used, 1)

            def nsa():
                c = BASE["cmp"]
                pe.wait_ge(sem("blocks_ready"), 4)
                for y in range(2):
                    for m in range(2):
                        for l in range(16):
                            s = y * 4 + l // 4
                            cc, a = c + s // 3, (s % 3) * SLOT + (l % 4) * S + m * P
                            if m == 0 and l % 4 == 0:
                                arrived(pe, cc)
                            last = mm(psA[:, y * 2 + m, 0:2 * NCMP], chunk(cc, a, a + P),
                                      BL[y][:, l, :, :].rearrange("p g c -> p (g c)"),
                                      start=(l == 0), stop=(l == 15))
                last.then_inc(sem("cmp_hid"), 1)
                pe.wait_ge(sem("hid_ready"), 1)
                w2 = 2 * SLOT
                arrived(pe, c + 2)
                for g in range(2):
                    for k in range(2):
                        a = w2 + (k * 2 + g) * P
                        mm(psG[:, 0, g * NCMP:(g + 1) * NCMP], chunk(c + 2, a, a + P), HID[:, 0, k, g, :],
                           start=(k == 0), stop=(k == 1))
                for g in range(2):
                    for k in range(2):
                        a = w2 + (4 + k * 2 + g) * P
                        last = mm(psG[0:NCMP, 1, g * P:(g + 1) * P], HID[:, 1, k, g, :], chunk(c + 2, a, a + P),
                                  start=(k == 0), stop=(k == 1))
                last.then_inc(sem("cmp_out"), 1)
                arrived(pe, msk)
                half = mask(M_HALF)
                pe.wait_ge(sem("nsa_sq"), 1)
                for t in range(NSA_T):
                    mm(psA[:, t // 2, (t % 2) * S:(t % 2 + 1) * S], half, SQ[:, t, :],
                       start=(t % 2 == 0), stop=True)
                for y in range(2):
                    mm(psA[:, 2, y * S:(y + 1) * S], half, SQ[:, 4 + y, :],
                       start=(y == 0), stop=True)
                pe.wait_ge(sem("nsa_sqc"), 1)
                mm(psA[:, 3, 0:2 * NCMP], half, SQ[:, 6, 0:2 * NCMP], start=True,
                   stop=True).then_inc(sem("nsa_sum"), 1)
                for y in range(2):
                    for t in range(TT):
                        last = nc.tensor.transpose(psS[:, 1, (y * TT + t) * P:(y * TT + t + 1) * P],
                                                   UKV[:, 2 * y + 1, t * P:(t + 1) * P], ident)
                last.then_inc(sem("nsa_v"), 1)
                pe.wait_ge(sem("nsa_ready"), 1)
                pe.sem_inc(chunk_used, 3)

                def key(y, g):
                    return KGC[:, g, :] if y == 0 else KG[:, y - 1, g, :]

                def scores(u):
                    t, y, g = NSA_UNITS[u]
                    w = NCMP if y == 0 else S
                    for i in range(TT):
                        last = mm(psA[:, u % 2, i * S:i * S + w], UQ[:, t, i * P:(i + 1) * P], key(y, g),
                                  start=(i == 0), stop=True)
                    return last

                def blocks(u):
                    t, y, g = NSA_UNITS[u]
                    if y == 0:
                        for i in range(TT):
                            last = nc.tensor.transpose(psA[0:NCMP, 2 + u % 2, i * P:(i + 1) * P],
                                                       NPB[:, u % 2, i * S:i * S + NCMP], ident)
                        return last
                    for kt in range(TT):
                        for i in range(TT):
                            last = nc.tensor.transpose(
                                psA[:, 2 + u % 2, kt * S + i * P:kt * S + (i + 1) * P],
                                NPB[:, u % 2, i * S + kt * P:i * S + (kt + 1) * P], ident)
                    return last

                def product(u):
                    t, y, g = NSA_UNITS[u]
                    first, final = (y == 0 and g == 0), (y == 2 and g == 1)
                    if first and t >= 2:
                        pe.wait_ge(sem("nsa_o"), t - 1)
                    if y == 0:
                        return mm(psG[:, t % 2, 0:S], VGC[:, g, :], NPTB[0:NCMP, u % 2, 0:S],
                                  start=first, stop=False)
                    for kt in range(TT):
                        last = mm(psG[:, t % 2, 0:S], VG[:, y - 1, kt, g, :],
                                  NPTB[:, u % 2, kt * S:(kt + 1) * S], start=False, stop=(final and kt == 1))
                    return last

                attention(len(NSA_UNITS), "nsa_", lambda u: None, scores, blocks, product, lambda u: None)

            def gdn():
                pe.wait_ge(sem("gdn_sq"), 1)
                pe.wait_ge(sem("nsa_o"), NSA_T)
                for b in range(4):
                    last = mm(psA[:, b, :], ones, SQ[:, 2 * b:2 * b + 2, :].rearrange("p a s -> p (a s)"),
                              start=True, stop=True)
                last.then_inc(sem("gdn_sum"), 1)
                pe.wait_ge(sem("gdn_g"), 1)
                mm(psS[:, 0, 0:NU], mask(M_TRI), GG, start=True, stop=True).then_inc(sem("gdn_gc"), 1)
                pe.wait_ge(sem("gdn_gu"), 1)
                for b in range(2):
                    last = mm(psG[:, b, :], ones, DEC[:, 4 * b:4 * b + 4, :].rearrange("p u s -> p (u s)"),
                              start=True, stop=True)
                last.then_inc(sem("gdn_row"), 1)
                pe.wait_ge(sem("gdn_qk"), 1)
                for u in range(NU):
                    h, n = divmod(u, 2)
                    nc.tensor.transpose(psA[:, u // 4, (u % 4) * P:(u % 4 + 1) * P],
                                        KTT[:, h, n * P:(n + 1) * P], ident)
                for u in range(NU):
                    h, n = divmod(u, 2)
                    last = nc.tensor.transpose(psA[:, 2 + u // 4, (u % 4) * P:(u % 4 + 1) * P],
                                               VT[:, h, n * P:(n + 1) * P], ident)
                last.then_inc(sem("gdn_kv"), 1)
                pe.wait_ge(sem("gdn_kvtok"), 1)
                for u in range(NU):
                    h, n = divmod(u, 2)
                    k = KTT[:, h, n * P:(n + 1) * P]
                    mm(psA[:, u // 4, (u % 4) * P:(u % 4 + 1) * P], k, k, start=(u % 4 == 0),
                       stop=True)
                    last = mm(psA[:, 2 + u // 4, (u % 4) * P:(u % 4 + 1) * P], QT[:, h, n * P:(n + 1) * P], k,
                              start=(u % 4 == 0), stop=True)
                last.then_inc(sem("gdn_gram"), 1)
                pe.wait_ge(sem("gdn_l"), 1)
                for u in range(NU):
                    nc.tensor.transpose(psA[:, u // 4, (u % 4) * P:(u % 4 + 1) * P], L_[:, u, :], ident)
                    last = nc.tensor.transpose(psA[:, 2 + u // 4, (u % 4) * P:(u % 4 + 1) * P],
                                               AT_[:, u, :], ident)
                last.then_inc(sem("gdn_lt"), 1)

                def each(ps, b0, lhs, rhs):
                    for u in range(NU):
                        last = mm(ps[:, b0 + u // 4, (u % 4) * P:(u % 4 + 1) * P], lhs[:, u, :], rhs[:, u, :],
                                  start=(u % 4 == 0), stop=True)
                    return last

                pe.wait_ge(sem("gdn_att"), 1)
                for lev in range(1, 7):
                    pe.wait_ge(sem("gdn_x"), lev + 1)
                    pe.wait_ge(sem("gdn_t"), lev)
                    each(psA, 0, XMT, TM)
                    each(psA, 2, XM, TMT).then_inc(sem("gdn_p1"), 1)
                    pe.wait_ge(sem("gdn_p1out"), lev)
                    each(psG, 0, TMT, P1)
                    each(psS, 0, TM, Q1).then_inc(sem("gdn_r"), 1)
                pe.wait_ge(sem("gdn_t"), 7)
                each(psA, 0, KBG, TMT)
                each(psA, 2, TMT, VB).then_inc(sem("gdn_wu"), 1)
                pe.wait_ge(sem("gdn_wuout"), 1)
                for h in range(GH):
                    mm(psG[:, 0, h * P:(h + 1) * P], KDEC[:, 2 * h, :], UU[:, 2 * h, :],
                       start=(h == 0), stop=True)
                    last = mm(psS[:, 0, h * P:(h + 1) * P], UU[:, 2 * h, :], ATT[:, 2 * h, :],
                              start=(h == 0), stop=True)
                last.then_inc(sem("gdn_s1"), 1)
                pe.wait_ge(sem("gdn_state"), 1)
                for h in range(GH):
                    last = mm(psG[:, 1, h * P:(h + 1) * P], WT[:, 2 * h + 1, :], SST[:, h, :],
                              start=(h == 0), stop=True)
                last.then_inc(sem("gdn_ws"), 1)
                pe.wait_ge(sem("gdn_vnew"), 1)
                for h in range(GH):
                    mm(psS[:, 1, h * P:(h + 1) * P], SST[:, h, :], ER[:, 2 * h + 1, :],
                       start=(h == 0), stop=False)
                    last = mm(psS[:, 1, h * P:(h + 1) * P], VNEW[:, h, :], ATT[:, 2 * h + 1, :],
                              start=False, stop=True)
                last.then_inc(sem("gdn_o1"), 1)
                pe.wait_ge(sem("gdn_osq"), 1)
                for b in range(2):
                    last = mm(psA[:, b, :], ones, blk(0)[:, b * 512:(b + 1) * 512], start=True, stop=True)
                last.then_inc(chunk_used, 1)

            def merge():
                c = BASE["mrg"]
                pe.wait_ge(sem("yg_ready"), 1)
                branch = [YA, YN, YG]
                for j in range(24):
                    m, r = divmod(j, 3)
                    cc, s = c + j // 2, j % 2
                    arrived(pe, cc)
                    if j >= 2:
                        pe.wait_ge(sem("mrg_out"), j - 1)
                    for k in range(KT):
                        mm(psG[:, j % 2, 0:S], chunk(cc, s * SLOT + k * P, s * SLOT + k * P + P), H[:, k, :],
                           start=(k == 0), stop=(k == KT - 1))
                    for k in range(4):
                        a = 2 * SLOT + (s * 4 + k) * P
                        last = mm(psG[:, j % 2, S:2 * S], chunk(cc, a, a + P), branch[r][:, k, :],
                                  start=False, stop=(k == 3))
                    last.then_inc(sem("mrg_ps"), 1)
                    if s == 1:
                        pe.wait_ge(sem("mrg_ps"), j + 1)
                        pe.sem_inc(chunk_used, 1)
                c = BASE["out"]
                for m in range(KT):
                    cc, s = c + m // 3, m % 3
                    arrived(pe, cc)
                    for k in range(KT):
                        if m == 0 and k == 0:
                            pe.wait_ge(sem("merged"), KT)
                        last = mm(psA[:, m // 2, (m % 2) * S:(m % 2 + 1) * S],
                                  chunk(cc, s * SLOT + k * P, s * SLOT + k * P + P), Y[:, k, :],
                                  start=(m % 2 == 0 and k == 0), stop=(k == KT - 1))
                    if s == 2:
                        last.then_inc(chunk_used, 1)
                last.then_inc(sem("hyb_acc"), 1)

            def router():
                c = BASE["out"] + 2
                for t in range(TT):
                    for k in range(KT):
                        pe.wait_ge(h_ready, 8 * 7 + k + 1)
                        a = 2 * SLOT + k * 36
                        last = mm(psS[:, 1, t * 36:(t + 1) * 36], H[:, k, t * P:(t + 1) * P],
                                  chunk(c, a, a + 36), start=(k == 0), stop=(k == KT - 1))
                last.then_inc(chunk_used, 1)
                for t in range(TT):
                    for k in range(KT):
                        last = nc.tensor.transpose(psA[:, 2 * t + k // 4, (k % 4) * P:(k % 4 + 1) * P],
                                                   H[:, k, t * P:(t + 1) * P], ident)
                last.then_inc(sem("rt_htok"), 1)
                pe.wait_ge(sem("rt_asg"), 1)
                mm(psS[:, 0, 0:E], before, ASG[:, 0, :], start=True, stop=True)
                mm(psS[:, 0, E:2 * E], before, ASG[:, 1, :], start=False, stop=False)
                mm(psS[:, 0, E:2 * E], ones, ASG[:, 0, :], start=False, stop=True).then_inc(sem("rt_cnt"), 1)
                pe.wait_ge(sem("rt_max1"), 1)
                nc.tensor.transpose(psS[0:1, 0, 256:256 + P], blk(22)[:, 128:129], ident).then_inc(sem("rt_max1t"), 1)

            def half(c, g, a=0, n=512):
                a += (g % 6) * 512
                return chunk(c + g // 6, a, a + n)

            def sparse():
                c0 = BASE["moe"]

                def gather(r, p):
                    if p == 0 and isinstance(r, int):
                        pe.wait_ge(sem("sp_sel"), 1)
                        pe.wait_ge(sem("sp_gt"), NP // 2)
                    for b in range(2):
                        for k in range(4 * b, 4 * b + 4):
                            for t in range(TT):
                                off = t * E * CAP + p * P
                                src = SEL[:, off:off + P] if isinstance(r, int) else \
                                    SEL[:, bass.ds(r * (3 * P) + off, P)]
                                last = mm(psG[:, b, (k % 4) * P:(k % 4 + 1) * P], HTOK[:, t, k * P:(k + 1) * P],
                                          src, start=(k % 4 == 0 and t == 0), stop=(t == 1))
                        last.then_inc(sem("sp_ga"), 1)

                def gate_up(r, p):
                    pe.wait_ge(sem("sp_xe"), r * 6 + 2 * (p + 1))
                    c = c0 + 8 * p
                    for u in range(2):
                        for k in range(KT):
                            for e in range(2):
                                g = (u * KT + k) * 2 + e
                                if g % 6 == 0:
                                    arrived(pe, c + g // 6, r * 24)
                                last = mm(psS[64 * e:64 * e + 64, u, :], XE[:, k, e * CAP:(e + 1) * CAP],
                                          half(c, g), start=(k == 0), stop=(k == KT - 1))
                                if g % 6 == 5:
                                    last.then_inc(chunk_used, 1)
                    last.then_inc(sem("sp_gu"), 1)

                def turn(r, p):
                    pe.wait_ge(sem("sp_act"), r * 3 + (p + 1))
                    for f in range(FE):
                        last = nc.tensor.transpose(psS[:, 0, f * P:(f + 1) * P], HACT[:, f * P:(f + 1) * P], ident)
                    last.then_inc(sem("sp_ht"), 1)

                def down(r, p):
                    pe.wait_ge(sem("sp_htout"), r * 3 + (p + 1))
                    c = c0 + 8 * p
                    for h in range(2):
                        if p < NP - 1 or not isinstance(r, int):
                            pe.wait_ge(sem("sp_xe"), r * 6 + (2 * (p + 1) + h + 1))
                        for f in range(FE):
                            for e in range(2):
                                g = 2 * 2 * KT + (h * FE + f) * 2 + e
                                if g % 6 == 0:
                                    arrived(pe, c + g // 6, r * 24)
                                last = mm(psG[64 * e:64 * e + 64, h, :], HT[:, f, e * CAP:(e + 1) * CAP],
                                          half(c, g), start=(f == 0), stop=(f == FE - 1))
                                if g % 6 == 5:
                                    last.then_inc(chunk_used, 1)
                        if h == 0:
                            last.then_inc(sem("sp_dn"), 1)

                def scatter(r, p, final=False):
                    pe.wait_ge(sem("sp_ys"), r * 6 + 2 * (p + 1))
                    for m in range(KT):
                        src = SELGT[:, p * S:(p + 1) * S] if isinstance(r, int) else \
                            SELGT[:, bass.ds(r * (3 * S) + p * S, S)]
                        last = mm(psA[:, m // 2, (m % 2) * S:(m % 2 + 1) * S], YS[:, m * P:(m + 1) * P], src,
                                  start=(isinstance(r, int) and p == 0 and m % 2 == 0), stop=final)
                    return last

                def step(r, p):
                    gate_up(r, p)
                    if p or not isinstance(r, int):
                        scatter(r, p - 1)
                    turn(r, p)
                    if not isinstance(r, int) or p < NP - 1:
                        gather(r, p + 1)
                    down(r, p)

                pe.wait_ge(sem("sp_selg"), 1)
                pe.wait_ge(sem("htok_out"), 1)
                for p in range(NP):
                    b = p // 2
                    if p % 2 == 0 and b >= 2:
                        pe.wait_ge(sem("sp_gt"), b - 1)
                    for t in range(TT):
                        last = nc.tensor.transpose(psG[:, b % 2, ((p % 2) * 2 + t) * P:((p % 2) * 2 + t + 1) * P],
                                                   SELG[:, t * E * CAP + p * P:t * E * CAP + (p + 1) * P], ident)
                    if p % 2 == 1:
                        last.then_inc(sem("sp_gtps"), 1)
                gather(0, 0)
                step(0, 0)
                step(0, 1)
                with pe.Fori(0, 4) as r:
                    for j in range(3):
                        step(r, 2 + j)
                for p in range(14, NP):
                    step(0, p)
                scatter(0, NP - 1, final=True).then_inc(sem("moe_acc"), 1)

            def dense():
                c0, t0 = BASE["moe"], 4 * NF
                for t in range(TT):
                    last = nc.tensor.transpose(psS[0:E, 1, t * P:(t + 1) * P], blk(24)[:, t * E:(t + 1) * E], ident)
                last.then_inc(sem("dn_tr"), 1)
                pe.wait_ge(sem("dn_gt"), 1)
                for j in range(NP):
                    if j >= 2:
                        pe.wait_ge(sem("dn_bc"), j - 1)
                    for i in range(2):
                        e = 2 * j + i
                        last = mm(psG[:, j % 2, i * S:(i + 1) * S], ident[0:E, e:e + 1].to_broadcast([E, P]),
                                  blk(25)[0:E, 0:S], start=(i == 0), stop=True)
                    last.then_inc(sem("dn_ps"), 1)
                pe.wait_ge(sem("dn_bc"), NP)
                pe.wait_ge(sem("htok_out"), 1)

                def step(r, p):
                    c, n = c0 + 8 * p, t0 + 8 * p
                    for i in range(RING):
                        arrived(pe, c + i, r * 24)
                    for j in range(8):
                        e, f = divmod(j, FE)
                        pe.wait_ge(sem("act_ready"), r * 24 + (n + j - 1))
                        for u in range(2):
                            for k in range(KT):
                                last = mm(psG[:, j % 2, u * S:(u + 1) * S],
                                          half(c, (u * KT + k) * 2 + e, f * P, P), H[:, k, :],
                                          start=(u == 0 and k == 0), stop=(k == KT - 1))
                        last.then_inc(sem("gu_ready"), 1)
                    pe.wait_ge(sem("act_ready"), r * 24 + (n + 8))
                    pe.sem_inc(chunk_used, 5)
                    for h in range(2):
                        for f in range(FE):
                            for e in range(2):
                                g = 2 * 2 * KT + (h * FE + f) * 2 + e
                                if g % 6 == 0:
                                    arrived(pe, c + g // 6, r * 24)
                                for m in range(4 * h, 4 * h + 4):
                                    first = isinstance(r, int) and p == 0 and e == f == 0 and m % 2 == 0
                                    last = mm(psA[:, m // 2, (m % 2) * S:(m % 2 + 1) * S],
                                              half(c, g, (m % 4) * P, P), HD[:, e * FE + f, :],
                                              start=first, stop=(e == 1 and f == FE - 1))
                                if g % 6 == 5:
                                    last.then_inc(chunk_used, 1)

                step(0, 0)
                with pe.Fori(0, 5) as r:
                    for j in range(3):
                        step(r, 1 + j)
                pe.wait_ge(chunk_used, NCHUNK)
                pe.sem_inc(sem("moe_acc"), 1)

            for t in range(ADA[0]):
                ada(0, t)
            pre_norm(0)
            ffn(BASE["ffn0"], 0, NF, 0, ADA[1], 6)
            post_norm(0)
            pre_norm(1)
            pool()
            post_norm(1)
            pre_norm(2)
            ffn(BASE["ffn1"], NF, NF, 2, ADA[2], 24)
            post_norm(2)
            pre_norm(3)
            ffn(BASE["ffn2"], 2 * NF, NF, 3, ADA[3], 42)
            post_norm(3)
            pre_norm(4)
            mla()
            post_norm(4)
            pre_norm(5)
            ffn(BASE["ffn3"], 3 * NF, NF, 5)
            post_norm(5)
            pre_norm(6)
            hybrid_in()
            nsa()
            gdn()
            merge()
            pre_norm(7)
            router()
            pe.wait_ge(sem("rt_flag"), 1)
            n = pe.value_load(most[0:1, 0:1], min_val=0, max_val=S)
            with pe.If(n <= CAP):
                sparse()
            with pe.Else():
                dense()
            pe.wait_ge(sem("moe_acc"), 1)

        @block.scalar
        def _(ac):
            A = nc.scalar.activation
            ch = Chain(ac, "act_step")

            def root(dst, ps, scale):
                A(dst, ps, ACT.Sqrt, bias=eps[:, 0:1], scale=scale).then_inc(sem("root_ready"), 1)

            def pre_norm(n):
                ac.wait_ge(x_ready, n + 1)
                A(SQ[:, 0:4, :], X[:, 0:4, :], ACT.Square).then_inc(sem("pre_sq_act"), 1)
                ac.wait_ge(sem("pre_sum"), n + 1)
                root(rstd[:, :], psS[:, 0, 0:S], 1.0 / D)

            def post_norm(n):
                for b in range(4):
                    ac.wait_ge(sem("y_ready"), 4 * n + b + 1)
                    A(SQ[:, 2 * b:2 * b + 2, :], Y[:, 2 * b:2 * b + 2, :], ACT.Square).then_inc(sem("post_sq"), 1)
                ac.wait_ge(sem("post_sum"), n + 1)
                root(rstd[:, :], psS[:, 0, 0:S], 1.0 / D)

            def ffn(t0, nf):
                def one(i, t):
                    ac.wait_ge(sem("gu_ready"), i + (t + 1))
                    if t >= 2:
                        ac.wait_ge(sem("act_ready"), i + (t - 1))
                    A(sg[:, t % 2, :], psG[:, t % 2, 0:S], ACT.Silu).then_inc(sem("silu_ready"), 1)
                one(0, t0)
                one(0, t0 + 1)
                with ac.Fori(0, nf - 2, 2) as i:
                    one(i, t0 + 2)
                    one(i, t0 + 3)

            def attention(n, p, src, dst, width, copy, extra):
                for u in range(-1, n + 1):
                    if u + 1 < n:
                        v = u + 1
                        ac.wait_ge(sem(p + "max"), v + 1)
                        if v >= 2:
                            ac.wait_ge(sem(p + "tr"), v - 1)
                        for t in range(TT):
                            w = width(v)
                            A(dst(v)[:, t * S:t * S + w], src(v)[:, t * S:t * S + w], ACT.Exp,
                              bias=NMAX[:, v % 2, t:t + 1],
                              accum_out=SUM[:, v % 2, t:t + 1]).then_inc(sem(p + "exp"), 1)
                    if 0 <= u < n:
                        ac.wait_ge(sem(p + "tr"), u + 1)
                        if u >= 2:
                            ac.wait_ge(sem(p + "pv"), u - 1)
                        copy(u).then_inc(sem(p + "pt"), 1)
                    extra(u)

            def mla():
                ac.wait_ge(sem("mla_lat"), 1)
                for m in range(4):
                    A(LAT[:, m, :], psA[:, m, 0:S], ACT.Copy)
                for m in range(3):
                    last = A(ROT[:, m, :], psA[:, m, 0:S], ACT.Square)
                last.then_inc(sem("mla_sq"), 1)
                ac.wait_ge(sem("mla_sum"), 1)
                root(rstd[:, :], psS[:, 0, 0:S], 1.0 / 256)
                root(CQN[:, 3, :], psS[:, 1, 0:S], 1.0 / 128)
                for g in range(3):
                    if g < 2:
                        ac.wait_ge(sem("mla_qps"), 1) if g == 0 else ac.wait_ge(chunk_used, BASE["mla"] + 2)
                    else:
                        ac.wait_ge(sem("mla_qps"), 2)
                    for b in range(4):
                        if g < 2:
                            last = A(QN[:, 4 * g + b, :], psA[:, b, 0:S], ACT.Copy)
                        else:
                            last = A(QR[:, b, :], psA[:, b, 0:S], ACT.Copy)
                    last.then_inc(sem("mla_q"), 1)

                def extra(u):
                    if u + 2 < HEADS:
                        query(u + 2)
                    if u >= 1:
                        h = u - 1
                        ac.wait_ge(sem("mla_pv"), h + 1)
                        if h >= 2:
                            ac.wait_ge(sem("mla_up"), h - 1)
                        A(OL[:, h % 2, :], psG[:, h % 2, 0:S], ACT.Copy).then_inc(sem("mla_ol"), 1)

                def query(h):
                    ac.wait_ge(sem("mla_qlps"), h + 1)
                    if h >= 2:
                        ac.wait_ge(sem("mla_score"), h - 1)
                    A(QL[:, h % 2, :], psS[:, 0, 0:S], ACT.Copy, scale=MLA_SCALE).then_inc(sem("mla_ql"), 1)

                query(0)
                attention(HEADS, "mla_", lambda u: psA[:, u % 2, :], lambda u: PB[:, u % 2, :], lambda u: S,
                          lambda u: A(PTB[:, u % 2, :], psA[:, 2 + u % 2, :], ACT.Copy), extra)

            def hybrid_in():
                dst = [UA[:, 2 * j:2 * j + 2] for j in range(6)] + [UQ[:, 0:2], UQ[:, 2:4]]
                dst += [UK[:, 0:2], UK[:, 2:4], UKV[:, 0:2], UKV[:, 2:4]]
                dst += [UG[:, 2 * j:2 * j + 2] for j in range(6)] + [UZ[:, 0:2], UZ[:, 2:4]]
                for j in range(20):
                    ac.wait_ge(sem("u_ps"), j + 1)
                    src = psG[:, j % 2, :].rearrange("p (a s) -> p a s", a=2)
                    if j in (8, 9):
                        A(dst[j][0:64], src[0:64], ACT.Copy)
                        A(dst[j][64:P, :, 0:S - 1], src[64:P, :, 1:S], ACT.Copy).then_inc(sem("u_out"), 1)
                    else:
                        A(dst[j], src, ACT.Silu if j >= 18 else ACT.Copy).then_inc(sem("u_out"), 1)
                ac.wait_ge(chunk_used, BASE["hyb"] + 14)
                ch.link(A(GT, psS[:, 0, 0:64].rearrange("p (t c) -> p t c", t=2), ACT.Copy), "gt_out")
                A(GATE, GT[:, :, 0:24], ACT.Sigmoid).then_inc(sem("gate_sig"), 1)
                beta = BETA.rearrange("p (t h) -> p t h", t=2)
                A(beta, GT[:, :, 24:28], ACT.Sigmoid).then_inc(sem("beta_ready"), 1)

            def nsa():
                A(SQ[:, 0:4, :], UQ, ACT.Square)
                ch.link(A(SQ[:, 4:6, :], UKV[:, 0:3:2, :], ACT.Square), "nsa_sq")
                ac.wait_ge(sem("cmp_hid"), 1)
                A(HID.rearrange("p y m g c -> p (y m) (g c)"), psA[:, :, 0:2 * NCMP],
                  ACT.Gelu_apprx_tanh).then_inc(sem("hid_ready"), 1)
                ac.wait_ge(sem("cmp_out"), 1)
                A(SQ[:, 6, 0:2 * NCMP], psG[:, 0, 0:2 * NCMP], ACT.Square).then_inc(sem("nsa_sqc"), 1)

                ac.wait_ge(sem("nsa_sum"), 1)
                root(SQ[:, 0:6, :].rearrange("p (b a) s -> p b (a s)", a=2), psA[:, 0:3, :], 1.0 / 64)
                root(SQ[:, 6, 0:2 * NCMP], psA[:, 3, 0:2 * NCMP], 1.0 / 64)

                def copy(u):
                    if NSA_UNITS[u][1] == 0:
                        return A(NPTB[0:NCMP, u % 2, 0:S], psA[0:NCMP, 2 + u % 2, 0:S], ACT.Copy)
                    return A(NPTB[:, u % 2, :], psA[:, 2 + u % 2, :], ACT.Copy)

                def extra(u):
                    if u >= 1 and u % 6 == 0:
                        ac.wait_ge(sem("nsa_pv"), u)
                        t = u // 6 - 1
                        A(YN[:, t, :], psG[:, t % 2, 0:S], ACT.Copy).then_inc(sem("nsa_o"), 1)

                attention(len(NSA_UNITS), "nsa_", lambda u: NPB[:, u % 2, :], lambda u: NPB[:, u % 2, :],
                          lambda u: NCMP if NSA_UNITS[u][1] == 0 else S, copy, extra)

            def gdn():
                ac.wait_ge(sem("gdn_z"), 1)
                A(AL, col("a_log", 0, 4), ACT.Exp)
                ch.link(A(EGC, GX, ACT.Abs))
                ch.link(A(EGC, EGC, ACT.Exp, scale=-1.0))
                A(EGC, EGC, ACT.Ln, bias=ones[:, 0:1]).then_inc(sem("gdn_ln"), 1)
                ac.wait_ge(sem("gdn_conv"), 1)
                ch.link(A(blk(16, 3), blk(16, 3), ACT.Silu), "gdn_cv")
                A(blk(2, 2), blk(16, 2), ACT.Square).then_inc(sem("gdn_sq"), 1)
                ac.wait_ge(sem("gdn_sum"), 1)
                root(blk(2, 2).rearrange("p (b n) -> p b n", b=4), psA[:, :, :], 1.0)
                ac.wait_ge(sem("gdn_diff"), 1)
                A(ER.rearrange("p u s -> p (u s)").rearrange("p (b n) -> p b n", b=2), psG[:, :, :],
                  ACT.Exp).then_inc(sem("gdn_er"), 1)
                A(blk(22), blk(22), ACT.Exp, scale=-1.0)
                A(EGC, GC, ACT.Exp)
                A(KD, GX, ACT.Exp).then_inc(sem("gdn_exps"), 1)
                ac.wait_ge(sem("gdn_lt"), 1)
                A(blk(25).rearrange("p (b n) -> p b n", b=2), psA[:, 0:2, :], ACT.Copy).then_inc(sem("gdn_ltout"), 1)
                A(blk(6).rearrange("p (b n) -> p b n", b=2), psA[:, 2:4, :], ACT.Copy).then_inc(sem("gdn_att"), 1)
                for lev in range(1, 7):
                    ac.wait_ge(sem("gdn_p1"), lev)
                    A(blk(11).rearrange("p (b n) -> p b n", b=2), psA[:, 0:2, :], ACT.Copy)
                    A(blk(12).rearrange("p (b n) -> p b n", b=2), psA[:, 2:4, :], ACT.Copy)\
                        .then_inc(sem("gdn_p1out"), 1)
                ac.wait_ge(sem("gdn_wu"), 1)
                A(blk(0).rearrange("p (b n) -> p b n", b=2), psA[:, 0:2, :], ACT.Copy)
                A(blk(1).rearrange("p (b n) -> p b n", b=2), psA[:, 2:4, :], ACT.Copy).then_inc(sem("gdn_wuout"), 1)
                ac.wait_ge(sem("gdn_o1"), 1)
                A(OT[:, :, 0, :], psS[:, 0, :].rearrange("p (h s) -> p h s", h=GH), ACT.Copy)
                ch.link(A(OT[:, :, 1, :], psS[:, 1, :].rearrange("p (h s) -> p h s", h=GH), ACT.Copy))
                A(blk(0), blk(3), ACT.Square).then_inc(sem("gdn_osq"), 1)
                ac.wait_ge(chunk_used, msk + 1)
                root(blk(0).rearrange("p (b n) -> p b n", b=2), psA[:, 0:2, :], 1.0 / P)

            def merge():
                for j in range(24):
                    m, r = divmod(j, 3)
                    ac.wait_ge(sem("mrg_ps"), j + 1)
                    if j >= 2:
                        ac.wait_ge(sem("mrg_out"), j - 1)
                    A(sg[:, j % 2, :], psG[:, j % 2, 0:S], ACT.Sigmoid,
                      bias=col("b_gate", 8 * r + m)).then_inc(sem("mrg_sig"), 1)

            def router():
                ac.wait_ge(sem("rt_htok"), 1)
                A(HTOK.rearrange("p t (b n) -> p (t b) n", b=2), psA[:, :, :], ACT.Copy).then_inc(sem("htok_out"), 1)
                ac.wait_ge(sem("rt_max"), 1)
                A(blk(24)[:, 256:264], blk(24)[:, 256:264], ACT.Exp)
                A(blk(24)[:, 128:192], blk(24)[:, 128:192], ACT.Exp).then_inc(sem("rt_exp"), 1)

            def sparse():
                for b in range(NP // 2):
                    ac.wait_ge(sem("sp_gtps"), b + 1)
                    A(SELGT[:, b * 512:(b + 1) * 512], psG[:, b % 2, :], ACT.Copy).then_inc(sem("sp_gt"), 1)
                with ac.Fori(0, NP) as p:
                    ac.wait_ge(sem("sp_gu"), p + 1)
                    A(HSIL, psS[:, 0, :], ACT.Silu).then_inc(sem("sp_si"), 1)
                    ac.wait_ge(sem("sp_ht"), p + 1)
                    A(HT.rearrange("p f s -> p (f s)"), psS[:, 0, :], ACT.Copy).then_inc(sem("sp_htout"), 1)

            def dense():
                for j in range(NP):
                    ac.wait_ge(sem("dn_ps"), j + 1)
                    A(GB[:, j * 512:(j + 1) * 512], psG[:, j % 2, :], ACT.Copy).then_inc(sem("dn_bc"), 1)
                ffn(4 * NF, E * FE)

            ac.wait_ge(sem("cols_in"), 16)
            A(silc[:, :], col("c", 0, 8), ACT.Silu).then_inc(sem("silc_ready"), 1)
            pre_norm(0)
            ffn(0, NF)
            post_norm(0)
            pre_norm(1)
            post_norm(1)
            pre_norm(2)
            ffn(NF, NF)
            post_norm(2)
            pre_norm(3)
            ffn(2 * NF, NF)
            post_norm(3)
            pre_norm(4)
            mla()
            post_norm(4)
            pre_norm(5)
            ffn(3 * NF, NF)
            post_norm(5)
            pre_norm(6)
            hybrid_in()
            nsa()
            gdn()
            merge()
            pre_norm(7)
            router()
            ac.wait_ge(sem("rt_flag"), 1)
            n = ac.value_load(most[0:1, 0:1], min_val=0, max_val=S)
            with ac.If(n <= CAP):
                sparse()
            with ac.Else():
                dense()
            ac.wait_ge(sem("moe_acc"), 1)

        @block.vector
        def _(ve):
            V = nc.vector
            ch = Chain(ve, "dve_step")
            link = ch.link

            def ada(n, c, t, i=0, used=None):
                arrived(ve, c, i if isinstance(i, int) else i * 2)
                if used is not None:
                    ve.wait_ge(chunk_used, (i if isinstance(i, int) else i * 2) + used)
                out = ADP[:, (n + t) % 2]
                w = chunk(c).rearrange("p (m k n) -> p m k n", m=3, k=KT)
                V.tensor_scalar(out, w[:, :, 0, :], silc[:, 0:1], None, ALU.mult).then_inc(sem("ada_step"), 1)
                for k in range(1, KT):
                    ve.wait_ge(sem("ada_step"), i * (KT - 1) + ((n + t) * (KT - 1) + k))
                    V.scalar_tensor_tensor(out, w[:, :, k, :], silc[:, k:k + 1], out, ALU.mult, ALU.add)\
                        .then_inc(sem("ada_step" if k < KT - 1 else "ada_prod"), 1)

            def mod_out(layer, a, n):
                link(V.tensor_tensor(mod[:, layer, a:a + n], psS[:, 1, 0:n],
                                     col("ada_b", 72 * layer + a, n), ALU.add))
                for s in range(3):
                    for q, out in ((1, modA), (2, modC)):
                        end = 24 * s + 8 * q + 8
                        if a < end <= a + n:
                            link(V.scalar_tensor_tensor(out[:, layer, s, :], mod[:, layer, end - 8:end], 1.0,
                                                        col("norm_g", 48 * layer + 16 * s + 8 * (q - 1), 8),
                                                        ALU.add, ALU.mult))
                            if q == 2 and s != 1:
                                link(V.tensor_scalar(out[:, layer, s, :], out[:, layer, s, :], 0.5, None, ALU.mult))

            roots = Chain(ve, "root_used")

            def root(dst):
                n = roots.n.get("root_used", 0) + 1
                ve.wait_ge(sem("root_ready"), n)
                roots.link(V.reciprocal(dst, dst))

            def pre_norm(n):
                V.tensor_tensor(SQ[:, 4:8, :], X[:, 4:8, :], X[:, 4:8, :], ALU.mult).then_inc(sem("pre_sq_dve"), 1)
                root(rstd[:, :])
                scale, shift = pre_cols(n)
                for b in range(2):
                    link(V.tensor_tensor(H[:, 4 * b:4 * b + 4, :], X[:, 4 * b:4 * b + 4, :],
                                         rstd[:, None, :].to_broadcast([P, 4, S]), ALU.mult))
                    for k in range(4 * b, 4 * b + 4):
                        if shift is None:
                            ins = V.tensor_scalar(H[:, k, :], H[:, k, :], scale(k), None, ALU.mult)
                        else:
                            ins = V.tensor_scalar(H[:, k, :], H[:, k, :], scale(k), shift(k), ALU.mult, ALU.add)
                        ins.then_inc(h_ready, 1)

            def post_norm(n, done, layer, s, from_acc=True):
                if from_acc:
                    ve.wait_ge(chunk_used, done)
                    for b in range(4):
                        V.tensor_copy(Y[:, 2 * b:2 * b + 2, :], psA[:, b, :].rearrange("p (a s) -> p a s", a=2))\
                            .then_inc(sem("y_ready"), 1)
                root(rstd[:, :])
                for k in range(KT):
                    last = V.scalar_tensor_tensor(Y[:, k, :], Y[:, k, :], modC[:, layer, s, k:k + 1], rstd[:, :],
                                                  ALU.mult, ALU.mult)
                link(last)
                link(V.tensor_tensor(X[:, :, :], X[:, :, :], Y, ALU.add), "x_ready")

            def ffn(c0, t0, nf, na=0, n=0):
                def one(i, t):
                    ve.wait_ge(sem("silu_ready"), i + (t + 1))
                    V.tensor_tensor(act[:, t % 2, :], sg[:, t % 2, :], psG[:, t % 2, S:2 * S],
                                    ALU.mult).then_inc(sem("act_ready"), 1)
                if na:
                    one(0, t0)
                    with ve.Fori(0, na, RING) as i:
                        for j in range(RING):
                            one(i, t0 + 1 + j)
                            ada(n, c0 + 2 + 2 * j, j, i, c0 + 2 * j - 1)
                    one(0, t0 + na + 1)
                    na += 2
                with ve.Fori(na, nf, 2) as i:
                    one(i, t0)
                    one(i, t0 + 1)

            def sparse():
                iot = iota[:, None, :].to_broadcast([P, E, CAP])
                for t in range(TT):
                    sel = SEL[:, t * E * CAP:(t + 1) * E * CAP].rearrange("p (e s) -> p e s", s=CAP)
                    last = V.tensor_tensor(sel, iot, POS[:, t, :, None].to_broadcast([P, E, CAP]), ALU.is_equal)
                link(last, "sp_sel")
                for t in range(TT):
                    sel = SEL[:, t * E * CAP:(t + 1) * E * CAP].rearrange("p (e s) -> p e s", s=CAP)
                    selg = SELG[:, t * E * CAP:(t + 1) * E * CAP].rearrange("p (e s) -> p e s", s=CAP)
                    gate = blk(24)[:, t * E:(t + 1) * E][:, :, None].to_broadcast([P, E, CAP])
                    last = V.tensor_tensor(selg, sel, gate, ALU.mult)
                link(last, "sp_selg")

                def hidden(p):
                    ve.wait_ge(sem("sp_si"), p + 1)
                    V.tensor_tensor(HACT, HSIL, psS[:, 1, :], ALU.mult).then_inc(sem("sp_act"), 1)

                def xe(p):
                    for b in range(2):
                        ve.wait_ge(sem("sp_ga"), p * 2 + (b + 1))
                        V.tensor_copy(XE[:, 4 * b:4 * b + 4, :].rearrange("p k s -> p (k s)"), psG[:, b, :])\
                            .then_inc(sem("sp_xe"), 1)

                def ys(p):
                    ve.wait_ge(sem("sp_dn"), p + 1)
                    V.tensor_copy(YS[:, 0:512], psG[:, 0, :]).then_inc(sem("sp_ys"), 1)
                    ve.wait_ge(chunk_used, p * 8 + (BASE["moe"] + 8))
                    V.tensor_copy(YS[:, 512:1024], psG[:, 1, :]).then_inc(sem("sp_ys"), 1)

                xe(0)
                with ve.Fori(0, NP - 1) as p:
                    hidden(p)
                    xe(p + 1)
                    ys(p)
                hidden(NP - 1)
                ys(NP - 1)

            def dense():
                ve.wait_ge(sem("dn_tr"), 1)
                V.tensor_copy(blk(25)[0:E, 0:S], psS[0:E, 1, 0:S]).then_inc(sem("dn_gt"), 1)
                ve.wait_ge(sem("dn_bc"), NP)
                with ve.Fori(0, NP) as p:
                    for j in range(8):
                        t = 4 * NF + j
                        ve.wait_ge(sem("silu_ready"), p * 8 + (t + 1))
                        V.tensor_tensor(sg[:, t % 2, :], sg[:, t % 2, :],
                                        GB[:, bass.ds(p * (2 * S) + (j // FE) * S, S)], ALU.mult)\
                            .then_inc(sem("gated"), 1)
                        ve.wait_ge(sem("gated"), p * 8 + (j + 1))
                        V.tensor_tensor(HD[:, j, :], sg[:, t % 2, :], psG[:, t % 2, S:2 * S],
                                        ALU.mult).then_inc(sem("act_ready"), 1)

            def pool():
                c = BASE["pool"]
                arrived(ve, c)
                w = S + 16
                pa = blk(4, 3)[:, 0:8 * w].rearrange("p (k s) -> p k s", s=w)
                pb = blk(7, 3)[:, 0:8 * w].rearrange("p (k s) -> p k s", s=w)
                V.memset(blk(4, 3)[:, 0:8 * w], 0.0)
                link(V.memset(blk(7, 3)[:, 0:8 * w], 0.0))
                link(V.tensor_copy(pa[:, :, 8:8 + S], H[:, :, :]))
                link(V.tensor_tensor(pb[:, :, 1:w], pa[:, :, 0:w - 1], pa[:, :, 1:w], ALU.add))
                link(V.tensor_tensor(pa[:, 2:8, 1:w - 1], pb[:, 2:8, 0:w - 2], pb[:, 2:8, 2:w], ALU.add))
                link(V.tensor_tensor(pb[:, 4:8, 2:w - 2], pa[:, 4:8, 0:w - 4], pa[:, 4:8, 4:w], ALU.add))
                link(V.tensor_tensor(pa[:, 6:8, 4:w - 4], pb[:, 6:8, 0:w - 8], pb[:, 6:8, 8:w], ALU.add))
                for g in range(4):
                    src = (pb, pa, pb, pa)[g]
                    inv = chunk(c, 2048 + g * S, 2048 + (g + 1) * S)
                    last = V.tensor_tensor(SQ[:, 2 * g:2 * g + 2, :], src[:, 2 * g:2 * g + 2, 8:8 + S],
                                           inv[:, None, :].to_broadcast([P, 2, S]), ALU.mult)
                link(last)
                link(V.tensor_tensor(SQ[:, :, :], SQ[:, :, :], H[:, :, :], ALU.subtract), "pooled")
                ve.wait_ge(chunk_used, c + 1)
                for m in range(KT):
                    last = V.tensor_scalar(Y[:, m, :], psA[:, m // 2, (m % 2) * S:(m % 2 + 1) * S],
                                           col("pool_b", m), col("pool_scale", m), ALU.add, ALU.mult)
                    if m % 2 == 1:
                        last.then_inc(sem("y_ready"), 1)

            def attention(n, p, first, finish):
                for u in range(-1, n):
                    if u + 1 < n:
                        v = u + 1
                        ve.wait_ge(sem(p + "score"), v + 1)
                        first(v)
                    if u >= 0:
                        ve.wait_ge(sem(p + "exp"), 2 * u + 2)
                        finish(u)

            def negate_max(src, u, name):
                link(V.tensor_reduce(FAC[:, u % 2, :], src, AX.X, ALU.max))
                link(V.tensor_scalar(NMAX[:, u % 2, :], FAC[:, u % 2, :], -1.0, None, ALU.mult), name)

            def mla():
                c = BASE["mla"]
                root(rstd[:, :])
                for k in range(2):
                    V.scalar_tensor_tensor(CQN[:, k, :], LAT[:, k, :], col("q_norm", k), rstd[:, :],
                                           ALU.mult, ALU.mult)
                root(CQN[:, 3, :])
                link(V.scalar_tensor_tensor(CQN[:, 2, :], LAT[:, 2, :], col("kv_norm", 0), CQN[:, 3, :],
                                            ALU.mult, ALU.mult), "mla_cqn")
                ve.wait_ge(sem("mla_rot"), 1)
                arrived(ve, c + 3)
                cos = chunk(c + 3, 2 * SLOT, 2 * SLOT + S)
                sin = chunk(c + 3, 2 * SLOT + S, 2 * SLOT + 2 * S)
                link(V.tensor_tensor(ROT, psA[:, 0:2, :].rearrange("p b (a s) -> p (b a) s", a=2),
                                     sin[:, None, :].to_broadcast([P, 4, S]), ALU.mult))
                link(V.tensor_tensor(QR, QR, cos[:, None, :].to_broadcast([P, 4, S]), ALU.mult))
                link(V.tensor_tensor(QR, QR, ROT, ALU.add))
                link(V.tensor_scalar(QR, QR, MLA_SCALE, None, ALU.mult))
                link(V.tensor_tensor(ROT[:, 0, :], psG[:, 0, 0:S], sin, ALU.mult))
                link(V.tensor_tensor(LAT[:, 3, :], LAT[:, 3, :], cos, ALU.mult))
                link(V.tensor_tensor(LAT[:, 3, :], LAT[:, 3, :], ROT[:, 0, :], ALU.add))
                link(V.memset(KRM, 0.0))
                for j in range(4):
                    V.tensor_copy(KRM[32 * j:32 * j + 32, j, :], LAT[32 * j:32 * j + 32, 3, :])
                link(V.tensor_copy(KVTOK, psG[:, 1, 0:S].rearrange("p (t c) -> p t c", t=2)), "mla_ready")

                def first(u):
                    negate_max(psA[:, u % 2, :].rearrange("p (t s) -> p t s", t=2), u, "mla_max")

                def finish(u):
                    link(V.reciprocal(FAC[:, u % 2, :], SUM[:, u % 2, :]))
                    for t in range(TT):
                        last = V.tensor_scalar(PB[:, u % 2, t * S:(t + 1) * S], PB[:, u % 2, t * S:(t + 1) * S],
                                               FAC[:, u % 2, t:t + 1], None, ALU.mult)
                    last.then_inc(sem("mla_p"), 1)
                    if u % 2 == 1 and u >= 3:
                        out(u - 2)

                def out(h):
                    ve.wait_ge(sem("mla_up"), h + 1)
                    V.tensor_copy(MO[:, h // 2, :], psS[:, 1, 0:S]).then_inc(sem("mla_o"), 1)

                attention(HEADS, "mla_", first, finish)
                out(HEADS - 1)

            def small():
                ve.wait_ge(sem("u_out"), 6)
                link(V.tensor_tensor(UA[:, 4:8, :], UA[:, 4:8, :], UA[:, 8:12, :], ALU.mult))
                for j in (2, 1, 0):
                    d = 2 - j
                    for k in range(4):
                        w = col("conv_a", 4 * j + k)
                        if d == 0:
                            last = V.tensor_scalar(UA[:, 8 + k, :], UA[:, 4 + k, :], w, None, ALU.mult)
                        else:
                            last = V.scalar_tensor_tensor(UA[:, 8 + k, d:S], UA[:, 4 + k, 0:S - d], w,
                                                          UA[:, 8 + k, d:S], ALU.mult, ALU.add)
                    link(last)
                link(V.tensor_tensor(YA, UA[:, 0:4, :], UA[:, 8:12, :], ALU.mult))
                ve.wait_ge(sem("u_out"), 10)
                for y in range(2):
                    pe_ = col("pe", 16 * y, 16)
                    for g in range(2):
                        base = UK[:, 2 * y + g, :]
                        src = base.copy()
                        src = windows(base)
                        V.tensor_tensor(BL[y][:, :, g, :], src, pe_[:, :, None].to_broadcast([P, 16, NCMP]),
                                        ALU.add).then_inc(sem("blocks_ready"), 1)

            def windows(base):
                a = list(base.ap)
                return bass.AP(tensor=base.tensor, offset=base.offset, ap=[list(a[0]), [2, 16], [16, NCMP]])

            def nsa():
                ve.wait_ge(sem("cmp_out"), 1)
                arrived(ve, msk)
                V.tensor_copy(VGC, psG[0:NCMP, 1, 0:2 * P].rearrange("p (g c) -> p g c", g=2))
                root(SQ[:, 0:6, :])
                root(SQ[:, 6, 0:2 * NCMP])
                link(V.scalar_tensor_tensor(UQ, UQ, col("qk_gain", 0), SQ[:, 0:4, :], ALU.mult, ALU.mult))
                V.tensor_scalar(UQ, UQ, 64 ** -0.5, None, ALU.mult)
                V.memset(KG, 0.0)
                for y in range(2):
                    last = V.scalar_tensor_tensor(UKV[:, 2 * y, :], UKV[:, 2 * y, :], col("qk_gain", 2 + y),
                                                  SQ[:, 4 + y, :], ALU.mult, ALU.mult)
                link(last)
                for y in range(2):
                    for g in range(2):
                        V.tensor_copy(KG[64 * g:64 * g + 64, y, g, :], UKV[64 * g:64 * g + 64, 2 * y, :])
                V.scalar_tensor_tensor(KGC, psG[:, 0, 0:2 * NCMP].rearrange("p (g c) -> p g c", g=2),
                                       col("qk_gain", 1),
                                       SQ[:, 6, 0:2 * NCMP].rearrange("p (g c) -> p g c", g=2),
                                       ALU.mult, ALU.mult)
                ve.wait_ge(sem("nsa_v"), 1)
                link(V.memset(VG, 0.0))
                for y in range(2):
                    for g in range(2):
                        V.tensor_copy(VG[:, y, :, g, 64 * g:64 * g + 64],
                                      psS[:, 1, y * S:(y + 1) * S].rearrange("p (t c) -> p t c", t=2)
                                      [:, :, 64 * g:64 * g + 64])
                ve.wait_ge(sem("gate_sig"), 1)
                for t in range(TT):
                    last = V.tensor_scalar(GATE[:, t, 0:8], GATE[:, t, 0:8], mask(M_OK + t, 1), None, ALU.mult)
                link(last, "nsa_ready")

                def first(u):
                    t, y, g = NSA_UNITS[u]
                    w = NCMP if y == 0 else S
                    slope = 2.0 ** (-(g * 4 + t + 1))
                    v3 = lambda a: a.rearrange("p (t s) -> p t s", t=2)[:, :, 0:w]
                    nd = mask(M_OK + 2, 2 * NCMP).rearrange("p (t s) -> p t s", t=2) if y == 0 else \
                        v3(mask(M_ND, 512))
                    if u >= 2:
                        ve.wait_ge(sem("nsa_tr"), u - 1)
                    link(V.scalar_tensor_tensor(v3(NPB[:, u % 2, :]), nd, slope, v3(psA[:, u % 2, :]),
                                                ALU.mult, ALU.add))
                    negate_max(v3(NPB[:, u % 2, :]), u, "nsa_max")

                def finish(u):
                    t, y, g = NSA_UNITS[u]
                    w = NCMP if y == 0 else S
                    link(V.reciprocal(FAC[:, u % 2, :], SUM[:, u % 2, :]))
                    link(V.tensor_tensor(FAC[:, u % 2, :], FAC[:, u % 2, :], GATE[:, :, y * 8 + g * 4 + t], ALU.mult))
                    for i in range(TT):
                        last = V.tensor_scalar(NPB[:, u % 2, i * S:i * S + w], NPB[:, u % 2, i * S:i * S + w],
                                               FAC[:, u % 2, i:i + 1], None, ALU.mult)
                    last.then_inc(sem("nsa_p"), 1)

                attention(len(NSA_UNITS), "nsa_", first, finish)

            def gdn():
                ve.wait_ge(sem("nsa_o"), NSA_T)
                z3 = GX.rearrange("p (t h) -> p t h", t=2)
                dt3 = col("dt", 0, 4)[:, None, :].to_broadcast([P, 2, 4])
                link(V.tensor_tensor(z3, GT[:, :, 28:32], dt3, ALU.add), "gdn_z")
                link(V.tensor_scalar(GG, GX, 0.0, None, ALU.max))
                for j in (3, 2, 1, 0):
                    d = 3 - j
                    for k in range(12):
                        w = col("conv_g", 12 * j + k)
                        if d == 0:
                            last = V.tensor_scalar(CV[:, k, :], UG[:, k, :], w, None, ALU.mult)
                        else:
                            last = V.scalar_tensor_tensor(CV[:, k, d:S], UG[:, k, 0:S - d], w, CV[:, k, d:S],
                                                          ALU.mult, ALU.add)
                    link(last, "gdn_conv" if j == 0 else None)
                ve.wait_ge(sem("gdn_ln"), 1)
                link(V.tensor_tensor(GG, GG, EGC, ALU.add))
                g3 = GG.rearrange("p (t h) -> p t h", t=2)
                link(V.tensor_tensor(g3, g3, AL[:, None, :].to_broadcast([P, 2, 4]), ALU.mult))
                link(V.tensor_scalar(GG, GG, -1.0, None, ALU.mult), "gdn_g")
                for u in range(NU):
                    h, n = divmod(u, 2)
                    last = V.tensor_scalar(DEC[:, u, :], mask(M_TRI), unit_col(GG, h, n), None, ALU.mult)
                link(last, "gdn_gu")
                ve.wait_ge(sem("gdn_gc"), 1)
                link(V.tensor_copy(GC, psS[:, 0, 0:NU]))
                root(blk(2, 2))
                V.scalar_tensor_tensor(blk(16), blk(16), P ** -0.5, blk(2), ALU.mult, ALU.mult)
                link(V.tensor_tensor(blk(17), blk(17), blk(3), ALU.mult), "gdn_qk")
                ve.wait_ge(sem("gdn_row"), 1)
                row = psG[:, :, :].rearrange("p b (u s) -> p (b u) s", u=4)
                for u in range(NU):
                    h, n = divmod(u, 2)
                    V.tensor_scalar(DEC[:, u, :], row[:, u, :], unit_col(GC, h, n), 0.0, ALU.subtract, ALU.max)
                rl = RL.rearrange("p (n h) -> p h n", n=2)
                link(V.tensor_copy(rl, row[:, :, P - 1:P].rearrange("p (h n) o -> p h (n o)", n=2)))
                link(V.tensor_tensor(GX, RL, GC, ALU.subtract), "gdn_diff")
                ve.wait_ge(sem("gdn_exps"), 1)
                ve.wait_ge(sem("beta_ready"), 1)
                link(V.tensor_tensor(DEC, DEC, mask(M_TRIL)[:, None, :].to_broadcast([P, NU, P]), ALU.mult))
                link(V.tensor_tensor(BG, BETA, EGC, ALU.mult))
                ve.wait_ge(sem("gdn_kv"), 1)
                for u in range(NU):
                    h, n = divmod(u, 2)
                    k = psA[:, u // 4, (u % 4) * P:(u % 4 + 1) * P]
                    v = psA[:, 2 + u // 4, (u % 4) * P:(u % 4 + 1) * P]
                    V.tensor_scalar(KBG[:, u, :], k, unit_col(BG, h, n), None, ALU.mult)
                    V.tensor_scalar(KDEC[:, u, :], k, unit_col(KD, h, n), None, ALU.mult)
                    last = V.tensor_scalar(VB[:, u, :], v, unit_col(BETA, h, n), None, ALU.mult)
                link(last, "gdn_kvtok")
                ve.wait_ge(sem("gdn_gram"), 1)
                for u in range(NU):
                    h, n = divmod(u, 2)
                    V.scalar_tensor_tensor(L_[:, u, :], psA[:, u // 4, (u % 4) * P:(u % 4 + 1) * P],
                                           unit_col(BETA, h, n), DEC[:, u, :], ALU.mult, ALU.mult)
                link(V.tensor_tensor(AT_, psA[:, 2:4, :].rearrange("p b (u s) -> p (b u) s", u=4), DEC, ALU.mult))
                link(V.tensor_tensor(L_, L_, mask(M_STRICT)[:, None, :].to_broadcast([P, NU, P]), ALU.mult), "gdn_l")
                ve.wait_ge(sem("gdn_er"), 1)
                rl2 = GX.rearrange("p (n h) -> p h n", n=2)
                link(V.tensor_copy(rl2, ER[:, :, P - 1:P].rearrange("p (h n) o -> p h (n o)", n=2)))
                link(V.tensor_tensor(ER, ER, blk(16).rearrange("p (u s) -> p u s", u=NU), ALU.mult))
                idb = ident[:, None, :].to_broadcast([P, NU, P])
                ve.wait_ge(sem("gdn_x"), 1)
                V.tensor_tensor(TM, idb, XM, ALU.subtract)
                link(V.tensor_tensor(TMT, idb, XMT, ALU.subtract), "gdn_t")
                for lev in range(1, 7):
                    ve.wait_ge(sem("gdn_r"), lev)
                    V.tensor_tensor(TM, TM, psG[:, :, :].rearrange("p b (u s) -> p (b u) s", u=4), ALU.subtract)
                    link(V.tensor_tensor(TMT, TMT, psS[:, :, :].rearrange("p b (u s) -> p (b u) s", u=4),
                                         ALU.subtract), "gdn_t")
                ve.wait_ge(sem("gdn_s1"), 1)
                link(V.tensor_copy(SST, psG[:, 0, :].rearrange("p (h s) -> p h s", h=GH)), "gdn_state")
                ve.wait_ge(sem("gdn_ws"), 1)
                link(V.tensor_tensor(VNEW, UU[:, 1:NU:2, :], psG[:, 1, :].rearrange("p (h s) -> p h s", h=GH),
                                     ALU.subtract), "gdn_vnew")
                root(blk(0))
                link(V.scalar_tensor_tensor(blk(3), blk(3), col("out_gain", 0), blk(0), ALU.mult, ALU.mult))
                link(V.tensor_tensor(blk(15), blk(3), blk(13), ALU.mult), "yg_ready")

            def merge():
                for j in range(24):
                    m, r = divmod(j, 3)
                    ve.wait_ge(sem("mrg_sig"), j + 1)
                    ps = psG[:, j % 2, S:2 * S]
                    if r == 0:
                        link(V.tensor_tensor(Y[:, m, :], sg[:, j % 2, :], ps, ALU.mult), "mrg_out")
                    else:
                        link(V.tensor_tensor(act[:, 0, :], sg[:, j % 2, :], ps, ALU.mult), "mrg_out")
                        link(V.tensor_tensor(Y[:, m, :], Y[:, m, :], act[:, 0, :], ALU.add),
                             "merged" if r == 2 else None)
                ve.wait_ge(sem("hyb_acc"), 1)
                add_acc()

            def add_acc():
                for b in range(4):
                    last = V.tensor_tensor(X[:, 2 * b:2 * b + 2, :], X[:, 2 * b:2 * b + 2, :],
                                           psA[:, b, :].rearrange("p (a s) -> p a s", a=2), ALU.add)
                link(last, "x_ready")

            def router():
                w = blk(24)
                LG = w[:, 192:192 + 72]
                lg3 = w[:, 192:264]
                G3 = w[:, 0:64].rearrange("p (t e) -> p t e", t=2)
                LE = w[:, 128:192].rearrange("p (t e) -> p t e", t=2)
                EXL = w[:, 256:264].rearrange("p (t e) -> p t e", t=2)
                LGT = w[:, 264:336].rearrange("p (t e) -> p t e", t=2)
                OH = w[:, 336:344].rearrange("p (t e) -> p t e", t=2)
                T1 = w[:, 384:448].rearrange("p (t e) -> p t e", t=2)
                O1 = w[:, 448:512].rearrange("p (t e) -> p t e", t=2)
                O2 = w[:, 512:576].rearrange("p (t e) -> p t e", t=2)
                W4 = w[:, 576:580]
                W32 = w[:, 584:616]
                Z = w[:, 640:656].rearrange("p (i t o) -> p i t o", i=8, t=2)
                for i in range(32):
                    V.memset(W32[:, i:i + 1], float(32 - i))
                for i in range(4):
                    V.memset(W4[:, i:i + 1], float(4 - i))
                ve.wait_ge(chunk_used, BASE["out"] + 3)
                rt = psS[:, 1, 0:72].rearrange("p (t c) -> p t c", t=2)
                b36 = col("b_rt", 0, 36)[:, None, :].to_broadcast([P, 2, 36])
                link(V.tensor_tensor(LGT, rt, b36, ALU.add))

                def first_max(src, weights, out, best, n):
                    link(V.tensor_reduce(Z[:, best], src, AX.X, ALU.max))
                    link(V.tensor_tensor(out, src, Z[:, best].to_broadcast([P, 2, n]), ALU.is_equal))
                    link(V.tensor_tensor(out, out, weights[:, None, :].to_broadcast([P, 2, n]), ALU.mult))
                    link(V.tensor_reduce(Z[:, 7], out, AX.X, ALU.max))
                    link(V.tensor_tensor(out, out, Z[:, 7].to_broadcast([P, 2, n]), ALU.is_equal))

                first_max(LGT[:, :, 0:4], W4, OH, 0, 4)
                link(V.tensor_tensor(EXL, LGT[:, :, 0:4], Z[:, 0].to_broadcast([P, 2, 4]), ALU.subtract))
                for t in range(2):
                    o4 = OH[:, t, :][:, :, None].to_broadcast([P, 4, 8])
                    le = LGT[:, t, 4:36].rearrange("p (g e) -> p g e", g=4)
                    link(V.tensor_tensor(LE[:, t, :].rearrange("p (g e) -> p g e", g=4), le, o4, ALU.mult))
                    link(V.tensor_scalar(OH[:, t, :], OH[:, t, :], 1.0, 1e30, ALU.subtract, ALU.mult))
                    link(V.tensor_tensor(LE[:, t, :].rearrange("p (g e) -> p g e", g=4),
                                         LE[:, t, :].rearrange("p (g e) -> p g e", g=4), o4, ALU.add))
                link(V.tensor_reduce(Z[:, 1], LE, AX.X, ALU.max))
                link(V.tensor_tensor(LE, LE, Z[:, 1].to_broadcast([P, 2, 32]), ALU.subtract), "rt_max")
                ve.wait_ge(sem("rt_exp"), 1)
                link(V.tensor_reduce(Z[:, 2], EXL, AX.X, ALU.add))
                first_max(LE, W32, O1, 3, 32)
                link(V.scalar_tensor_tensor(T1, O1, -2.0, LE, ALU.mult, ALU.add))
                first_max(T1, W32, O2, 4, 32)
                link(V.tensor_tensor(ASG, O1, O2, ALU.add), "rt_asg")
                link(V.tensor_tensor(Z[:, 5], Z[:, 3], Z[:, 4], ALU.add))
                link(V.tensor_tensor(Z[:, 5], Z[:, 5], Z[:, 2], ALU.mult))
                link(V.reciprocal(Z[:, 5], Z[:, 5]))
                link(V.tensor_tensor(Z[:, 3], Z[:, 3], Z[:, 5], ALU.mult))
                link(V.tensor_tensor(Z[:, 4], Z[:, 4], Z[:, 5], ALU.mult))
                link(V.tensor_tensor(O1, O1, Z[:, 3].to_broadcast([P, 2, 32]), ALU.mult))
                link(V.tensor_tensor(O2, O2, Z[:, 4].to_broadcast([P, 2, 32]), ALU.mult))
                link(V.tensor_tensor(G3, O1, O2, ALU.add), "rt_gate")
                ve.wait_ge(sem("rt_cnt"), 1)
                link(V.tensor_tensor(POS, ASG, psS[:, 0, 0:2 * E].rearrange("p (t e) -> p t e", t=2), ALU.mult))
                link(V.tensor_reduce(blk(22)[:, 128:129], blk(22)[:, 64:128], AX.X, ALU.max), "rt_max1")
                link(V.tensor_scalar(POS, POS, -1.0, None, ALU.add))
                ve.wait_ge(sem("rt_max1t"), 1)
                link(V.tensor_reduce(blk(22)[0:1, 130:131], psS[0:1, 0, 256:256 + P], AX.X, ALU.max))
                link(V.tensor_copy(most[0:1, 0:1], blk(22)[0:1, 130:131]), "rt_flag")

            V.memset(eps[:, :], EPS)
            ve.wait_ge(sem("cols_in"), 16)
            ve.wait_ge(sem("x_in"), 16)
            link(V.memset(st[:, :], 0.0), "x_ready")
            ve.wait_ge(sem("silc_ready"), 1)
            for t in range(ADA[0]):
                ada(0, t, t, 0, t - 1 if t >= 2 else None)
            ve.wait_ge(chunk_used, ADA[0])
            mod_out(0, 0, 18)
            pre_norm(0)
            ffn(BASE["ffn0"], 0, NF, ADA[1], 6)
            ve.wait_ge(chunk_used, BASE["pool"])
            mod_out(0, 18, 54)
            post_norm(0, BASE["pool"], 0, 0)
            pre_norm(1)
            ve.wait_ge(h_ready, 16)
            pool()
            post_norm(1, 0, 0, 1, from_acc=False)
            pre_norm(2)
            ffn(BASE["ffn1"], NF, NF, ADA[2], 24)
            ve.wait_ge(chunk_used, BASE["ffn2"])
            mod_out(1, 0, 54)
            post_norm(2, BASE["ffn2"], 0, 2)
            pre_norm(3)
            ffn(BASE["ffn2"], 2 * NF, NF, ADA[3], 42)
            ve.wait_ge(chunk_used, BASE["mla"])
            mod_out(1, 54, 18)
            post_norm(3, BASE["mla"], 1, 0)
            pre_norm(4)
            mla()
            post_norm(4, BASE["mla"] + 7, 1, 1)
            pre_norm(5)
            ffn(BASE["ffn3"], 3 * NF, NF)
            post_norm(5, BASE["ffn3"] + NF, 1, 2)
            pre_norm(6)
            small()
            nsa()
            gdn()
            merge()
            pre_norm(7)
            router()
            n = ve.value_load(most[0:1, 0:1], min_val=0, max_val=S)
            with ve.If(n <= CAP):
                sparse()
            with ve.Else():
                dense()
            ve.wait_ge(sem("moe_acc"), 1)
            add_acc()

        @block.gpsimd
        def _(po):
            for lev in range(7):
                if lev == 0:
                    po.wait_ge(sem("gdn_ltout"), 1)
                    po.wait_ge(sem("gdn_l"), 1)
                    arrived(po, msk)
                else:
                    if lev == 1:
                        po.wait_ge(sem("gdn_t"), 1)
                    else:
                        po.wait_ge(sem("gdn_p1"), lev - 1)
                low = mask(M_LOW + lev * P)[:, None, :].to_broadcast([P, NU, P])
                upp = mask(M_UPP + lev * P)[:, None, :].to_broadcast([P, NU, P])
                nc.gpsimd.tensor_tensor(XM, L_, low, ALU.mult)
                nc.gpsimd.tensor_tensor(XMT, LT, upp, ALU.mult).then_inc(sem("gdn_x"), 1)


def _slots(w):
    import numpy as np
    k, m = w.shape
    w = w.reshape(k // P, P, m // P, P).transpose(2, 1, 0, 3)
    return [np.ascontiguousarray(w[i]).reshape(P, -1) for i in range(m // P)]


def _pack_stream(a):
    import numpy as np
    out = np.zeros((NCHUNK, P, CHUNK), np.float32)

    def put(name, parts, at=0):
        c, w = BASE[name], at
        for p in parts:
            n = p.shape[1]
            while n:
                q, o = divmod(w, CHUNK)
                k = min(n, CHUNK - o)
                out[c + q, :p.shape[0], o:o + k] = p[:, p.shape[1] - n:p.shape[1] - n + k]
                w, n = w + k, n - k

    ada = np.stack(_slots(a["ada_w"][0]) + _slots(a["ada_w"][1])).reshape(-1, 3, P, SLOT)
    ada = ada.transpose(0, 2, 1, 3).reshape(-1, P, CHUNK)
    out[0:ADA[0]] = ada[0:ADA[0]]
    for j in range(3):
        a0 = sum(ADA[:j + 1])
        for t in range(ADA[j + 1]):
            out[BASE[f"ffn{j}"] + 2 + 2 * t] = ada[a0 + t]
    for j in range(4):
        w_in, w_out = a["ffn_w_in"][j // 2, j % 2], a["ffn_w_out"][j // 2, j % 2]
        up = w_in.reshape(KT, P, 2, NF, P)
        at = [BASE[f"ffn{j}"] + ffn_pos(f, ADA[j + 1] if j < 3 else 0) for f in range(NF)]
        both = up.transpose(3, 1, 2, 0, 4).reshape(NF, P, 2 * SLOT)
        out[at] = np.concatenate([both, w_out.reshape(NF, P, SLOT)], axis=2)
    pw = a["pool_w"][0].reshape(4, 2, P, 2, P).transpose(2, 0, 3, 1, 4).reshape(P, 2048)
    t = np.arange(S)
    inv = np.stack([1.0 / (np.clip(t + w // 2, 0, S) - np.clip(t - w // 2, 0, S)) for w in (2, 4, 8, 16)])
    put("pool", [pw, np.broadcast_to(inv.astype(np.float32).reshape(1, -1), (P, 1024))])

    w = a["mla_w_in"][0]
    w = np.concatenate([w[:, :384]] + [w[:, 384:416]] * 4, axis=1)
    uq = a["mla_w_uq"][0]
    uq = np.concatenate([uq[:, :, :64].reshape(256, 1024), uq[:, :, 64:].reshape(256, 512)], axis=1)
    uq = uq.reshape(2, P, 12, P).transpose(1, 2, 0, 3).reshape(P, 24 * P)
    uk = np.zeros((P, HEADS, P), np.float32)
    uv = np.zeros((P, HEADS, P), np.float32)
    for h in range(HEADS):
        b = 64 * (h % 2)
        uk[b:b + 64, h, :] = a["mla_w_uk"][0][:, h, :].T
        uv[:, h, b:b + 64] = a["mla_w_uv"][0][:, h, :]
    ang = np.arange(S, dtype=np.float32)[None, :] * \
        (1.0 / (np.float32(10000.0) ** (np.arange(0, 32, 2, dtype=np.float32) / 32)))[:, None].astype(np.float32)
    cos = np.tile(np.cos(ang).astype(np.float32), (8, 1))
    sin = np.tile(np.sin(ang).astype(np.float32), (8, 1))
    rot = np.zeros((P, P), np.float32)
    for p in range(P):
        if p % 32 < 16:
            rot[p + 16, p] = -1.0
        else:
            rot[p - 16, p] = 1.0
    put("mla", _slots(w) + [uq, uk.reshape(P, -1), uv.reshape(P, -1), cos, sin, rot])
    put("mla", _slots(a["mla_w_o"][0]), 4 * CHUNK)

    w = a["w_in_2"][0]
    ua, uq_, ukv, ung, ugq, uz, ub, uaa = np.split(w, np.cumsum([1536, 512, 768, 24, 1536, 512, 4]), axis=1)
    uq_ = uq_.reshape(D, 2, 4, 64).transpose(0, 2, 1, 3).reshape(D, 512)
    kv = ukv.reshape(D, 6, 2, 64)
    dup = [kv[:, y, g] for y in (0, 1) for g in (0, 1) for _ in (0, 1)]
    rest = [kv[:, y].reshape(D, P) for y in range(2, 6)]
    big = np.concatenate([ua, uq_] + dup + rest + [ugq, uz], axis=1)
    small = np.concatenate([ung, ub, uaa], axis=1).reshape(KT, P, 32).transpose(1, 0, 2).reshape(P, 256)
    put("hyb", _slots(big) + [small])

    w1 = a["cmp_w1_2"][0].reshape(2, 16, P, 256).transpose(0, 2, 1, 3).reshape(2, P, 4096)
    w2 = np.zeros((2, P, 2, 2, P), np.float32)
    for g in range(2):
        w2[:, :, :, g, 64 * g:64 * g + 64] = a["cmp_w2_2"][0].reshape(2, 2, P, 64).transpose(0, 2, 1, 3)
    put("cmp", [w1[0], w1[1], w2[0].reshape(P, 512), w2[1].reshape(P, 512)])

    m = np.zeros((P, CHUNK), np.float32)
    q = np.arange(P)
    for i in range(TT):
        dist = (q + P * i)[:, None] - np.arange(S)[None, :]
        m[:, i * S:(i + 1) * S] = np.where(dist >= 0, -dist, -1e33)
        dc = (q + P * i)[:, None] - (np.arange(NCMP) * 16 + 31)[None, :]
        m[:, M_OK + 2 + i * NCMP:M_OK + 2 + (i + 1) * NCMP] = np.where(dc >= 0, -dc, -1e33)
        m[:, M_OK + i] = (dc >= 0).any(axis=1)
    for lev in range(7):
        b = 1 << lev
        low = (q[:, None] // (2 * b) == q[None, :] // (2 * b)) & (q[:, None] // b % 2 == 1) & (q[None, :] // b % 2 == 0)
        m[:, M_LOW + lev * P:M_LOW + (lev + 1) * P] = low
        m[:, M_UPP + lev * P:M_UPP + (lev + 1) * P] = low.T
    m[:, M_STRICT:M_STRICT + P] = q[:, None] > q[None, :]
    m[:, M_TRIL:M_TRIL + P] = q[:, None] >= q[None, :]
    m[:, M_HALF:M_HALF + P] = q[:, None] // 64 == q[None, :] // 64
    m[:, M_TRI:M_TRI + P] = q[:, None] <= q[None, :]
    put("msk", [m])

    gate = a["w_gate_2"][0].reshape(KT, P, 3, KT, P)
    br = a["w_branch_2"][0].reshape(3, 512, D).copy()
    br[1] = br[1].reshape(2, 4, 64, D).transpose(1, 0, 2, 3).reshape(512, D)
    br = br.reshape(3, 4, P, KT, P)
    for j in range(24):
        mt, r = divmod(j, 3)
        c, s = BASE["mrg"] + j // 2, j % 2
        out[c, :, s * SLOT:(s + 1) * SLOT] = gate[:, :, r, mt].transpose(1, 0, 2).reshape(P, SLOT)
        out[c, :, 2 * SLOT + s * 512:2 * SLOT + s * 512 + 512] = br[r, :, :, mt].transpose(1, 0, 2).reshape(P, 512)
    wr = np.concatenate([a["w_router_group_2"][0], a["w_router_expert_2"][0]], axis=1)
    put("out", _slots(a["w_out_2"][0]) + [wr.reshape(KT, P, 36).transpose(1, 0, 2).reshape(P, 288)])
    o = out[BASE["moe"]:].reshape(NP, 8, P, 6, 512)
    gate, up = (a[n][0].reshape(E, KT, P, FE * P) for n in ("w_expert_gate_2", "w_expert_up_2"))
    down = a["w_expert_down_2"][0].reshape(E, FE, P, 2, 512)
    for e in range(2):
        for k in range(KT):
            for u, w in enumerate((gate, up)):
                g = (u * KT + k) * 2 + e
                o[:, g // 6, :, g % 6] = w[e::2, k]
        for h in range(2):
            for f in range(FE):
                g = 4 * KT + (h * FE + f) * 2 + e
                o[:, g // 6, :, g % 6] = down[e::2, f, :, h]
    return out


def _pack_cols(a):
    import numpy as np
    out = np.zeros((P, NCOL), np.float32)

    def put(name, v):
        i, j = COLS[name]
        out[:, i:j] = v

    def by_channel(v):
        return v.reshape(-1, P).T

    put("c", by_channel(a["c"]))
    put("ada_b", by_channel(a["ada_b"]))
    put("norm_g", by_channel(a["norm_g"]))
    for name, key in (("pool_b", "pool_b"), ("pool_scale", "pool_scale"), ("norm_mix", "norm_mix_2"),
                      ("norm_ffn", "norm_ffn_2"), ("b_gate", "b_gate_2"), ("q_norm", "mla_q_norm"),
                      ("kv_norm", "mla_kv_norm"), ("conv_a", "conv_a_w_2"), ("conv_g", "gdn_conv_w_2"),
                      ("out_gain", "gdn_out_gain_2")):
        put(name, by_channel(a[key]))
    put("qk_gain", np.concatenate([a["nsa_qk_gain_2"][0].T] * 2, axis=0))
    put("pe", a["cmp_pe_2"][0].reshape(2, 16, P).transpose(2, 0, 1).reshape(P, 32))
    put("b_rt", np.concatenate([a["b_router_group_2"][0], a["b_router_expert_2"][0]])[None, :])
    put("a_log", a["gdn_a_log_2"][0][None, :])
    put("dt", a["gdn_dt_bias_2"][0][None, :])
    return out


def _consts():
    import numpy as np
    q = np.arange(P)
    return np.concatenate([np.eye(P), np.ones((P, P)), q[:, None] <= q[None, :],
                           np.broadcast_to(np.arange(CAP), (P, CAP))], axis=1).astype(np.float32)


def kernel(**inputs):
    import numpy as np
    import concourse.bacc as bacc
    from concourse.bass_utils import run_bass_kernel_spmd as run

    a = {k: np.asarray(v) for k, v in inputs.items()}
    arrays = {
        "stream": _pack_stream(a),
        "cols_in": _pack_cols(a),
        "consts": _consts(),
        "x_in": np.ascontiguousarray(a["x"][0].T.reshape(KT, P, S).transpose(1, 0, 2)),
    }
    nc = bacc.Bacc("TRN2", target_bir_lowering=False, num_devices=1)
    args = [nc.dram_tensor(n, v.shape, F32, kind="ExternalInput").ap() for n, v in arrays.items()]
    out = nc.dram_tensor("x_out", (P, KT, S), F32, kind="ExternalOutput").ap()
    build(nc, *args, out)
    r = run(nc, [arrays], core_ids=[0])
    y = np.asarray(r.results[0]["x_out"])
    return np.ascontiguousarray(y.transpose(1, 0, 2).reshape(D, S).T)[None]
```

```python
from contextlib import ExitStack

import concourse.bass as bass
from concourse import mybir

F32 = mybir.dt.float32
F32R = mybir.dt.float32r
ALU = mybir.AluOpType
ACT = mybir.ActivationFunctionType
AX = mybir.AxisListType

P = 128
S = 256
D = 1024
KT = D // P
TT = S // P
SLOT = KT * P
CHUNK = 3 * SLOT
RING = 6
EPS = 1e-6
DEPTH = 2
NF = 2816 // P
HEADS = 16
MLA_SCALE = (64 + 32) ** -0.5
NSA_T = 4
NCMP = 15
GH = 4
NU = GH * TT
E = 32
FE = 4
NP = E // 2
CAP = 64

ADA = [6, 18, 18, 6]
STAGES = [("ada", ADA[0]), ("ffn0", NF + ADA[1]), ("pool", 1), ("ffn1", NF + ADA[2]), ("ffn2", NF + ADA[3]),
          ("mla", 7), ("ffn3", NF), ("hyb", 14), ("cmp", 3), ("msk", 1), ("mrg", 12), ("out", 3),
          ("moe", E * FE)]
BASE = {}


def ffn_pos(f, na):
    return f + min(max(f - 1, 0), na)


_at = 0
for _n, _c in STAGES:
    BASE[_n] = _at
    _at += _c
NCHUNK = _at

COLS = {}
NCOL = 0
for _n, _c in [("c", 8), ("ada_b", 144), ("norm_g", 96), ("pool_b", 8), ("pool_scale", 8),
               ("norm_mix", 8), ("norm_ffn", 8), ("b_gate", 24), ("q_norm", 2), ("kv_norm", 1),
               ("conv_a", 12), ("conv_g", 48), ("qk_gain", 4), ("out_gain", 1), ("pe", 32),
               ("b_rt", 36), ("a_log", 4), ("dt", 4)]:
    COLS[_n] = (NCOL, NCOL + _c)
    NCOL += _c

M_ND, M_LOW, M_UPP = 0, 512, 512 + 7 * P
M_STRICT, M_TRIL, M_HALF, M_TRI, M_OK = 2304, 2432, 2560, 2688, 2816


def build(nc, stream, cols_d, ident_d, x_d, out_d):
    ctx = ExitStack()
    with ctx:
        def sb(name, shape):
            return ctx.enter_context(nc.sbuf_tensor(name, shape, F32))

        names = {}

        def sem(name):
            if name not in names:
                names[name] = ctx.enter_context(nc.semaphore(name))
            return names[name]

        ring = sb("ring", [P, RING, CHUNK])
        X = sb("X", [P, KT, S])
        H = sb("H", [P, KT, S])
        mem_at = nc.sbuf_base
        mem = sb("mem", [P, 26, 1024])
        cols = sb("cols", [P, NCOL])
        cst = sb("cst", [P, 3 * P + CAP])
        most = ctx.enter_context(nc.sbuf_tensor("most", [1, 1], mybir.dt.int32))
        mod = sb("mod", [P, DEPTH, 72])
        modA = sb("modA", [P, DEPTH, 3, KT])
        modC = sb("modC", [P, DEPTH, 3, KT])
        silc = sb("silc", [P, KT])
        rstd = sb("rstd", [P, S])
        act = sb("act", [P, 2, S])
        sg = sb("sg", [P, 2, S])
        eps = sb("eps", [P, 1])
        st = sb("st", [P, 512])
        psA = ctx.enter_context(nc.psum_tensor("psA", [P, 4, 512], F32))
        psG = ctx.enter_context(nc.psum_tensor("psG", [P, 2, 512], F32))
        psS = ctx.enter_context(nc.psum_tensor("psS", [P, 2, 512], F32))
        ident, ones, before = cst[:, 0:P], cst[:, P:2 * P], cst[:, 2 * P:3 * P]
        iota = cst[:, 3 * P:3 * P + CAP]

        def blk(i, n=1):
            return mem[:, i:i + n, :].rearrange("p a b -> p (a b)")

        def tiles(i, n=1, w=S):
            return blk(i, n).rearrange("p (t s) -> p t s", s=w)

        def col(name, i, n=1):
            a = COLS[name][0] + i
            return cols[:, a:a + n]

        def chunk(n, a=0, b=CHUNK):
            return ring[:, n % RING, a:b]

        Y, SQ = tiles(0, 2), tiles(2, 2)
        ADP = blk(24)[:, 0:6 * P].rearrange("p (b m n) -> p b m n", b=2, m=3)
        parts = nc.alloc_sbuf_tensor_at("parts", [P, 23, 1024], F32R, offset=mem_at)

        def part(i, n=1):
            return parts[:, i:i + n, :].rearrange("p a b -> p (a b)")

        WG = [part(4 + 4 * b, 4).rearrange("p (h n) -> p h n", h=2) for b in range(2)]
        WD = [part(12 + 2 * b, 2).rearrange("p (h n) -> p h n", h=2) for b in range(3)]
        HP = part(18, 4).rearrange("p (h k s) -> p h k s", h=2, k=KT)
        HY = part(0, 4).rearrange("p (h k s) -> p h k s", h=2, k=KT)
        WS = [part(i, 2).rearrange("p (h n) -> p h n", h=2) for i in (14, 16, 20)]
        HM = part(16, 4).rearrange("p (h k s) -> p h k s", h=2, k=KT)
        BM = [part(i, 2).rearrange("p (h k s) -> p h k s", h=2, k=4) for i in (6, 8, 10)]
        WM = [part(i, 3).rearrange("p (h n) -> p h n", h=2) for i in (20, 2)]
        AP = part(22).rearrange("p (b h s) -> p b h s", b=2, h=2)
        chunk_used, h_ready, x_ready = sem("chunk_used"), sem("h_ready"), sem("x_ready")
        full = [sem(f"chunk_full{j}") for j in range(RING)]

        def arrived(eng, n, i=0):
            if isinstance(i, int):
                eng.wait_ge(full[(n + i) % RING], 16 * ((n + i) // RING + 1))
            else:
                eng.wait_ge(full[n % RING], i * 16 // RING + 16 * (n // RING + 1))

        def take_over(eng, stage):
            arrived(eng, BASE[stage] - 1 + RING)

        class Chain:

            def __init__(self, eng, name):
                self.eng, self.name, self.n = eng, name, {}

            def link(self, ins, name=None):
                name = name or self.name
                self.n[name] = self.n.get(name, 0) + 1
                ins.then_inc(sem(name), 1)
                self.eng.wait_ge(sem(name), self.n[name])

        def pre_cols(n):
            if n < 6:
                i, s = divmod(n, 3)
                return (lambda k: modA[:, i, s, k:k + 1]), (lambda k: mod[:, i, 24 * s + k:24 * s + k + 1])
            name = "norm_mix" if n == 6 else "norm_ffn"
            return (lambda k: col(name, k)), None

        block = ctx.enter_context(nc.Block())

        @block.sync
        def _(sp):
            sp.dma_start(cols[:, :], cols_d).then_inc(sem("cols_in"), 16)
            sp.dma_start(cst[:, :], ident_d).then_inc(sem("cst_in"), 16)
            for j in range(RING):
                sp.dma_start(ring[:, j, :], stream[j, :, :]).then_inc(full[j], 16)
                if j == 2:
                    sp.dma_start(X[:, :, :], x_d).then_inc(sem("x_in"), 16)
            whole = NCHUNK // RING * RING
            with sp.Fori(1, NCHUNK // RING) as r:
                i = r * RING
                for j in range(RING):
                    sp.wait_ge(chunk_used, i + (j + 1 - RING))
                    sp.dma_start(ring[:, j, :], stream[bass.ds(i + j, 1), :, :].rearrange("o p n -> (o p) n")).then_inc(full[j], 16)
            for n in range(whole, NCHUNK):
                sp.wait_ge(chunk_used, n + 1 - RING)
                sp.dma_start(ring[:, n % RING, :], stream[n, :, :]).then_inc(full[n % RING], 16)
            sp.wait_ge(x_ready, 4 * 9)
            sp.dma_start(out_d, X[:, :, :]).then_inc(sem("out_written"), 16)
            sp.wait_ge(sem("out_written"), 16)

        LAT, CQN, QN, QR, ROT, KRM = tiles(4), tiles(5), tiles(6, 2), tiles(8), tiles(9), tiles(10)
        KVTOK = blk(11)[:, 0:S].rearrange("p (t c) -> p t c", t=TT)
        QL = blk(11)[:, 512:1024].rearrange("p (b s) -> p b s", b=2)
        PB, PTB = tiles(12, 1, 512), tiles(13, 1, 512)
        OL = blk(14)[:, 0:512].rearrange("p (b s) -> p b s", b=2)
        MO = tiles(15, 2)
        UA, UQ, UK, UKV, UG, UZ = tiles(4, 3), tiles(7), tiles(8), tiles(9), tiles(10, 3), tiles(13)
        YN, YG = tiles(14), tiles(15)
        YA = tiles(5)
        KG = blk(16).rearrange("p (y g s) -> p y g s", y=2, g=2)
        VG = blk(17).rearrange("p (y t g c) -> p y t g c", y=2, t=TT, g=2)
        BL = [blk(18)[:, 512 * y:512 * y + 480].rearrange("p (l g c) -> p l g c", l=16, g=2) for y in range(2)]
        HID = blk(19)[:, 0:120].rearrange("p (y m g c) -> p y m g c", y=2, m=2, g=2)
        KGC = blk(19)[:, 128:128 + 2 * NCMP].rearrange("p (g c) -> p g c", g=2)
        VGC = blk(19)[0:NCMP, 256:512].rearrange("p (g c) -> p g c", g=2)
        NPB, NPTB = tiles(20, 1, 512), tiles(21, 1, 512)
        GT = st[:, 0:64].rearrange("p (t c) -> p t c", t=TT)
        GATE = st[:, 64:64 + 48].rearrange("p (t c) -> p t c", t=TT)
        NMAX = st[:, 120:124].rearrange("p (b t) -> p b t", b=2)
        SUM = st[:, 124:128].rearrange("p (b t) -> p b t", b=2)
        FAC = st[:, 128:132].rearrange("p (b t) -> p b t", b=2)
        BETA, GG, GC, EGC, KD, BG, GX = (st[:, 136 + 8 * i:144 + 8 * i] for i in range(7))
        AL = st[:, 200:204]
        RL = st[:, 208:216]

        def unit_col(t, h, n):
            return t[:, n * GH + h:n * GH + h + 1]

        def units(b):
            return blk(b).rearrange("p (u s) -> p u s", u=NU)

        CV = tiles(23, 3)
        KBG, KDEC, VB, DEC, ER, L_, LT = (units(i) for i in (19, 20, 21, 22, 16, 17, 18))
        TM, TMT, XM, XMT, P1 = (units(i) for i in (7, 8, 9, 10, 11))
        AT_, ATT, WT, UU = units(4), units(6), units(0), units(1)
        SST = blk(2)[:, 0:512].rearrange("p (h s) -> p h s", h=GH)
        VNEW = blk(2)[:, 512:1024].rearrange("p (h s) -> p h s", h=GH)
        OT = blk(3).rearrange("p (h n s) -> p h n s", h=GH, n=2)
        QT, KTT, VT = CV[:, 0:4], CV[:, 4:8], CV[:, 8:12]
        ASG = blk(22)[:, 0:64].rearrange("p (t e) -> p t e", t=TT)
        POS = blk(22)[:, 64:128].rearrange("p (t e) -> p t e", t=TT)
        SEL, SELG, SELGT = blk(4, 4), blk(8, 4), blk(12, 4)
        HTOK, XE, YS = tiles(16, 2, D), tiles(18, 1, P), blk(20)
        HT = blk(19)[:, 0:512].rearrange("p (f s) -> p f s", f=FE)
        HACT, HSIL = blk(21)[:, 0:512], blk(21)[:, 512:1024]
        GB = blk(4, 8)
        HD = tiles(12, 2)

        msk = BASE["msk"]

        def mask(a, n=P):
            return chunk(msk, a, a + n)

        NSA_UNITS = [(t, y, g) for t in range(NSA_T) for y in range(3) for g in range(2)]

        @block.tensor
        def _(pe):
            def mm(out, lhsT, rhs, start, stop):
                return nc.tensor.matmul(out, lhsT, rhs, start=start, stop=stop, skip_group_check=True)

            pe.wait_ge(sem("cst_in"), 16)

            def ada(n, t, i=0):
                pe.wait_ge(sem("ada_prod"), i + (n + t + 1))
                for m in range(3):
                    at = psS[:, 1, 3 * t + m:3 * t + m + 1] if isinstance(i, int) else \
                        psS[:, 1, bass.ds(i * 3 + (3 * t + m), 1)]
                    last = mm(at, ADP[:, (n + t) % 2, m, :], ones[:, 0:1], start=True, stop=True)
                last.then_inc(sem("ada_sum"), 1)

            def pre_norm(n):
                for k in range(KT):
                    if k % 2 == 0:
                        pe.wait_ge(sem("pre_sq"), 4 * n + k // 2 + 1)
                    last = mm(psS[:, 0, 0:S], ones, SQ[:, k, :], start=(k == 0), stop=(k == KT - 1))
                last.then_inc(sem("pre_sum"), 1)

            def post_norm(n):
                for k in range(KT):
                    if k % 2 == 0:
                        pe.wait_ge(sem("post_sq"), 4 * n + k // 2 + 1)
                    last = mm(psS[:, 0, 0:S], ones, SQ[:, k, :], start=(k == 0), stop=(k == KT - 1))
                last.then_inc(sem("post_sum"), 1)

            def ffn(t0, nf, layer, na=0, n=0):
                def gate_up(i, f):
                    t = t0 + f
                    pe.wait_ge(sem("lo_gu"), i + (t + 1))
                    if t >= 2:
                        pe.wait_ge(sem("act_ready"), i + (t - 1))
                    for u in range(2):
                        out = psG[:, t % 2, u * S:(u + 1) * S]
                        w = WG[f % 2][:, :, u * SLOT:(u + 1) * SLOT]
                        for terms in (((1, 0), (0, 1)), ((0, 0),)):
                            for k in range(KT):
                                if isinstance(i, int) and f == 0 and u == 0:
                                    pe.wait_ge(sem("h_lo"), 8 * layer + k + 1)
                                for g, h in terms:
                                    last = mm(out, w[:, g, k * P:(k + 1) * P], HP[:, h, k, :],
                                              start=(u == 0 and k == 0 and g == 1),
                                              stop=(g == h == 0 and k == KT - 1))
                    last.then_inc(sem("gu_ready"), 1)

                def down(i, f, first=False, final=False):
                    t = t0 + f
                    pe.wait_ge(sem("lo_dn"), i + (t + 1))
                    pe.wait_ge(sem("act_ready"), i + (t + 1))
                    for m in range(KT):
                        for g, h in ((1, 0), (0, 1), (0, 0)):
                            last = mm(psA[:, m // 2, (m % 2) * S:(m % 2 + 1) * S],
                                      WD[f % 3][:, g, m * P:(m + 1) * P], AP[:, t % 2, h, :],
                                      start=(first and m % 2 == 0 and g == 1), stop=final and g == h == 0)
                    last.then_inc(sem("down_done"), 1)

                gate_up(0, 0)
                gate_up(0, 1)
                down(0, 0, first=True)
                whole = (nf - 2) // RING * RING
                if na:
                    with pe.Fori(0, na, RING) as i:
                        for j in range(RING):
                            ada(n, j, i)
                            gate_up(i, 2 + j)
                            down(i, 1 + j)
                if na < whole:
                    with pe.Fori(na, whole, RING) as i:
                        for j in range(RING):
                            gate_up(i, 2 + j)
                            down(i, 1 + j)
                for f in range(2 + whole, nf):
                    gate_up(0, f)
                    down(0, f - 1)
                down(0, nf - 1, final=True)

            def pool():
                c = BASE["pool"]
                arrived(pe, c)
                take_over(pe, "pool")
                for m in range(KT):
                    g, dt = divmod(m, 2)
                    pe.wait_ge(sem("pooled"), g + 1)
                    for k in range(2):
                        a = (g * 4 + dt * 2 + k) * P
                        last = mm(psA[:, m // 2, (m % 2) * S:(m % 2 + 1) * S], chunk(c, a, a + P),
                                  SQ[:, 2 * g + k, :], start=(m % 2 == 0 and k == 0),
                                  stop=(k == 1))
                last.then_inc(chunk_used, 1)

            def attention(n, p, prep, scores, blocks, product, after):
                for u in range(-1, n + 1):
                    if u + 1 < n:
                        prep(u + 1)
                        if u >= 1:
                            pe.wait_ge(sem(p + "exp"), 2 * u)
                        scores(u + 1).then_inc(sem(p + "score"), 1)
                    if 0 <= u - 1:
                        pe.wait_ge(sem(p + "pt"), u)
                        product(u - 1).then_inc(sem(p + "pv"), 1)
                        after(u - 1)
                    if 0 <= u < n:
                        pe.wait_ge(sem(p + "p"), u + 1)
                        if u >= 2:
                            pe.wait_ge(sem(p + "pt"), u - 1)
                        blocks(u).then_inc(sem(p + "tr"), 1)

            def mla():
                c = BASE["mla"]
                take_over(pe, "mla")
                for m in range(4):
                    cc, s = c + m // 3, m % 3
                    arrived(pe, cc)
                    for k in range(KT):
                        if m == 0:
                            pe.wait_ge(h_ready, 8 * 4 + k + 1)
                        last = mm(psA[:, m, 0:S], chunk(cc, s * SLOT + k * P, s * SLOT + k * P + P),
                                  H[:, k, :], start=(k == 0), stop=(k == KT - 1))
                    if m == 2:
                        last.then_inc(chunk_used, 1)
                last.then_inc(sem("mla_lat"), 1)
                pe.wait_ge(sem("mla_sq"), 1)
                for k in range(2):
                    mm(psS[:, 0, 0:S], ones, ROT[:, k, :], start=(k == 0), stop=(k == 1))
                mm(psS[:, 1, 0:S], ones, ROT[:, 2, :], start=True, stop=True).then_inc(sem("mla_sum"), 1)
                pe.wait_ge(sem("mla_cqn"), 1)
                for m in range(12):
                    b = m % 4
                    if m % 4 == 0 and m:
                        pe.wait_ge(sem("mla_q"), m // 4)
                    for k in range(2):
                        j = 2 * m + k
                        cc, a = (c + 1, SLOT + j * P) if j < 16 else (c + 2, (j - 16) * P)
                        if j in (0, 16):
                            arrived(pe, cc)
                        last = mm(psA[:, b, 0:S], chunk(cc, a, a + P), CQN[:, k, :],
                                  start=(k == 0), stop=(k == 1))
                    if m == 7:
                        last.then_inc(chunk_used, 1)
                    if m in (3, 11):
                        last.then_inc(sem("mla_qps"), 1)
                arrived(pe, c + 3)
                pe.wait_ge(sem("mla_q"), 3)
                rot = chunk(c + 3, 2 * SLOT + 512, 2 * SLOT + 640)
                for m in range(4):
                    mm(psA[:, m // 2, (m % 2) * S:(m % 2 + 1) * S], rot, QR[:, m, :],
                       start=(m % 2 == 0), stop=True)
                mm(psG[:, 0, 0:S], rot, LAT[:, 3, :], start=True, stop=True)
                for t in range(TT):
                    last = nc.tensor.transpose(psG[:, 1, t * P:(t + 1) * P], CQN[:, 2, t * P:(t + 1) * P], ident)
                last.then_inc(sem("mla_rot"), 1)
                pe.wait_ge(sem("mla_ready"), 1)

                def prep(h):
                    if h >= 1:
                        pe.wait_ge(sem("mla_ql"), h)
                    a = SLOT + h * P
                    ins = mm(psS[:, 0, 0:S], chunk(c + 2, a, a + P), QN[:, h // 2, :], start=True, stop=True)
                    ins.then_inc(sem("mla_qlps"), 1)

                def scores(h):
                    pe.wait_ge(sem("mla_ql"), h + 1)
                    for t in range(TT):
                        mm(psA[:, h % 2, t * S:(t + 1) * S], QL[:, h % 2, t * P:(t + 1) * P],
                           CQN[:, 2, :], start=(t == 0), stop=False)
                        last = mm(psA[:, h % 2, t * S:(t + 1) * S], QR[:, h // 4, t * P:(t + 1) * P],
                                  KRM[:, h % 4, :], start=False, stop=True)
                    return last

                def blocks(h):
                    for kt in range(TT):
                        for t in range(TT):
                            last = nc.tensor.transpose(
                                psA[:, 2 + h % 2, kt * S + t * P:kt * S + (t + 1) * P],
                                PB[:, h % 2, t * S + kt * P:t * S + (kt + 1) * P], ident)
                    return last

                def product(h):
                    if h >= 2:
                        pe.wait_ge(sem("mla_ol"), h - 1)
                    for kt in range(TT):
                        last = mm(psG[:, h % 2, 0:S], KVTOK[:, kt, :], PTB[:, h % 2, kt * S:(kt + 1) * S],
                                  start=(kt == 0), stop=(kt == 1))
                    return last

                def up(h):
                    if h < 0:
                        return
                    pe.wait_ge(sem("mla_ol"), h + 1)
                    if h % 2 == 0 and h:
                        pe.wait_ge(sem("mla_o"), h // 2)
                    last = mm(psS[:, 1, 0:S], chunk(c + 3, h * P, h * P + P), OL[:, h % 2, :],
                              start=(h % 2 == 0), stop=(h % 2 == 1))
                    last.then_inc(sem("mla_up"), 1)

                attention(HEADS, "mla_", prep, scores, blocks, product, lambda h: up(h - 1))
                up(HEADS - 1)
                pe.wait_ge(sem("mla_up"), HEADS)
                pe.sem_inc(chunk_used, 2)
                pe.wait_ge(sem("mla_o"), HEADS // 2)
                for m in range(KT):
                    cc, s = c + 4 + m // 3, m % 3
                    arrived(pe, cc)
                    for k in range(KT):
                        last = mm(psA[:, m // 2, (m % 2) * S:(m % 2 + 1) * S],
                                  chunk(cc, s * SLOT + k * P, s * SLOT + k * P + P), MO[:, k, :],
                                  start=(m % 2 == 0 and k == 0), stop=(k == KT - 1))
                    if s == 2 or m == KT - 1:
                        last.then_inc(chunk_used, 1)

            def hybrid_in():
                c = BASE["hyb"]
                take_over(pe, "hyb")
                for m in range(40):
                    j = m // 2
                    pe.wait_ge(sem("slot_lo"), m + 1)
                    if m % 2 == 0 and j >= 2:
                        pe.wait_ge(sem("u_out"), j - 1)
                    out, w = psG[:, j % 2, (m % 2) * S:(m % 2 + 1) * S], WS[m % 3]
                    for terms in (((1, 0), (0, 1)), ((0, 0),)):
                        for k in range(KT):
                            if m == 0:
                                pe.wait_ge(sem("hy_lo"), k + 1)
                            for g, h in terms:
                                last = mm(out, w[:, g, k * P:(k + 1) * P], HY[:, h, k, :],
                                          start=(m % 2 == 0 and k == 0 and g == 1),
                                          stop=(g == h == 0 and k == KT - 1))
                    last.then_inc(sem("slot_done"), 1)
                    if m % 3 == 2:
                        pe.sem_inc(chunk_used, 1)
                arrived(pe, c + 13)
                for t in range(TT):
                    for k in range(KT):
                        a = SLOT + k * 32
                        last = mm(psS[:, 0, t * 32:(t + 1) * 32], H[:, k, t * P:(t + 1) * P],
                                  chunk(c + 13, a, a + 32), start=(k == 0), stop=(k == KT - 1))
                last.then_inc(chunk_used, 1)

            def nsa():
                c = BASE["cmp"]
                pe.wait_ge(sem("blocks_ready"), 4)
                for y in range(2):
                    for m in range(2):
                        for l in range(16):
                            s = y * 4 + l // 4
                            cc, a = c + s // 3, (s % 3) * SLOT + (l % 4) * S + m * P
                            if m == 0 and l % 4 == 0:
                                arrived(pe, cc)
                            last = mm(psA[:, y * 2 + m, 0:2 * NCMP], chunk(cc, a, a + P),
                                      BL[y][:, l, :, :].rearrange("p g c -> p (g c)"),
                                      start=(l == 0), stop=(l == 15))
                last.then_inc(sem("cmp_hid"), 1)
                pe.wait_ge(sem("hid_ready"), 1)
                w2 = 2 * SLOT
                arrived(pe, c + 2)
                for g in range(2):
                    for k in range(2):
                        a = w2 + (k * 2 + g) * P
                        mm(psG[:, 0, g * NCMP:(g + 1) * NCMP], chunk(c + 2, a, a + P), HID[:, 0, k, g, :],
                           start=(k == 0), stop=(k == 1))
                for g in range(2):
                    for k in range(2):
                        a = w2 + (4 + k * 2 + g) * P
                        last = mm(psG[0:NCMP, 1, g * P:(g + 1) * P], HID[:, 1, k, g, :], chunk(c + 2, a, a + P),
                                  start=(k == 0), stop=(k == 1))
                last.then_inc(sem("cmp_out"), 1)
                arrived(pe, msk)
                half = mask(M_HALF)
                pe.wait_ge(sem("nsa_sq"), 1)
                for t in range(NSA_T):
                    mm(psA[:, t // 2, (t % 2) * S:(t % 2 + 1) * S], half, SQ[:, t, :],
                       start=(t % 2 == 0), stop=True)
                for y in range(2):
                    mm(psA[:, 2, y * S:(y + 1) * S], half, SQ[:, 4 + y, :],
                       start=(y == 0), stop=True)
                pe.wait_ge(sem("nsa_sqc"), 1)
                mm(psA[:, 3, 0:2 * NCMP], half, SQ[:, 6, 0:2 * NCMP], start=True,
                   stop=True).then_inc(sem("nsa_sum"), 1)
                for y in range(2):
                    for t in range(TT):
                        last = nc.tensor.transpose(psS[:, 1, (y * TT + t) * P:(y * TT + t + 1) * P],
                                                   UKV[:, 2 * y + 1, t * P:(t + 1) * P], ident)
                last.then_inc(sem("nsa_v"), 1)
                pe.wait_ge(sem("nsa_ready"), 1)
                pe.sem_inc(chunk_used, 3)

                def key(y, g):
                    return KGC[:, g, :] if y == 0 else KG[:, y - 1, g, :]

                def scores(u):
                    t, y, g = NSA_UNITS[u]
                    w = NCMP if y == 0 else S
                    for i in range(TT):
                        last = mm(psA[:, u % 2, i * S:i * S + w], UQ[:, t, i * P:(i + 1) * P], key(y, g),
                                  start=(i == 0), stop=True)
                    return last

                def blocks(u):
                    t, y, g = NSA_UNITS[u]
                    if y == 0:
                        for i in range(TT):
                            last = nc.tensor.transpose(psA[0:NCMP, 2 + u % 2, i * P:(i + 1) * P],
                                                       NPB[:, u % 2, i * S:i * S + NCMP], ident)
                        return last
                    for kt in range(TT):
                        for i in range(TT):
                            last = nc.tensor.transpose(
                                psA[:, 2 + u % 2, kt * S + i * P:kt * S + (i + 1) * P],
                                NPB[:, u % 2, i * S + kt * P:i * S + (kt + 1) * P], ident)
                    return last

                def product(u):
                    t, y, g = NSA_UNITS[u]
                    first, final = (y == 0 and g == 0), (y == 2 and g == 1)
                    if first and t >= 2:
                        pe.wait_ge(sem("nsa_o"), t - 1)
                    if y == 0:
                        return mm(psG[:, t % 2, 0:S], VGC[:, g, :], NPTB[0:NCMP, u % 2, 0:S],
                                  start=first, stop=False)
                    for kt in range(TT):
                        last = mm(psG[:, t % 2, 0:S], VG[:, y - 1, kt, g, :],
                                  NPTB[:, u % 2, kt * S:(kt + 1) * S], start=False, stop=(final and kt == 1))
                    return last

                attention(len(NSA_UNITS), "nsa_", lambda u: None, scores, blocks, product, lambda u: None)

            def gdn():
                pe.wait_ge(sem("nsa_o"), NSA_T)
                pe.wait_ge(sem("gdn_g"), 1)
                mm(psS[:, 0, 0:NU], mask(M_TRI), GG, start=True, stop=True).then_inc(sem("gdn_gc"), 1)
                pe.wait_ge(sem("gdn_gu"), 1)
                for b in range(2):
                    last = mm(psG[:, b, :], ones, DEC[:, 4 * b:4 * b + 4, :].rearrange("p u s -> p (u s)"),
                              start=True, stop=True)
                last.then_inc(sem("gdn_row"), 1)
                pe.wait_ge(sem("gdn_sq"), 1)
                pe.wait_ge(sem("nsa_o"), NSA_T)
                for b in range(4):
                    last = mm(psA[:, b, :], ones, SQ[:, 2 * b:2 * b + 2, :].rearrange("p a s -> p (a s)"),
                              start=True, stop=True)
                last.then_inc(sem("gdn_sum"), 1)
                pe.wait_ge(sem("gdn_k"), 1)
                pe.wait_ge(sem("root_ready"), 7 + 6 + 2 + 2 + 2)
                for u in range(NU):
                    h, n = divmod(u, 2)
                    nc.tensor.transpose(psA[:, u // 4, (u % 4) * P:(u % 4 + 1) * P],
                                        KTT[:, h, n * P:(n + 1) * P], ident)
                for u in range(NU):
                    h, n = divmod(u, 2)
                    last = nc.tensor.transpose(psA[:, 2 + u // 4, (u % 4) * P:(u % 4 + 1) * P],
                                               VT[:, h, n * P:(n + 1) * P], ident)
                last.then_inc(sem("gdn_kv"), 1)
                pe.wait_ge(sem("gdn_kvtok"), 1)
                pe.wait_ge(sem("gdn_q"), 1)
                pe.wait_ge(sem("gdn_vb"), 1)
                for u in range(NU):
                    h, n = divmod(u, 2)
                    k = KTT[:, h, n * P:(n + 1) * P]
                    mm(psA[:, u // 4, (u % 4) * P:(u % 4 + 1) * P], k, k, start=(u % 4 == 0),
                       stop=True)
                    last = mm(psA[:, 2 + u // 4, (u % 4) * P:(u % 4 + 1) * P], QT[:, h, n * P:(n + 1) * P], k,
                              start=(u % 4 == 0), stop=True)
                last.then_inc(sem("gdn_gram"), 1)
                pe.wait_ge(sem("gdn_l"), 1)
                for u in range(NU):
                    nc.tensor.transpose(psA[:, u // 4, (u % 4) * P:(u % 4 + 1) * P], L_[:, u, :], ident)
                    last = nc.tensor.transpose(psA[:, 2 + u // 4, (u % 4) * P:(u % 4 + 1) * P],
                                               AT_[:, u, :], ident)
                last.then_inc(sem("gdn_lt"), 1)

                def each(ps, b0, lhs, rhs):
                    for u in range(NU):
                        last = mm(ps[:, b0 + u // 4, (u % 4) * P:(u % 4 + 1) * P], lhs[:, u, :], rhs[:, u, :],
                                  start=(u % 4 == 0), stop=True)
                    return last

                pe.wait_ge(sem("gdn_att"), 1)
                def transpose_inverse():
                    for u in range(NU):
                        last = nc.tensor.transpose(psS[:, u // 4, (u % 4) * P:(u % 4 + 1) * P], TM[:, u, :], ident)
                    last.then_inc(sem("gdn_r"), 1)

                for lev in range(1, 7):
                    pe.wait_ge(sem("gdn_x"), lev + 1)
                    pe.wait_ge(sem("gdn_t"), max(2 * lev - 2, 1))
                    each(psA, 0, XMT, TM).then_inc(sem("gdn_p1"), 1)
                    if lev > 1:
                        transpose_inverse()
                    pe.wait_ge(sem("gdn_p1out"), lev)
                    pe.wait_ge(sem("gdn_t"), 2 * lev - 1)
                    each(psG, 0, TMT, P1).then_inc(sem("gdn_r"), 1)
                pe.wait_ge(sem("gdn_t"), 12)
                transpose_inverse()
                pe.wait_ge(sem("gdn_t"), 13)
                each(psA, 0, KBG, TMT)
                each(psA, 2, TMT, VB).then_inc(sem("gdn_wu"), 1)
                pe.wait_ge(sem("gdn_wuout"), 1)
                for h in range(GH):
                    mm(psG[:, 0, h * P:(h + 1) * P], KDEC[:, 2 * h, :], UU[:, 2 * h, :],
                       start=(h == 0), stop=True)
                    last = mm(psS[:, 0, h * P:(h + 1) * P], UU[:, 2 * h, :], ATT[:, 2 * h, :],
                              start=(h == 0), stop=True)
                last.then_inc(sem("gdn_s1"), 1)
                pe.wait_ge(sem("gdn_state"), 1)
                for h in range(GH):
                    last = mm(psG[:, 1, h * P:(h + 1) * P], WT[:, 2 * h + 1, :], SST[:, h, :],
                              start=(h == 0), stop=True)
                last.then_inc(sem("gdn_ws"), 1)
                pe.wait_ge(sem("gdn_vnew"), 1)
                for h in range(GH):
                    mm(psS[:, 1, h * P:(h + 1) * P], SST[:, h, :], ER[:, 2 * h + 1, :],
                       start=(h == 0), stop=False)
                    last = mm(psS[:, 1, h * P:(h + 1) * P], VNEW[:, h, :], ATT[:, 2 * h + 1, :],
                              start=False, stop=True)
                last.then_inc(sem("gdn_o1"), 1)
                pe.wait_ge(sem("gdn_osq"), 1)
                for b in range(2):
                    last = mm(psA[:, b, :], ones, blk(0)[:, b * 512:(b + 1) * 512], start=True, stop=True)
                last.then_inc(chunk_used, 1)

            def merge():
                c = BASE["mrg"]
                for j in range(24):
                    m, r = divmod(j, 3)
                    pe.wait_ge(sem("slot_lo"), 40 + j + 1)
                    if j == 0:
                        pe.wait_ge(sem("hy_lo"), KT + 1)
                    if j < 3:
                        pe.wait_ge(sem("h_lo"), 4 * KT + r + 1)
                    if j >= 2:
                        pe.wait_ge(sem("mrg_out"), j - 1)
                    w = WM[j % 2]
                    for n, at, x in ((KT, 0, HM), (4, 1, BM[r])):
                        out = psG[:, j % 2, at * S:(at + 1) * S]
                        for terms in (((1, 0), (0, 1)), ((0, 0),)):
                            for k in range(n):
                                for g, h in terms:
                                    a = at * SLOT + k * P
                                    last = mm(out, w[:, g, a:a + P], x[:, h, k, :],
                                              start=(at == 0 and k == 0 and g == 1),
                                              stop=(g == h == 0 and k == n - 1))
                    last.then_inc(sem("mrg_ps"), 1)
                    if j % 2 == 1:
                        pe.sem_inc(chunk_used, 1)
                c = BASE["out"]
                for m in range(KT):
                    cc, s = c + m // 3, m % 3
                    arrived(pe, cc)
                    for k in range(KT):
                        if m == 0 and k == 0:
                            pe.wait_ge(sem("merged"), KT)
                        last = mm(psA[:, m // 2, (m % 2) * S:(m % 2 + 1) * S],
                                  chunk(cc, s * SLOT + k * P, s * SLOT + k * P + P), Y[:, k, :],
                                  start=(m % 2 == 0 and k == 0), stop=(k == KT - 1))
                    if s == 2:
                        last.then_inc(chunk_used, 1)
                last.then_inc(sem("hyb_acc"), 1)

            def router():
                c = BASE["out"] + 2
                for t in range(TT):
                    for k in range(KT):
                        pe.wait_ge(h_ready, 8 * 7 + k + 1)
                        a = 2 * SLOT + k * 36
                        last = mm(psS[:, 1, t * 36:(t + 1) * 36], H[:, k, t * P:(t + 1) * P],
                                  chunk(c, a, a + 36), start=(k == 0), stop=(k == KT - 1))
                last.then_inc(chunk_used, 1)
                for t in range(TT):
                    for k in range(KT):
                        last = nc.tensor.transpose(psA[:, 2 * t + k // 4, (k % 4) * P:(k % 4 + 1) * P],
                                                   H[:, k, t * P:(t + 1) * P], ident)
                last.then_inc(sem("rt_htok"), 1)
                pe.wait_ge(sem("rt_asg"), 1)
                mm(psS[:, 0, 0:E], before, ASG[:, 0, :], start=True, stop=True)
                mm(psS[:, 0, E:2 * E], before, ASG[:, 1, :], start=False, stop=False)
                mm(psS[:, 0, E:2 * E], ones, ASG[:, 0, :], start=False, stop=True).then_inc(sem("rt_cnt"), 1)
                pe.wait_ge(sem("rt_max1"), 1)
                nc.tensor.transpose(psS[0:1, 0, 256:256 + P], blk(22)[:, 128:129], ident).then_inc(sem("rt_max1t"), 1)

            def half(c, g, a=0, n=512):
                a += (g % 6) * 512
                return chunk(c + g // 6, a, a + n)

            def sparse():
                c0 = BASE["moe"]

                def gather(r, p):
                    if p == 0 and isinstance(r, int):
                        pe.wait_ge(sem("sp_sel"), 1)
                        pe.wait_ge(sem("sp_gt"), NP // 2)
                    for b in range(2):
                        for k in range(4 * b, 4 * b + 4):
                            for t in range(TT):
                                off = t * E * CAP + p * P
                                src = SEL[:, off:off + P] if isinstance(r, int) else \
                                    SEL[:, bass.ds(r * (3 * P) + off, P)]
                                last = mm(psG[:, b, (k % 4) * P:(k % 4 + 1) * P], HTOK[:, t, k * P:(k + 1) * P],
                                          src, start=(k % 4 == 0 and t == 0), stop=(t == 1))
                        last.then_inc(sem("sp_ga"), 1)

                def gate_up(r, p):
                    pe.wait_ge(sem("sp_xe"), r * 6 + 2 * (p + 1))
                    c = c0 + 8 * p
                    for u in range(2):
                        for k in range(KT):
                            for e in range(2):
                                g = (u * KT + k) * 2 + e
                                if g % 6 == 0:
                                    arrived(pe, c + g // 6, r * 24)
                                last = mm(psS[64 * e:64 * e + 64, u, :], XE[:, k, e * CAP:(e + 1) * CAP],
                                          half(c, g), start=(k == 0), stop=(k == KT - 1))
                                if g % 6 == 5:
                                    last.then_inc(chunk_used, 1)
                    last.then_inc(sem("sp_gu"), 1)

                def turn(r, p):
                    pe.wait_ge(sem("sp_act"), r * 3 + (p + 1))
                    for f in range(FE):
                        last = nc.tensor.transpose(psS[:, 0, f * P:(f + 1) * P], HACT[:, f * P:(f + 1) * P], ident)
                    last.then_inc(sem("sp_ht"), 1)

                def down(r, p):
                    pe.wait_ge(sem("sp_htout"), r * 3 + (p + 1))
                    c = c0 + 8 * p
                    for h in range(2):
                        if p < NP - 1 or not isinstance(r, int):
                            pe.wait_ge(sem("sp_xe"), r * 6 + (2 * (p + 1) + h + 1))
                        for f in range(FE):
                            for e in range(2):
                                g = 2 * 2 * KT + (h * FE + f) * 2 + e
                                if g % 6 == 0:
                                    arrived(pe, c + g // 6, r * 24)
                                last = mm(psG[64 * e:64 * e + 64, h, :], HT[:, f, e * CAP:(e + 1) * CAP],
                                          half(c, g), start=(f == 0), stop=(f == FE - 1))
                                if g % 6 == 5:
                                    last.then_inc(chunk_used, 1)
                        if h == 0:
                            last.then_inc(sem("sp_dn"), 1)

                def scatter(r, p, final=False):
                    pe.wait_ge(sem("sp_ys"), r * 6 + 2 * (p + 1))
                    for m in range(KT):
                        src = SELGT[:, p * S:(p + 1) * S] if isinstance(r, int) else \
                            SELGT[:, bass.ds(r * (3 * S) + p * S, S)]
                        last = mm(psA[:, m // 2, (m % 2) * S:(m % 2 + 1) * S], YS[:, m * P:(m + 1) * P], src,
                                  start=(isinstance(r, int) and p == 0 and m % 2 == 0), stop=final)
                    return last

                def step(r, p):
                    gate_up(r, p)
                    if p or not isinstance(r, int):
                        scatter(r, p - 1)
                    turn(r, p)
                    if not isinstance(r, int) or p < NP - 1:
                        gather(r, p + 1)
                    down(r, p)

                pe.wait_ge(sem("sp_selg"), 1)
                pe.wait_ge(sem("htok_out"), 1)
                for p in range(NP):
                    b = p // 2
                    if p % 2 == 0 and b >= 2:
                        pe.wait_ge(sem("sp_gt"), b - 1)
                    for t in range(TT):
                        last = nc.tensor.transpose(psG[:, b % 2, ((p % 2) * 2 + t) * P:((p % 2) * 2 + t + 1) * P],
                                                   SELG[:, t * E * CAP + p * P:t * E * CAP + (p + 1) * P], ident)
                    if p % 2 == 1:
                        last.then_inc(sem("sp_gtps"), 1)
                gather(0, 0)
                step(0, 0)
                step(0, 1)
                with pe.Fori(0, 4) as r:
                    for j in range(3):
                        step(r, 2 + j)
                for p in range(14, NP):
                    step(0, p)
                scatter(0, NP - 1, final=True).then_inc(sem("moe_acc"), 1)

            def dense():
                c0, t0 = BASE["moe"], 4 * NF
                for t in range(TT):
                    last = nc.tensor.transpose(psS[0:E, 1, t * P:(t + 1) * P], blk(24)[:, t * E:(t + 1) * E], ident)
                last.then_inc(sem("dn_tr"), 1)
                pe.wait_ge(sem("dn_gt"), 1)
                for j in range(NP):
                    if j >= 2:
                        pe.wait_ge(sem("dn_bc"), j - 1)
                    for i in range(2):
                        e = 2 * j + i
                        last = mm(psG[:, j % 2, i * S:(i + 1) * S], ident[0:E, e:e + 1].to_broadcast([E, P]),
                                  blk(25)[0:E, 0:S], start=(i == 0), stop=True)
                    last.then_inc(sem("dn_ps"), 1)
                pe.wait_ge(sem("dn_bc"), NP)
                pe.wait_ge(sem("htok_out"), 1)

                def step(r, p):
                    c, n = c0 + 8 * p, t0 + 8 * p
                    for i in range(RING):
                        arrived(pe, c + i, r * 24)
                    for j in range(8):
                        e, f = divmod(j, FE)
                        pe.wait_ge(sem("act_ready"), r * 24 + (n + j - 1))
                        for u in range(2):
                            for k in range(KT):
                                last = mm(psG[:, j % 2, u * S:(u + 1) * S],
                                          half(c, (u * KT + k) * 2 + e, f * P, P), H[:, k, :],
                                          start=(u == 0 and k == 0), stop=(k == KT - 1))
                        last.then_inc(sem("gu_ready"), 1)
                    pe.wait_ge(sem("act_ready"), r * 24 + (n + 8))
                    pe.sem_inc(chunk_used, 5)
                    for h in range(2):
                        for f in range(FE):
                            for e in range(2):
                                g = 2 * 2 * KT + (h * FE + f) * 2 + e
                                if g % 6 == 0:
                                    arrived(pe, c + g // 6, r * 24)
                                for m in range(4 * h, 4 * h + 4):
                                    first = isinstance(r, int) and p == 0 and e == f == 0 and m % 2 == 0
                                    last = mm(psA[:, m // 2, (m % 2) * S:(m % 2 + 1) * S],
                                              half(c, g, (m % 4) * P, P), HD[:, e * FE + f, :],
                                              start=first, stop=(e == 1 and f == FE - 1))
                                if g % 6 == 5:
                                    last.then_inc(chunk_used, 1)

                step(0, 0)
                with pe.Fori(0, 5) as r:
                    for j in range(3):
                        step(r, 1 + j)
                pe.wait_ge(chunk_used, NCHUNK)
                pe.sem_inc(sem("moe_acc"), 1)

            pe.sem_inc(sem("down_done"), 1)
            for t in range(ADA[0]):
                ada(0, t)
            pre_norm(0)
            ffn(0, NF, 0, ADA[1], 6)
            post_norm(0)
            pre_norm(1)
            pool()
            post_norm(1)
            pre_norm(2)
            ffn(NF, NF, 1, ADA[2], 24)
            post_norm(2)
            pre_norm(3)
            ffn(2 * NF, NF, 2, ADA[3], 42)
            post_norm(3)
            pre_norm(4)
            mla()
            post_norm(4)
            pre_norm(5)
            ffn(3 * NF, NF, 3)
            post_norm(5)
            pre_norm(6)
            hybrid_in()
            nsa()
            gdn()
            merge()
            pre_norm(7)
            router()
            pe.wait_ge(sem("rt_flag"), 1)
            n = pe.value_load(most[0:1, 0:1], min_val=0, max_val=S)
            with pe.If(n <= CAP):
                sparse()
            with pe.Else():
                dense()
            pe.wait_ge(sem("moe_acc"), 1)

        @block.scalar
        def _(ac):
            A = nc.scalar.activation
            ch = Chain(ac, "act_step")

            def root(dst, ps, scale):
                A(dst, ps, ACT.Sqrt, bias=eps[:, 0:1], scale=scale).then_inc(sem("root_ready"), 1)

            def weight_parts(i, j, c, t, f):
                arrived(ac, c, j)
                if f >= 2:
                    ac.wait_ge(sem("down_done"), i + (t - 1))
                A(WG[f % 2][:, 0, :], chunk(c, 0, 2 * SLOT), ACT.Copy).then_inc(sem("hi_gu"), 1)
                A(WD[f % 3][:, 0, :], chunk(c, 2 * SLOT, CHUNK), ACT.Copy).then_inc(sem("hi_dn"), 1)

            def pre_norm(n, layer=None):
                for b in range(4):
                    ac.wait_ge(x_ready, 4 * n + b + 1)
                    A(SQ[:, 2 * b:2 * b + 2, :], X[:, 2 * b:2 * b + 2, :], ACT.Square).then_inc(sem("pre_sq"), 1)
                if layer is not None:
                    weight_parts(0, 0, BASE[f"ffn{layer}"], NF * layer, 0)
                ac.wait_ge(sem("pre_sum"), n + 1)
                root(rstd[:, :], psS[:, 0, 0:S], 1.0 / D)
                if layer is not None:
                    shift = pre_cols(n)[1]
                    for k in range(KT):
                        ac.wait_ge(h_ready, 8 * n + k + 1)
                        A(HP[:, 0, k, :], H[:, k, :], ACT.Identity, bias=shift(k)).then_inc(sem("h_hi"), 1)
                    weight_parts(0, 0, BASE[f"ffn{layer}"] + 1, NF * layer + 1, 1)

            def post_norm(n):
                for b in range(4):
                    ac.wait_ge(sem("y_ready"), 4 * n + b + 1)
                    A(SQ[:, 2 * b:2 * b + 2, :], Y[:, 2 * b:2 * b + 2, :], ACT.Square).then_inc(sem("post_sq"), 1)
                ac.wait_ge(sem("post_sum"), n + 1)
                root(rstd[:, :], psS[:, 0, 0:S], 1.0 / D)

            def silu(i, t):
                ac.wait_ge(sem("gu_ready"), i + (t + 1))
                if t >= 2:
                    ac.wait_ge(sem("act_ready"), i + (t - 1))
                A(sg[:, t % 2, :], psG[:, t % 2, 0:S], ACT.Silu).then_inc(sem("silu_ready"), 1)

            def ffn(c0, t0, nf, na=0):
                def one(i, f):
                    silu(i, t0 + f)
                    ac.wait_ge(sem("hidden"), i + (t0 + f + 1))
                    A(AP[:, f % 2, 0, :], act[:, f % 2, :], ACT.Copy).then_inc(sem("hidden_hi"), 1)

                whole = (nf - 2) // RING * RING
                if na:
                    with ac.Fori(0, na, RING) as i:
                        for j in range(RING):
                            one(i, j)
                            weight_parts(i, i * 2, c0 + 2 * j + 3, t0 + j + 2, j + 2)
                if na < whole:
                    with ac.Fori(na, whole, RING) as i:
                        for j in range(RING):
                            one(i, j)
                            weight_parts(i, i, c0 + na + j + 2, t0 + j + 2, j + 2)
                for f in range(whole, nf):
                    one(0, f)
                    if f + 2 < nf:
                        weight_parts(0, 0, c0 + na + f + 2, t0 + f + 2, f + 2)

            def attention(n, p, src, dst, width, copy, extra):
                for u in range(-1, n + 1):
                    if u + 1 < n:
                        v = u + 1
                        ac.wait_ge(sem(p + "max"), v + 1)
                        if v >= 2:
                            ac.wait_ge(sem(p + "tr"), v - 1)
                        for t in range(TT):
                            w = width(v)
                            A(dst(v)[:, t * S:t * S + w], src(v)[:, t * S:t * S + w], ACT.Exp,
                              bias=NMAX[:, v % 2, t:t + 1],
                              accum_out=SUM[:, v % 2, t:t + 1]).then_inc(sem(p + "exp"), 1)
                    if 0 <= u < n:
                        ac.wait_ge(sem(p + "tr"), u + 1)
                        if u >= 2:
                            ac.wait_ge(sem(p + "pv"), u - 1)
                        copy(u).then_inc(sem(p + "pt"), 1)
                    extra(u)

            def mla():
                ac.wait_ge(sem("mla_lat"), 1)
                for m in range(4):
                    A(LAT[:, m, :], psA[:, m, 0:S], ACT.Copy)
                for m in range(3):
                    last = A(ROT[:, m, :], psA[:, m, 0:S], ACT.Square)
                last.then_inc(sem("mla_sq"), 1)
                ac.wait_ge(sem("mla_sum"), 1)
                root(rstd[:, :], psS[:, 0, 0:S], 1.0 / 256)
                root(CQN[:, 3, :], psS[:, 1, 0:S], 1.0 / 128)
                for g in range(3):
                    if g < 2:
                        ac.wait_ge(sem("mla_qps"), 1) if g == 0 else ac.wait_ge(chunk_used, BASE["mla"] + 2)
                    else:
                        ac.wait_ge(sem("mla_qps"), 2)
                    for b in range(4):
                        if g < 2:
                            last = A(QN[:, 4 * g + b, :], psA[:, b, 0:S], ACT.Copy)
                        else:
                            last = A(QR[:, b, :], psA[:, b, 0:S], ACT.Copy)
                    last.then_inc(sem("mla_q"), 1)

                def extra(u):
                    if u + 2 < HEADS:
                        query(u + 2)
                    if u >= 1:
                        h = u - 1
                        ac.wait_ge(sem("mla_pv"), h + 1)
                        if h >= 2:
                            ac.wait_ge(sem("mla_up"), h - 1)
                        A(OL[:, h % 2, :], psG[:, h % 2, 0:S], ACT.Copy).then_inc(sem("mla_ol"), 1)

                def query(h):
                    ac.wait_ge(sem("mla_qlps"), h + 1)
                    if h >= 2:
                        ac.wait_ge(sem("mla_score"), h - 1)
                    A(QL[:, h % 2, :], psS[:, 0, 0:S], ACT.Copy, scale=MLA_SCALE).then_inc(sem("mla_ql"), 1)

                query(0)
                attention(HEADS, "mla_", lambda u: psA[:, u % 2, :], lambda u: PB[:, u % 2, :], lambda u: S,
                          lambda u: A(PTB[:, u % 2, :], psA[:, 2 + u % 2, :], ACT.Copy), extra)

            def hybrid_in():
                dst = [UA[:, 2 * j:2 * j + 2] for j in range(6)] + [UQ[:, 0:2], UQ[:, 2:4]]
                dst += [UK[:, 0:2], UK[:, 2:4], UKV[:, 0:2], UKV[:, 2:4]]
                dst += [UG[:, 2 * j:2 * j + 2] for j in range(6)] + [UZ[:, 0:2], UZ[:, 2:4]]
                c = BASE["hyb"]

                def high(m):
                    arrived(ac, c + m // 3)
                    A(WS[m % 3][:, 0, :], chunk(c + m // 3, (m % 3) * SLOT, (m % 3 + 1) * SLOT), ACT.Copy)\
                        .then_inc(sem("slot_hi"), 1)

                for m in range(3):
                    high(m)
                for k in range(KT):
                    ac.wait_ge(h_ready, 8 * 6 + k + 1)
                    A(HY[:, 0, k, :], H[:, k, :], ACT.Copy).then_inc(sem("hy_hi"), 1)
                for m in range(40):
                    ac.wait_ge(sem("slot_done"), m + 1)
                    if m + 3 < 40 and m % 2 == 0:
                        high(m + 3)
                    if m % 2 == 0:
                        continue
                    j = m // 2
                    src = psG[:, j % 2, :].rearrange("p (a s) -> p a s", a=2)
                    if j in (8, 9):
                        A(dst[j][0:64], src[0:64], ACT.Copy)
                        A(dst[j][64:P, :, 0:S - 1], src[64:P, :, 1:S], ACT.Copy).then_inc(sem("u_out"), 1)
                    else:
                        A(dst[j], src, ACT.Silu if j >= 18 else ACT.Copy).then_inc(sem("u_out"), 1)
                    if m + 3 < 40:
                        high(m + 3)
                ac.wait_ge(chunk_used, BASE["hyb"] + 14)
                ch.link(A(GT, psS[:, 0, 0:64].rearrange("p (t c) -> p t c", t=2), ACT.Copy), "gt_out")
                A(GATE, GT[:, :, 0:24], ACT.Sigmoid).then_inc(sem("gate_sig"), 1)
                beta = BETA.rearrange("p (t h) -> p t h", t=2)
                A(beta, GT[:, :, 24:28], ACT.Sigmoid).then_inc(sem("beta_ready"), 1)

            def nsa():
                A(SQ[:, 0:4, :], UQ, ACT.Square)
                ch.link(A(SQ[:, 4:6, :], UKV[:, 0:3:2, :], ACT.Square), "nsa_sq")
                ac.wait_ge(sem("cmp_hid"), 1)
                A(HID.rearrange("p y m g c -> p (y m) (g c)"), psA[:, :, 0:2 * NCMP],
                  ACT.Gelu_apprx_tanh).then_inc(sem("hid_ready"), 1)
                ac.wait_ge(sem("cmp_out"), 1)
                A(SQ[:, 6, 0:2 * NCMP], psG[:, 0, 0:2 * NCMP], ACT.Square).then_inc(sem("nsa_sqc"), 1)

                ac.wait_ge(sem("nsa_sum"), 1)
                root(SQ[:, 0:6, :].rearrange("p (b a) s -> p b (a s)", a=2), psA[:, 0:3, :], 1.0 / 64)
                root(SQ[:, 6, 0:2 * NCMP], psA[:, 3, 0:2 * NCMP], 1.0 / 64)
                ac.wait_ge(sem("gdn_z"), 1)
                A(AL, col("a_log", 0, 4), ACT.Exp)
                ch.link(A(EGC, GX, ACT.Abs))
                ch.link(A(EGC, EGC, ACT.Exp, scale=-1.0))
                A(EGC, EGC, ACT.Ln, bias=ones[:, 0:1]).then_inc(sem("gdn_ln"), 1)
                ac.wait_ge(sem("gdn_conv"), 12)
                ch.link(A(blk(23, 3), blk(23, 3), ACT.Silu), "gdn_cv")

                def copy(u):
                    if NSA_UNITS[u][1] == 0:
                        return A(NPTB[0:NCMP, u % 2, 0:S], psA[0:NCMP, 2 + u % 2, 0:S], ACT.Copy)
                    return A(NPTB[:, u % 2, :], psA[:, 2 + u % 2, :], ACT.Copy)

                def extra(u):
                    if u >= 1 and u % 6 == 0:
                        ac.wait_ge(sem("nsa_pv"), u)
                        t = u // 6 - 1
                        A(YN[:, t, :], psG[:, t % 2, 0:S], ACT.Copy).then_inc(sem("nsa_o"), 1)

                attention(len(NSA_UNITS), "nsa_", lambda u: NPB[:, u % 2, :], lambda u: NPB[:, u % 2, :],
                          lambda u: NCMP if NSA_UNITS[u][1] == 0 else S, copy, extra)

            def gdn():
                ac.wait_ge(sem("nsa_o"), NSA_T)
                A(blk(2, 2), blk(23, 2), ACT.Square).then_inc(sem("gdn_sq"), 1)
                ac.wait_ge(sem("gdn_sum"), 1)
                for b in (1, 0):
                    root(blk(2 + b).rearrange("p (b n) -> p b n", b=2), psA[:, 2 * b:2 * b + 2, :], 1.0)
                ac.wait_ge(sem("gdn_diff"), 1)
                A(ER.rearrange("p u s -> p (u s)").rearrange("p (b n) -> p b n", b=2), psG[:, :, :],
                  ACT.Exp).then_inc(sem("gdn_er"), 1)
                A(blk(22), blk(22), ACT.Exp, scale=-1.0)
                A(EGC, GC, ACT.Exp)
                A(KD, GX, ACT.Exp).then_inc(sem("gdn_exps"), 1)
                ac.wait_ge(sem("gdn_kv"), 1)
                for u in range(NU):
                    h, n = divmod(u, 2)
                    last = A(VB[:, u, :], psA[:, 2 + u // 4, (u % 4) * P:(u % 4 + 1) * P], ACT.Copy,
                             scale=unit_col(BETA, h, n))
                last.then_inc(sem("gdn_vb"), 1)
                ac.wait_ge(sem("gdn_lt"), 1)
                A(blk(18).rearrange("p (b n) -> p b n", b=2), psA[:, 0:2, :], ACT.Copy).then_inc(sem("gdn_ltout"), 1)
                A(blk(6).rearrange("p (b n) -> p b n", b=2), psA[:, 2:4, :], ACT.Copy).then_inc(sem("gdn_att"), 1)
                for lev in range(1, 7):
                    ac.wait_ge(sem("gdn_p1"), lev)
                    A(blk(11).rearrange("p (b n) -> p b n", b=2), psA[:, 0:2, :], ACT.Copy)\
                        .then_inc(sem("gdn_p1out"), 1)
                ac.wait_ge(sem("gdn_wu"), 1)
                A(blk(0).rearrange("p (b n) -> p b n", b=2), psA[:, 0:2, :], ACT.Copy)
                A(blk(1).rearrange("p (b n) -> p b n", b=2), psA[:, 2:4, :], ACT.Copy).then_inc(sem("gdn_wuout"), 1)
                ac.wait_ge(sem("gdn_o1"), 1)
                A(OT[:, :, 0, :], psS[:, 0, :].rearrange("p (h s) -> p h s", h=GH), ACT.Copy)
                ch.link(A(OT[:, :, 1, :], psS[:, 1, :].rearrange("p (h s) -> p h s", h=GH), ACT.Copy))
                A(blk(0), blk(3), ACT.Square).then_inc(sem("gdn_osq"), 1)
                ac.wait_ge(chunk_used, msk + 1)
                root(blk(0).rearrange("p (b n) -> p b n", b=2), psA[:, 0:2, :], 1.0 / P)

            def merge():
                def high(j):
                    c, s = BASE["mrg"] + j // 2, j % 2
                    arrived(ac, c)
                    A(WM[j % 2][:, 0, 0:SLOT], chunk(c, s * SLOT, (s + 1) * SLOT), ACT.Copy)
                    a = 2 * SLOT + s * 512
                    A(WM[j % 2][:, 0, SLOT:SLOT + 512], chunk(c, a, a + 512), ACT.Copy).then_inc(sem("slot_hi"), 1)

                ac.wait_ge(chunk_used, msk + 1)
                high(0)
                A(HM[:, 0], H[:, :, :], ACT.Copy).then_inc(sem("hy_hi"), 1)
                for r, y in enumerate((YA, YN, YG)):
                    if r == 2:
                        ac.wait_ge(sem("yg_ready"), 1)
                    A(BM[r][:, 0], y, ACT.Copy).then_inc(sem("h_hi"), 1)
                high(1)
                for j in range(24):
                    m, r = divmod(j, 3)
                    ac.wait_ge(sem("mrg_ps"), j + 1)
                    if j >= 2:
                        ac.wait_ge(sem("mrg_out"), j - 1)
                    A(sg[:, j % 2, :], psG[:, j % 2, 0:S], ACT.Sigmoid,
                      bias=col("b_gate", 8 * r + m)).then_inc(sem("mrg_sig"), 1)
                    if j + 2 < 24:
                        high(j + 2)

            def router():
                ac.wait_ge(sem("rt_htok"), 1)
                A(HTOK.rearrange("p t (b n) -> p (t b) n", b=2), psA[:, :, :], ACT.Copy).then_inc(sem("htok_out"), 1)
                ac.wait_ge(sem("rt_max"), 1)
                A(blk(24)[:, 256:264], blk(24)[:, 256:264], ACT.Exp)
                A(blk(24)[:, 128:192], blk(24)[:, 128:192], ACT.Exp).then_inc(sem("rt_exp"), 1)

            def sparse():
                for b in range(NP // 2):
                    ac.wait_ge(sem("sp_gtps"), b + 1)
                    A(SELGT[:, b * 512:(b + 1) * 512], psG[:, b % 2, :], ACT.Copy).then_inc(sem("sp_gt"), 1)
                with ac.Fori(0, NP) as p:
                    ac.wait_ge(sem("sp_gu"), p + 1)
                    A(HSIL, psS[:, 0, :], ACT.Silu).then_inc(sem("sp_si"), 1)
                    ac.wait_ge(sem("sp_ht"), p + 1)
                    A(HT.rearrange("p f s -> p (f s)"), psS[:, 0, :], ACT.Copy).then_inc(sem("sp_htout"), 1)

            def dense():
                for j in range(NP):
                    ac.wait_ge(sem("dn_ps"), j + 1)
                    A(GB[:, j * 512:(j + 1) * 512], psG[:, j % 2, :], ACT.Copy).then_inc(sem("dn_bc"), 1)
                with ac.Fori(0, E * FE, 2) as i:
                    silu(i, 4 * NF)
                    silu(i, 4 * NF + 1)

            ac.wait_ge(sem("cols_in"), 16)
            A(silc[:, :], col("c", 0, 8), ACT.Silu).then_inc(sem("silc_ready"), 1)
            pre_norm(0, 0)
            ffn(BASE["ffn0"], 0, NF, ADA[1])
            post_norm(0)
            pre_norm(1)
            post_norm(1)
            pre_norm(2, 1)
            ffn(BASE["ffn1"], NF, NF, ADA[2])
            post_norm(2)
            pre_norm(3, 2)
            ffn(BASE["ffn2"], 2 * NF, NF, ADA[3])
            post_norm(3)
            pre_norm(4)
            mla()
            post_norm(4)
            pre_norm(5, 3)
            ffn(BASE["ffn3"], 3 * NF, NF)
            post_norm(5)
            pre_norm(6)
            hybrid_in()
            nsa()
            gdn()
            merge()
            pre_norm(7)
            router()
            ac.wait_ge(sem("rt_flag"), 1)
            n = ac.value_load(most[0:1, 0:1], min_val=0, max_val=S)
            with ac.If(n <= CAP):
                sparse()
            with ac.Else():
                dense()
            ac.wait_ge(sem("moe_acc"), 1)

        @block.vector
        def _(ve):
            V = nc.vector
            ch = Chain(ve, "dve_step")
            link = ch.link

            def ada(n, c, t, i=0, free=True):
                arrived(ve, c, i if isinstance(i, int) else i * 2)
                if free:
                    ve.wait_ge(sem("ada_sum"), i + (n + t - 1))
                out = ADP[:, (n + t) % 2]
                w = chunk(c).rearrange("p (m k n) -> p m k n", m=3, k=KT)
                V.tensor_scalar(out, w[:, :, 0, :], silc[:, 0:1], None, ALU.mult).then_inc(sem("ada_step"), 1)
                for k in range(1, KT):
                    ve.wait_ge(sem("ada_step"), i * (KT - 1) + ((n + t) * (KT - 1) + k))
                    V.scalar_tensor_tensor(out, w[:, :, k, :], silc[:, k:k + 1], out, ALU.mult, ALU.add)\
                        .then_inc(sem("ada_step" if k < KT - 1 else "ada_prod"), 1)

            def weight_parts(i, c, t, f):
                ve.wait_ge(sem("hi_gu"), i + (t + 1))
                V.tensor_tensor(WG[f % 2][:, 1, :], chunk(c, 0, 2 * SLOT), WG[f % 2][:, 0, :],
                                ALU.subtract).then_inc(sem("lo_gu"), 1)

            def mod_out(layer, a, n):
                link(V.tensor_tensor(mod[:, layer, a:a + n], psS[:, 1, 0:n],
                                     col("ada_b", 72 * layer + a, n), ALU.add))
                for s in range(3):
                    for q, out in ((1, modA), (2, modC)):
                        end = 24 * s + 8 * q + 8
                        if a < end <= a + n:
                            link(V.scalar_tensor_tensor(out[:, layer, s, :], mod[:, layer, end - 8:end], 1.0,
                                                        col("norm_g", 48 * layer + 16 * s + 8 * (q - 1), 8),
                                                        ALU.add, ALU.mult))
                            if q == 2 and s != 1:
                                link(V.tensor_scalar(out[:, layer, s, :], out[:, layer, s, :], 0.5, None, ALU.mult))

            roots = Chain(ve, "root_used")

            def root(dst):
                n = roots.n.get("root_used", 0) + 1
                ve.wait_ge(sem("root_ready"), n)
                roots.link(V.reciprocal(dst, dst))

            def pre_norm(n, layer=None):
                if layer is not None:
                    weight_parts(0, BASE[f"ffn{layer}"], NF * layer, 0)
                root(rstd[:, :])
                scale, shift = pre_cols(n)
                if layer is not None or shift is None:
                    for k in range(KT):
                        V.scalar_tensor_tensor(H[:, k, :], X[:, k, :], scale(k), rstd[:, :],
                                               ALU.mult, ALU.mult).then_inc(h_ready, 1)
                else:
                    for b in range(2):
                        link(V.tensor_tensor(H[:, 4 * b:4 * b + 4, :], X[:, 4 * b:4 * b + 4, :],
                                             rstd[:, None, :].to_broadcast([P, 4, S]), ALU.mult))
                        for k in range(4 * b, 4 * b + 4):
                            V.tensor_scalar(H[:, k, :], H[:, k, :], scale(k), shift(k),
                                            ALU.mult, ALU.add).then_inc(h_ready, 1)
                if layer is not None:
                    for k in range(KT):
                        ve.wait_ge(sem("h_hi"), 8 * layer + k + 1)
                        V.scalar_tensor_tensor(HP[:, 1, k, :], H[:, k, :], shift(k), HP[:, 0, k, :],
                                               ALU.add, ALU.subtract).then_inc(sem("h_lo"), 1)
                    weight_parts(0, BASE[f"ffn{layer}"] + 1, NF * layer + 1, 1)

            def post_norm(n, done, layer, s, from_acc=True):
                if from_acc:
                    ve.wait_ge(*done)
                    for b in range(4):
                        V.tensor_copy(Y[:, 2 * b:2 * b + 2, :], psA[:, b, :].rearrange("p (a s) -> p a s", a=2))\
                            .then_inc(sem("y_ready"), 1)
                root(rstd[:, :])

                def scaled(b):
                    for k in range(2 * b, 2 * b + 2):
                        last = V.scalar_tensor_tensor(Y[:, k, :], Y[:, k, :], modC[:, layer, s, k:k + 1],
                                                      rstd[:, :], ALU.mult, ALU.mult)
                    last.then_inc(sem("y_scaled"), 1)

                scaled(0)
                for b in range(4):
                    if b < 3:
                        scaled(b + 1)
                    ve.wait_ge(sem("y_scaled"), 4 * n + b + 1)
                    V.tensor_tensor(X[:, 2 * b:2 * b + 2, :], X[:, 2 * b:2 * b + 2, :], Y[:, 2 * b:2 * b + 2, :],
                                    ALU.add).then_inc(x_ready, 1)
                ve.wait_ge(x_ready, 4 * n + 8)

            def ffn(c0, t0, nf, na=0, n=0):
                def hidden(i, f):
                    ve.wait_ge(sem("silu_ready"), i + (t0 + f + 1))
                    V.tensor_tensor(act[:, f % 2, :], sg[:, f % 2, :], psG[:, f % 2, S:2 * S],
                                    ALU.mult).then_inc(sem("hidden"), 1)

                def low(i, f):
                    ve.wait_ge(sem("hidden_hi"), i + (t0 + f + 1))
                    V.tensor_tensor(AP[:, f % 2, 1, :], act[:, f % 2, :], AP[:, f % 2, 0, :],
                                    ALU.subtract).then_inc(sem("act_ready"), 1)

                whole = (nf - 2) // RING * RING
                if na:
                    with ve.Fori(0, na, RING) as i:
                        for j in range(RING):
                            hidden(i, j)
                            ada(n, c0 + 2 + 2 * j, j, i)
                            low(i, j)
                            weight_parts(i, c0 + 2 * j + 3, t0 + j + 2, j + 2)
                if na < whole:
                    with ve.Fori(na, whole, RING) as i:
                        for j in range(RING):
                            hidden(i, j)
                            low(i, j)
                            weight_parts(i, c0 + na + j + 2, t0 + j + 2, j + 2)
                for f in range(whole, nf):
                    hidden(0, f)
                    low(0, f)
                    if f + 2 < nf:
                        weight_parts(0, c0 + na + f + 2, t0 + f + 2, f + 2)

            def sparse():
                iot = iota[:, None, :].to_broadcast([P, E, CAP])
                for t in range(TT):
                    sel = SEL[:, t * E * CAP:(t + 1) * E * CAP].rearrange("p (e s) -> p e s", s=CAP)
                    last = V.tensor_tensor(sel, iot, POS[:, t, :, None].to_broadcast([P, E, CAP]), ALU.is_equal)
                link(last, "sp_sel")
                for t in range(TT):
                    sel = SEL[:, t * E * CAP:(t + 1) * E * CAP].rearrange("p (e s) -> p e s", s=CAP)
                    selg = SELG[:, t * E * CAP:(t + 1) * E * CAP].rearrange("p (e s) -> p e s", s=CAP)
                    gate = blk(24)[:, t * E:(t + 1) * E][:, :, None].to_broadcast([P, E, CAP])
                    last = V.tensor_tensor(selg, sel, gate, ALU.mult)
                link(last, "sp_selg")

                def hidden(p):
                    ve.wait_ge(sem("sp_si"), p + 1)
                    V.tensor_tensor(HACT, HSIL, psS[:, 1, :], ALU.mult).then_inc(sem("sp_act"), 1)

                def xe(p):
                    for b in range(2):
                        ve.wait_ge(sem("sp_ga"), p * 2 + (b + 1))
                        V.tensor_copy(XE[:, 4 * b:4 * b + 4, :].rearrange("p k s -> p (k s)"), psG[:, b, :])\
                            .then_inc(sem("sp_xe"), 1)

                def ys(p):
                    ve.wait_ge(sem("sp_dn"), p + 1)
                    V.tensor_copy(YS[:, 0:512], psG[:, 0, :]).then_inc(sem("sp_ys"), 1)
                    ve.wait_ge(chunk_used, p * 8 + (BASE["moe"] + 8))
                    V.tensor_copy(YS[:, 512:1024], psG[:, 1, :]).then_inc(sem("sp_ys"), 1)

                xe(0)
                with ve.Fori(0, NP - 1) as p:
                    hidden(p)
                    xe(p + 1)
                    ys(p)
                hidden(NP - 1)
                ys(NP - 1)

            def dense():
                ve.wait_ge(sem("dn_tr"), 1)
                V.tensor_copy(blk(25)[0:E, 0:S], psS[0:E, 1, 0:S]).then_inc(sem("dn_gt"), 1)
                ve.wait_ge(sem("dn_bc"), NP)
                with ve.Fori(0, NP) as p:
                    for j in range(8):
                        t = 4 * NF + j
                        ve.wait_ge(sem("silu_ready"), p * 8 + (t + 1))
                        V.tensor_tensor(sg[:, t % 2, :], sg[:, t % 2, :],
                                        GB[:, bass.ds(p * (2 * S) + (j // FE) * S, S)], ALU.mult)\
                            .then_inc(sem("gated"), 1)
                        ve.wait_ge(sem("gated"), p * 8 + (j + 1))
                        V.tensor_tensor(HD[:, j, :], sg[:, t % 2, :], psG[:, t % 2, S:2 * S],
                                        ALU.mult).then_inc(sem("act_ready"), 1)

            def pool():
                c = BASE["pool"]
                arrived(ve, c)
                w = S + 16
                pa = blk(4, 3)[:, 0:8 * w].rearrange("p (k s) -> p k s", s=w)
                pb = blk(7, 3)[:, 0:8 * w].rearrange("p (k s) -> p k s", s=w)
                for pad in (pa, pb):
                    V.memset(pad[:, :, 0:8], 0.0)
                    last = V.memset(pad[:, :, 8 + S:w], 0.0)
                link(last)
                V.tensor_copy(pb[:, :, 8:9], H[:, :, 0:1])
                V.tensor_copy(pb[:, :, 8 + S:9 + S], H[:, :, S - 1:S])
                link(V.tensor_tensor(pb[:, :, 9:8 + S], H[:, :, 0:S - 1], H[:, :, 1:S], ALU.add))
                link(V.tensor_tensor(pa[:, 2:8, 1:w - 1], pb[:, 2:8, 0:w - 2], pb[:, 2:8, 2:w], ALU.add))
                link(V.tensor_tensor(pb[:, 4:8, 2:w - 2], pa[:, 4:8, 0:w - 4], pa[:, 4:8, 4:w], ALU.add))
                link(V.tensor_tensor(pa[:, 6:8, 4:w - 4], pb[:, 6:8, 0:w - 8], pb[:, 6:8, 8:w], ALU.add))
                for g in range(4):
                    src = (pb, pa, pb, pa)[g]
                    inv = chunk(c, 2048 + g * S, 2048 + (g + 1) * S)
                    link(V.tensor_tensor(SQ[:, 2 * g:2 * g + 2, :], src[:, 2 * g:2 * g + 2, 8:8 + S],
                                         inv[:, None, :].to_broadcast([P, 2, S]), ALU.mult))
                    V.tensor_tensor(SQ[:, 2 * g:2 * g + 2, :], SQ[:, 2 * g:2 * g + 2, :], H[:, 2 * g:2 * g + 2, :],
                                    ALU.subtract).then_inc(sem("pooled"), 1)
                ve.wait_ge(chunk_used, c + 1)
                for m in range(KT):
                    last = V.tensor_scalar(Y[:, m, :], psA[:, m // 2, (m % 2) * S:(m % 2 + 1) * S],
                                           col("pool_b", m), col("pool_scale", m), ALU.add, ALU.mult)
                    if m % 2 == 1:
                        last.then_inc(sem("y_ready"), 1)

            def attention(n, p, first, finish):
                for u in range(-1, n):
                    if u + 1 < n:
                        v = u + 1
                        ve.wait_ge(sem(p + "score"), v + 1)
                        first(v)
                    if u >= 0:
                        ve.wait_ge(sem(p + "exp"), 2 * u + 2)
                        finish(u)

            def negate_max(src, u, name):
                link(V.tensor_reduce(FAC[:, u % 2, :], src, AX.X, ALU.max))
                link(V.tensor_scalar(NMAX[:, u % 2, :], FAC[:, u % 2, :], -1.0, None, ALU.mult), name)

            def mla():
                c = BASE["mla"]
                root(rstd[:, :])
                for k in range(2):
                    V.scalar_tensor_tensor(CQN[:, k, :], LAT[:, k, :], col("q_norm", k), rstd[:, :],
                                           ALU.mult, ALU.mult)
                root(CQN[:, 3, :])
                link(V.scalar_tensor_tensor(CQN[:, 2, :], LAT[:, 2, :], col("kv_norm", 0), CQN[:, 3, :],
                                            ALU.mult, ALU.mult), "mla_cqn")
                ve.wait_ge(sem("mla_rot"), 1)
                arrived(ve, c + 3)
                cos = chunk(c + 3, 2 * SLOT, 2 * SLOT + S)
                sin = chunk(c + 3, 2 * SLOT + S, 2 * SLOT + 2 * S)
                link(V.tensor_tensor(ROT, psA[:, 0:2, :].rearrange("p b (a s) -> p (b a) s", a=2),
                                     sin[:, None, :].to_broadcast([P, 4, S]), ALU.mult))
                link(V.tensor_tensor(QR, QR, cos[:, None, :].to_broadcast([P, 4, S]), ALU.mult))
                link(V.tensor_tensor(QR, QR, ROT, ALU.add))
                link(V.tensor_scalar(QR, QR, MLA_SCALE, None, ALU.mult))
                link(V.tensor_tensor(ROT[:, 0, :], psG[:, 0, 0:S], sin, ALU.mult))
                link(V.tensor_tensor(LAT[:, 3, :], LAT[:, 3, :], cos, ALU.mult))
                link(V.tensor_tensor(LAT[:, 3, :], LAT[:, 3, :], ROT[:, 0, :], ALU.add))
                link(V.memset(KRM, 0.0))
                for j in range(4):
                    V.tensor_copy(KRM[32 * j:32 * j + 32, j, :], LAT[32 * j:32 * j + 32, 3, :])
                link(V.tensor_copy(KVTOK, psG[:, 1, 0:S].rearrange("p (t c) -> p t c", t=2)), "mla_ready")

                def first(u):
                    negate_max(psA[:, u % 2, :].rearrange("p (t s) -> p t s", t=2), u, "mla_max")

                def finish(u):
                    link(V.reciprocal(FAC[:, u % 2, :], SUM[:, u % 2, :]))
                    for t in range(TT):
                        last = V.tensor_scalar(PB[:, u % 2, t * S:(t + 1) * S], PB[:, u % 2, t * S:(t + 1) * S],
                                               FAC[:, u % 2, t:t + 1], None, ALU.mult)
                    last.then_inc(sem("mla_p"), 1)
                    if u % 2 == 1 and u >= 3:
                        out(u - 2)

                def out(h):
                    ve.wait_ge(sem("mla_up"), h + 1)
                    V.tensor_copy(MO[:, h // 2, :], psS[:, 1, 0:S]).then_inc(sem("mla_o"), 1)

                attention(HEADS, "mla_", first, finish)
                out(HEADS - 1)

            def hybrid_in():
                c = BASE["hyb"]
                for k in range(KT):
                    ve.wait_ge(sem("hy_hi"), k + 1)
                    V.tensor_tensor(HY[:, 1, k, :], H[:, k, :], HY[:, 0, k, :], ALU.subtract)\
                        .then_inc(sem("hy_lo"), 1)
                link(V.tensor_scalar(col("qk_gain", 0), col("qk_gain", 0), 64 ** -0.5, None, ALU.mult))
                for m in range(40):
                    ve.wait_ge(sem("slot_hi"), m + 1)
                    V.tensor_tensor(WS[m % 3][:, 1, :], chunk(c + m // 3, (m % 3) * SLOT, (m % 3 + 1) * SLOT),
                                    WS[m % 3][:, 0, :], ALU.subtract).then_inc(sem("slot_lo"), 1)
                    if m == 15:
                        ve.wait_ge(sem("u_out"), 6)
                        link(V.tensor_tensor(UA[:, 4:8, :], UA[:, 4:8, :], UA[:, 8:12, :], ALU.mult))
                    if m in (16, 17, 18, 19):
                        taps(m - 16)
                    if m == 20:
                        link(V.tensor_tensor(YA, UA[:, 0:4, :], UA[:, 8:12, :], ALU.mult))
                    if m >= 28:
                        gdn_taps(m - 28)
                    if m in (24, 25, 26, 27):
                        ve.wait_ge(sem("u_out"), 10)
                        y, g = divmod(m - 24, 2)
                        V.tensor_tensor(BL[y][:, :, g, :], windows(UK[:, 2 * y + g, :]),
                                        col("pe", 16 * y, 16)[:, :, None].to_broadcast([P, 16, NCMP]),
                                        ALU.add).then_inc(sem("blocks_ready"), 1)

            def gdn_taps(k):
                ve.wait_ge(sem("u_out"), 12 + k // 2 + 1)
                for d in range(4):
                    w = col("conv_g", 12 * (3 - d) + k)
                    if d == 0:
                        link(V.tensor_scalar(CV[:, k, :], UG[:, k, :], w, None, ALU.mult))
                    else:
                        ins = V.scalar_tensor_tensor(CV[:, k, d:S], UG[:, k, 0:S - d], w, CV[:, k, d:S],
                                                     ALU.mult, ALU.add)
                        if d < 3:
                            link(ins)
                ins.then_inc(sem("gdn_conv"), 1)

            def taps(k):
                for d in range(3):
                    w = col("conv_a", 4 * (2 - d) + k)
                    if d == 0:
                        link(V.tensor_scalar(UA[:, 8 + k, :], UA[:, 4 + k, :], w, None, ALU.mult))
                    else:
                        link(V.scalar_tensor_tensor(UA[:, 8 + k, d:S], UA[:, 4 + k, 0:S - d], w,
                                                    UA[:, 8 + k, d:S], ALU.mult, ALU.add))

            def windows(base):
                a = list(base.ap)
                return bass.AP(tensor=base.tensor, offset=base.offset, ap=[list(a[0]), [2, 16], [16, NCMP]])

            def nsa():
                ve.wait_ge(sem("cmp_out"), 1)
                arrived(ve, msk)
                V.tensor_copy(VGC, psG[0:NCMP, 1, 0:2 * P].rearrange("p (g c) -> p g c", g=2))
                z3 = GX.rearrange("p (t h) -> p t h", t=2)
                dt3 = col("dt", 0, 4)[:, None, :].to_broadcast([P, 2, 4])
                link(V.tensor_tensor(z3, GT[:, :, 28:32], dt3, ALU.add), "gdn_z")
                link(V.tensor_scalar(GG, GX, 0.0, None, ALU.max))
                root(SQ[:, 0:6, :])
                root(SQ[:, 6, 0:2 * NCMP])
                link(V.scalar_tensor_tensor(UQ, UQ, col("qk_gain", 0), SQ[:, 0:4, :], ALU.mult, ALU.mult))
                ve.wait_ge(sem("lo_dn"), 4 * NF + 2)
                for y in range(2):
                    for g in range(2):
                        half_ = slice(64 * g, 64 * g + 64)
                        V.scalar_tensor_tensor(KG[half_, y, g, :], UKV[half_, 2 * y, :],
                                               col("qk_gain", 2 + y)[half_], SQ[half_, 4 + y, :],
                                               ALU.mult, ALU.mult)
                V.scalar_tensor_tensor(KGC, psG[:, 0, 0:2 * NCMP].rearrange("p (g c) -> p g c", g=2),
                                       col("qk_gain", 1),
                                       SQ[:, 6, 0:2 * NCMP].rearrange("p (g c) -> p g c", g=2),
                                       ALU.mult, ALU.mult)
                ve.wait_ge(sem("nsa_v"), 1)
                for y in range(2):
                    for g in range(2):
                        V.tensor_copy(VG[:, y, :, g, 64 * g:64 * g + 64],
                                      psS[:, 1, y * S:(y + 1) * S].rearrange("p (t c) -> p t c", t=2)
                                      [:, :, 64 * g:64 * g + 64])
                ve.wait_ge(sem("gate_sig"), 1)
                for t in range(TT):
                    last = V.tensor_scalar(GATE[:, t, 0:8], GATE[:, t, 0:8], mask(M_OK + t, 1), None, ALU.mult)
                link(last, "nsa_ready")

                def first(u):
                    t, y, g = NSA_UNITS[u]
                    w = NCMP if y == 0 else S
                    slope = 2.0 ** (-(g * 4 + t + 1))
                    v3 = lambda a: a.rearrange("p (t s) -> p t s", t=2)[:, :, 0:w]
                    nd = mask(M_OK + 2, 2 * NCMP).rearrange("p (t s) -> p t s", t=2) if y == 0 else \
                        v3(mask(M_ND, 512))
                    if u >= 2:
                        ve.wait_ge(sem("nsa_tr"), u - 1)
                    link(V.scalar_tensor_tensor(v3(NPB[:, u % 2, :]), nd, slope, v3(psA[:, u % 2, :]),
                                                ALU.mult, ALU.add))
                    negate_max(v3(NPB[:, u % 2, :]), u, "nsa_max")

                def finish(u):
                    t, y, g = NSA_UNITS[u]
                    w = NCMP if y == 0 else S
                    link(V.reciprocal(FAC[:, u % 2, :], SUM[:, u % 2, :]))
                    link(V.tensor_tensor(FAC[:, u % 2, :], FAC[:, u % 2, :], GATE[:, :, y * 8 + g * 4 + t], ALU.mult))
                    for i in range(TT):
                        last = V.tensor_scalar(NPB[:, u % 2, i * S:i * S + w], NPB[:, u % 2, i * S:i * S + w],
                                               FAC[:, u % 2, i:i + 1], None, ALU.mult)
                    last.then_inc(sem("nsa_p"), 1)

                attention(len(NSA_UNITS), "nsa_", first, finish)

            def gdn():
                ve.wait_ge(sem("nsa_o"), NSA_T)
                ve.wait_ge(sem("gdn_ln"), 1)
                link(V.tensor_tensor(GG, GG, EGC, ALU.add))
                g3 = GG.rearrange("p (t h) -> p t h", t=2)
                link(V.tensor_tensor(g3, g3, AL[:, None, :].to_broadcast([P, 2, 4]), ALU.mult))
                link(V.tensor_scalar(GG, GG, -1.0, None, ALU.mult), "gdn_g")
                for u in range(NU):
                    h, n = divmod(u, 2)
                    last = V.tensor_scalar(DEC[:, u, :], mask(M_TRI), unit_col(GG, h, n), None, ALU.mult)
                link(last, "gdn_gu")
                ve.wait_ge(sem("gdn_gc"), 1)
                link(V.tensor_copy(GC, psS[:, 0, 0:NU]))
                ve.wait_ge(sem("gdn_row"), 1)
                row = psG[:, :, :].rearrange("p b (u s) -> p (b u) s", u=4)
                for u in range(NU):
                    h, n = divmod(u, 2)
                    V.tensor_scalar(DEC[:, u, :], row[:, u, :], unit_col(GC, h, n), 0.0, ALU.subtract, ALU.max)
                rl = RL.rearrange("p (n h) -> p h n", n=2)
                link(V.tensor_copy(rl, row[:, :, P - 1:P].rearrange("p (h n) o -> p h (n o)", n=2)))
                link(V.tensor_tensor(GX, RL, GC, ALU.subtract), "gdn_diff")
                root(blk(3))
                link(V.tensor_tensor(blk(24), blk(24), blk(3), ALU.mult), "gdn_k")
                root(blk(2))
                link(V.scalar_tensor_tensor(blk(23), blk(23), P ** -0.5, blk(2), ALU.mult, ALU.mult), "gdn_q")
                ve.wait_ge(sem("gdn_exps"), 1)
                ve.wait_ge(sem("beta_ready"), 1)
                link(V.tensor_tensor(DEC, DEC, mask(M_TRIL)[:, None, :].to_broadcast([P, NU, P]), ALU.mult))
                link(V.tensor_tensor(BG, BETA, EGC, ALU.mult))
                ve.wait_ge(sem("gdn_kv"), 1)
                for u in range(NU):
                    h, n = divmod(u, 2)
                    k = psA[:, u // 4, (u % 4) * P:(u % 4 + 1) * P]
                    V.tensor_scalar(KBG[:, u, :], k, unit_col(BG, h, n), None, ALU.mult)
                    last = V.tensor_scalar(KDEC[:, u, :], k, unit_col(KD, h, n), None, ALU.mult)
                link(last, "gdn_kvtok")
                ve.wait_ge(sem("gdn_gram"), 1)
                for u in range(NU):
                    h, n = divmod(u, 2)
                    V.scalar_tensor_tensor(L_[:, u, :], psA[:, u // 4, (u % 4) * P:(u % 4 + 1) * P],
                                           unit_col(BETA, h, n), DEC[:, u, :], ALU.mult, ALU.mult)
                link(V.tensor_tensor(AT_, psA[:, 2:4, :].rearrange("p b (u s) -> p (b u) s", u=4), DEC, ALU.mult))
                link(V.tensor_tensor(L_, L_, mask(M_STRICT)[:, None, :].to_broadcast([P, NU, P]), ALU.mult), "gdn_l")
                ve.wait_ge(sem("gdn_er"), 1)
                rl2 = GX.rearrange("p (n h) -> p h n", n=2)
                link(V.tensor_copy(rl2, ER[:, :, P - 1:P].rearrange("p (h n) o -> p h (n o)", n=2)))
                link(V.tensor_tensor(ER, ER, blk(23).rearrange("p (u s) -> p u s", u=NU), ALU.mult))
                idb = ident[:, None, :].to_broadcast([P, NU, P])
                ve.wait_ge(sem("gdn_x"), 1)
                V.tensor_tensor(TM, idb, XM, ALU.subtract)
                link(V.tensor_tensor(TMT, idb, XMT, ALU.subtract), "gdn_t")
                def transposed():
                    link(V.tensor_copy(TMT, psS[:, :, :].rearrange("p b (u s) -> p (b u) s", u=4)), "gdn_t")

                for lev in range(1, 7):
                    if lev > 1:
                        ve.wait_ge(sem("gdn_r"), 2 * lev - 2)
                        transposed()
                    ve.wait_ge(sem("gdn_r"), 2 * lev - 1)
                    link(V.tensor_tensor(TM, TM, psG[:, :, :].rearrange("p b (u s) -> p (b u) s", u=4),
                                         ALU.subtract), "gdn_t")
                ve.wait_ge(sem("gdn_r"), 12)
                transposed()
                ve.wait_ge(sem("gdn_s1"), 1)
                link(V.tensor_copy(SST, psG[:, 0, :].rearrange("p (h s) -> p h s", h=GH)), "gdn_state")
                ve.wait_ge(sem("gdn_ws"), 1)
                link(V.tensor_tensor(VNEW, UU[:, 1:NU:2, :], psG[:, 1, :].rearrange("p (h s) -> p h s", h=GH),
                                     ALU.subtract), "gdn_vnew")
                root(blk(0))
                link(V.scalar_tensor_tensor(blk(3), blk(3), col("out_gain", 0), blk(0), ALU.mult, ALU.mult))
                link(V.tensor_tensor(blk(15), blk(3), blk(13), ALU.mult), "yg_ready")

            def merge():
                def low(j):
                    c, s = BASE["mrg"] + j // 2, j % 2
                    a = 2 * SLOT + s * 512
                    ve.wait_ge(sem("slot_hi"), 40 + j + 1)
                    w = WM[j % 2]
                    V.tensor_tensor(w[:, 1, 0:SLOT], chunk(c, s * SLOT, (s + 1) * SLOT), w[:, 0, 0:SLOT],
                                    ALU.subtract)
                    V.tensor_tensor(w[:, 1, SLOT:SLOT + 512], chunk(c, a, a + 512), w[:, 0, SLOT:SLOT + 512],
                                    ALU.subtract).then_inc(sem("slot_lo"), 1)

                low(0)
                for r, y in enumerate((YA, YN, YG)):
                    ve.wait_ge(sem("h_hi"), 4 * KT + r + 1)
                    V.tensor_tensor(BM[r][:, 1], y, BM[r][:, 0], ALU.subtract).then_inc(sem("h_lo"), 1)
                low(1)
                for j in range(24):
                    m, r = divmod(j, 3)
                    ve.wait_ge(sem("mrg_sig"), j + 1)
                    ps = psG[:, j % 2, S:2 * S]
                    if r == 0:
                        link(V.tensor_tensor(Y[:, m, :], sg[:, j % 2, :], ps, ALU.mult), "mrg_out")
                    else:
                        link(V.tensor_tensor(act[:, 0, :], sg[:, j % 2, :], ps, ALU.mult), "mrg_out")
                        link(V.tensor_tensor(Y[:, m, :], Y[:, m, :], act[:, 0, :], ALU.add),
                             "merged" if r == 2 else None)
                    if j + 2 < 24:
                        low(j + 2)
                ve.wait_ge(sem("hyb_acc"), 1)
                add_acc()

            def add_acc():
                for b in range(4):
                    V.tensor_tensor(X[:, 2 * b:2 * b + 2, :], X[:, 2 * b:2 * b + 2, :],
                                    psA[:, b, :].rearrange("p (a s) -> p a s", a=2), ALU.add).then_inc(x_ready, 1)

            def router():
                w = blk(24)
                LG = w[:, 192:192 + 72]
                lg3 = w[:, 192:264]
                G3 = w[:, 0:64].rearrange("p (t e) -> p t e", t=2)
                LE = w[:, 128:192].rearrange("p (t e) -> p t e", t=2)
                EXL = w[:, 256:264].rearrange("p (t e) -> p t e", t=2)
                LGT = w[:, 264:336].rearrange("p (t e) -> p t e", t=2)
                OH = w[:, 336:344].rearrange("p (t e) -> p t e", t=2)
                T1 = w[:, 384:448].rearrange("p (t e) -> p t e", t=2)
                O1 = w[:, 448:512].rearrange("p (t e) -> p t e", t=2)
                O2 = w[:, 512:576].rearrange("p (t e) -> p t e", t=2)
                W4 = w[:, 576:580]
                W32 = w[:, 584:616]
                Z = w[:, 640:656].rearrange("p (i t o) -> p i t o", i=8, t=2)
                for i in range(32):
                    V.memset(W32[:, i:i + 1], float(32 - i))
                for i in range(4):
                    V.memset(W4[:, i:i + 1], float(4 - i))
                ve.wait_ge(chunk_used, BASE["out"] + 3)
                rt = psS[:, 1, 0:72].rearrange("p (t c) -> p t c", t=2)
                b36 = col("b_rt", 0, 36)[:, None, :].to_broadcast([P, 2, 36])
                link(V.tensor_tensor(LGT, rt, b36, ALU.add))

                def first_max(src, weights, out, best, n):
                    link(V.tensor_reduce(Z[:, best], src, AX.X, ALU.max))
                    link(V.tensor_tensor(out, src, Z[:, best].to_broadcast([P, 2, n]), ALU.is_equal))
                    link(V.tensor_tensor(out, out, weights[:, None, :].to_broadcast([P, 2, n]), ALU.mult))
                    link(V.tensor_reduce(Z[:, 7], out, AX.X, ALU.max))
                    link(V.tensor_tensor(out, out, Z[:, 7].to_broadcast([P, 2, n]), ALU.is_equal))

                first_max(LGT[:, :, 0:4], W4, OH, 0, 4)
                link(V.tensor_tensor(EXL, LGT[:, :, 0:4], Z[:, 0].to_broadcast([P, 2, 4]), ALU.subtract))
                for t in range(2):
                    o4 = OH[:, t, :][:, :, None].to_broadcast([P, 4, 8])
                    le = LGT[:, t, 4:36].rearrange("p (g e) -> p g e", g=4)
                    link(V.tensor_tensor(LE[:, t, :].rearrange("p (g e) -> p g e", g=4), le, o4, ALU.mult))
                    link(V.tensor_scalar(OH[:, t, :], OH[:, t, :], 1.0, 1e30, ALU.subtract, ALU.mult))
                    link(V.tensor_tensor(LE[:, t, :].rearrange("p (g e) -> p g e", g=4),
                                         LE[:, t, :].rearrange("p (g e) -> p g e", g=4), o4, ALU.add))
                link(V.tensor_reduce(Z[:, 1], LE, AX.X, ALU.max))
                link(V.tensor_tensor(LE, LE, Z[:, 1].to_broadcast([P, 2, 32]), ALU.subtract), "rt_max")
                ve.wait_ge(sem("rt_exp"), 1)
                link(V.tensor_reduce(Z[:, 2], EXL, AX.X, ALU.add))
                first_max(LE, W32, O1, 3, 32)
                link(V.scalar_tensor_tensor(T1, O1, -2.0, LE, ALU.mult, ALU.add))
                first_max(T1, W32, O2, 4, 32)
                link(V.tensor_tensor(ASG, O1, O2, ALU.add), "rt_asg")
                link(V.tensor_tensor(Z[:, 5], Z[:, 3], Z[:, 4], ALU.add))
                link(V.tensor_tensor(Z[:, 5], Z[:, 5], Z[:, 2], ALU.mult))
                link(V.reciprocal(Z[:, 5], Z[:, 5]))
                link(V.tensor_tensor(Z[:, 3], Z[:, 3], Z[:, 5], ALU.mult))
                link(V.tensor_tensor(Z[:, 4], Z[:, 4], Z[:, 5], ALU.mult))
                link(V.tensor_tensor(O1, O1, Z[:, 3].to_broadcast([P, 2, 32]), ALU.mult))
                link(V.tensor_tensor(O2, O2, Z[:, 4].to_broadcast([P, 2, 32]), ALU.mult))
                link(V.tensor_tensor(G3, O1, O2, ALU.add), "rt_gate")
                ve.wait_ge(sem("rt_cnt"), 1)
                link(V.tensor_tensor(POS, ASG, psS[:, 0, 0:2 * E].rearrange("p (t e) -> p t e", t=2), ALU.mult))
                link(V.tensor_reduce(blk(22)[:, 128:129], blk(22)[:, 64:128], AX.X, ALU.max), "rt_max1")
                link(V.tensor_scalar(POS, POS, -1.0, None, ALU.add))
                ve.wait_ge(sem("rt_max1t"), 1)
                link(V.tensor_reduce(blk(22)[0:1, 130:131], psS[0:1, 0, 256:256 + P], AX.X, ALU.max))
                link(V.tensor_copy(most[0:1, 0:1], blk(22)[0:1, 130:131]), "rt_flag")

            V.memset(eps[:, :], EPS)
            ve.wait_ge(sem("cols_in"), 16)
            ve.wait_ge(sem("x_in"), 16)
            link(V.memset(st[:, :], 0.0))
            ve.sem_inc(x_ready, 4)
            ve.wait_ge(sem("silc_ready"), 1)
            for t in range(ADA[0]):
                ada(0, t, t, 0, t >= 2)
            ve.wait_ge(sem("ada_sum"), ADA[0])
            mod_out(0, 0, 18)
            pre_norm(0, 0)
            ffn(BASE["ffn0"], 0, NF, ADA[1], 6)
            ve.wait_ge(sem("ada_sum"), 24)
            mod_out(0, 18, 54)
            post_norm(0, (sem("down_done"), NF + 1), 0, 0)
            pre_norm(1)
            ve.wait_ge(h_ready, 16)
            pool()
            post_norm(1, None, 0, 1, from_acc=False)
            pre_norm(2, 1)
            ffn(BASE["ffn1"], NF, NF, ADA[2], 24)
            ve.wait_ge(sem("ada_sum"), 42)
            mod_out(1, 0, 54)
            post_norm(2, (sem("down_done"), 2 * NF + 1), 0, 2)
            pre_norm(3, 2)
            ffn(BASE["ffn2"], 2 * NF, NF, ADA[3], 42)
            ve.wait_ge(sem("ada_sum"), 48)
            mod_out(1, 54, 18)
            post_norm(3, (sem("down_done"), 3 * NF + 1), 1, 0)
            pre_norm(4)
            mla()
            post_norm(4, (chunk_used, BASE["mla"] + 7), 1, 1)
            pre_norm(5, 3)
            ffn(BASE["ffn3"], 3 * NF, NF)
            post_norm(5, (sem("down_done"), 4 * NF + 1), 1, 2)
            pre_norm(6)
            hybrid_in()
            nsa()
            gdn()
            merge()
            pre_norm(7)
            router()
            n = ve.value_load(most[0:1, 0:1], min_val=0, max_val=S)
            with ve.If(n <= CAP):
                sparse()
            with ve.Else():
                dense()
            ve.wait_ge(sem("moe_acc"), 1)
            add_acc()

        @block.gpsimd
        def _(po):
            def ada(n, t, i=0):
                po.wait_ge(sem("ada_prod"), i + (n + t + 1))
                po.sem_inc(chunk_used, 1)

            def weight_parts(i, c, t, f):
                po.wait_ge(sem("hi_dn"), i + (t + 1))
                nc.gpsimd.tensor_tensor(WD[f % 3][:, 1, :], chunk(c, 2 * SLOT, CHUNK), WD[f % 3][:, 0, :],
                                        ALU.subtract).then_inc(sem("lo_dn"), 1)
                po.wait_ge(sem("lo_dn"), i + (t + 1))
                po.wait_ge(sem("lo_gu"), i + (t + 1))
                po.sem_inc(chunk_used, 1)

            def ffn(c0, t0, nf, na=0, n=0):
                for f in range(2):
                    weight_parts(0, c0 + f, t0 + f, f)
                whole = (nf - 2) // RING * RING
                if na:
                    with po.Fori(0, na, RING) as i:
                        for j in range(RING):
                            ada(n, j, i)
                            weight_parts(i, c0 + 2 * j + 3, t0 + j + 2, j + 2)
                if na < whole:
                    with po.Fori(na, whole, RING) as i:
                        for j in range(RING):
                            weight_parts(i, c0 + na + j + 2, t0 + j + 2, j + 2)
                for f in range(2 + whole, nf):
                    weight_parts(0, c0 + na + f, t0 + f, f)

            for t in range(ADA[0]):
                ada(0, t)
            for layer, n in enumerate((6, 24, 42, 48)):
                if layer in (1, 3):
                    take_over(po, f"ffn{layer}")
                ffn(BASE[f"ffn{layer}"], NF * layer, NF, (ADA + [0])[layer + 1], n)
            po.wait_ge(sem("slot_done"), 40)
            nc.gpsimd.memset(KG, 0.0).then_inc(sem("lo_dn"), 1)
            nc.gpsimd.memset(VG, 0.0).then_inc(sem("lo_dn"), 1)
            for lev in range(7):
                if lev == 0:
                    po.wait_ge(sem("gdn_l"), 1)
                    arrived(po, msk)
                else:
                    if lev == 1:
                        po.wait_ge(sem("gdn_t"), 1)
                    else:
                        po.wait_ge(sem("gdn_p1"), lev - 1)
                upp = mask(M_UPP + lev * P)[:, None, :].to_broadcast([P, NU, P])
                if lev == 0:
                    low = mask(M_LOW)[:, None, :].to_broadcast([P, NU, P])
                    nc.gpsimd.tensor_tensor(XM, L_, low, ALU.mult)
                    po.wait_ge(sem("gdn_ltout"), 1)
                nc.gpsimd.tensor_tensor(XMT, LT, upp, ALU.mult).then_inc(sem("gdn_x"), 1)
            po.wait_ge(sem("hy_hi"), KT + 1)
            nc.gpsimd.tensor_tensor(HM[:, 1], H[:, :, :], HM[:, 0], ALU.subtract).then_inc(sem("hy_lo"), 1)


def _slots(w):
    import numpy as np
    k, m = w.shape
    w = w.reshape(k // P, P, m // P, P).transpose(2, 1, 0, 3)
    return [np.ascontiguousarray(w[i]).reshape(P, -1) for i in range(m // P)]


def _pack_stream(a):
    import numpy as np
    out = np.zeros((NCHUNK, P, CHUNK), np.float32)

    def put(name, parts, at=0):
        c, w = BASE[name], at
        for p in parts:
            n = p.shape[1]
            while n:
                q, o = divmod(w, CHUNK)
                k = min(n, CHUNK - o)
                out[c + q, :p.shape[0], o:o + k] = p[:, p.shape[1] - n:p.shape[1] - n + k]
                w, n = w + k, n - k

    ada = np.stack(_slots(a["ada_w"][0]) + _slots(a["ada_w"][1])).reshape(-1, 3, P, SLOT)
    ada = ada.transpose(0, 2, 1, 3).reshape(-1, P, CHUNK)
    out[0:ADA[0]] = ada[0:ADA[0]]
    for j in range(3):
        a0 = sum(ADA[:j + 1])
        for t in range(ADA[j + 1]):
            out[BASE[f"ffn{j}"] + 2 + 2 * t] = ada[a0 + t]
    for j in range(4):
        w_in, w_out = a["ffn_w_in"][j // 2, j % 2], a["ffn_w_out"][j // 2, j % 2]
        up = w_in.reshape(KT, P, 2, NF, P)
        at = [BASE[f"ffn{j}"] + ffn_pos(f, ADA[j + 1] if j < 3 else 0) for f in range(NF)]
        both = up.transpose(3, 1, 2, 0, 4).reshape(NF, P, 2 * SLOT)
        out[at] = np.concatenate([both, w_out.reshape(NF, P, SLOT)], axis=2)
    pw = a["pool_w"][0].reshape(4, 2, P, 2, P).transpose(2, 0, 3, 1, 4).reshape(P, 2048)
    t = np.arange(S)
    inv = np.stack([1.0 / (np.clip(t + w // 2, 0, S) - np.clip(t - w // 2, 0, S)) for w in (2, 4, 8, 16)])
    put("pool", [pw, np.broadcast_to(inv.astype(np.float32).reshape(1, -1), (P, 1024))])

    w = a["mla_w_in"][0]
    w = np.concatenate([w[:, :384]] + [w[:, 384:416]] * 4, axis=1)
    uq = a["mla_w_uq"][0]
    uq = np.concatenate([uq[:, :, :64].reshape(256, 1024), uq[:, :, 64:].reshape(256, 512)], axis=1)
    uq = uq.reshape(2, P, 12, P).transpose(1, 2, 0, 3).reshape(P, 24 * P)
    uk = np.zeros((P, HEADS, P), np.float32)
    uv = np.zeros((P, HEADS, P), np.float32)
    for h in range(HEADS):
        b = 64 * (h % 2)
        uk[b:b + 64, h, :] = a["mla_w_uk"][0][:, h, :].T
        uv[:, h, b:b + 64] = a["mla_w_uv"][0][:, h, :]
    ang = np.arange(S, dtype=np.float32)[None, :] * \
        (1.0 / (np.float32(10000.0) ** (np.arange(0, 32, 2, dtype=np.float32) / 32)))[:, None].astype(np.float32)
    cos = np.tile(np.cos(ang).astype(np.float32), (8, 1))
    sin = np.tile(np.sin(ang).astype(np.float32), (8, 1))
    rot = np.zeros((P, P), np.float32)
    for p in range(P):
        if p % 32 < 16:
            rot[p + 16, p] = -1.0
        else:
            rot[p - 16, p] = 1.0
    put("mla", _slots(w) + [uq, uk.reshape(P, -1), uv.reshape(P, -1), cos, sin, rot])
    put("mla", _slots(a["mla_w_o"][0]), 4 * CHUNK)

    w = a["w_in_2"][0]
    ua, uq_, ukv, ung, ugq, uz, ub, uaa = np.split(w, np.cumsum([1536, 512, 768, 24, 1536, 512, 4]), axis=1)
    uq_ = uq_.reshape(D, 2, 4, 64).transpose(0, 2, 1, 3).reshape(D, 512)
    kv = ukv.reshape(D, 6, 2, 64)
    dup = [kv[:, y, g] for y in (0, 1) for g in (0, 1) for _ in (0, 1)]
    rest = [kv[:, y].reshape(D, P) for y in range(2, 6)]
    big = np.concatenate([ua, uq_] + dup + rest + [ugq, uz], axis=1)
    small = np.concatenate([ung, ub, uaa], axis=1).reshape(KT, P, 32).transpose(1, 0, 2).reshape(P, 256)
    put("hyb", _slots(big) + [small])

    w1 = a["cmp_w1_2"][0].reshape(2, 16, P, 256).transpose(0, 2, 1, 3).reshape(2, P, 4096)
    w2 = np.zeros((2, P, 2, 2, P), np.float32)
    for g in range(2):
        w2[:, :, :, g, 64 * g:64 * g + 64] = a["cmp_w2_2"][0].reshape(2, 2, P, 64).transpose(0, 2, 1, 3)
    put("cmp", [w1[0], w1[1], w2[0].reshape(P, 512), w2[1].reshape(P, 512)])

    m = np.zeros((P, CHUNK), np.float32)
    q = np.arange(P)
    for i in range(TT):
        dist = (q + P * i)[:, None] - np.arange(S)[None, :]
        m[:, i * S:(i + 1) * S] = np.where(dist >= 0, -dist, -1e33)
        dc = (q + P * i)[:, None] - (np.arange(NCMP) * 16 + 31)[None, :]
        m[:, M_OK + 2 + i * NCMP:M_OK + 2 + (i + 1) * NCMP] = np.where(dc >= 0, -dc, -1e33)
        m[:, M_OK + i] = (dc >= 0).any(axis=1)
    for lev in range(7):
        b = 1 << lev
        low = (q[:, None] // (2 * b) == q[None, :] // (2 * b)) & (q[:, None] // b % 2 == 1) & (q[None, :] // b % 2 == 0)
        m[:, M_LOW + lev * P:M_LOW + (lev + 1) * P] = low
        m[:, M_UPP + lev * P:M_UPP + (lev + 1) * P] = low.T
    m[:, M_STRICT:M_STRICT + P] = q[:, None] > q[None, :]
    m[:, M_TRIL:M_TRIL + P] = q[:, None] >= q[None, :]
    m[:, M_HALF:M_HALF + P] = q[:, None] // 64 == q[None, :] // 64
    m[:, M_TRI:M_TRI + P] = q[:, None] <= q[None, :]
    put("msk", [m])

    gate = a["w_gate_2"][0].reshape(KT, P, 3, KT, P)
    br = a["w_branch_2"][0].reshape(3, 512, D).copy()
    br[1] = br[1].reshape(2, 4, 64, D).transpose(1, 0, 2, 3).reshape(512, D)
    br = br.reshape(3, 4, P, KT, P)
    for j in range(24):
        mt, r = divmod(j, 3)
        c, s = BASE["mrg"] + j // 2, j % 2
        out[c, :, s * SLOT:(s + 1) * SLOT] = gate[:, :, r, mt].transpose(1, 0, 2).reshape(P, SLOT)
        out[c, :, 2 * SLOT + s * 512:2 * SLOT + s * 512 + 512] = br[r, :, :, mt].transpose(1, 0, 2).reshape(P, 512)
    wr = np.concatenate([a["w_router_group_2"][0], a["w_router_expert_2"][0]], axis=1)
    put("out", _slots(a["w_out_2"][0]) + [wr.reshape(KT, P, 36).transpose(1, 0, 2).reshape(P, 288)])
    o = out[BASE["moe"]:].reshape(NP, 8, P, 6, 512)
    gate, up = (a[n][0].reshape(E, KT, P, FE * P) for n in ("w_expert_gate_2", "w_expert_up_2"))
    down = a["w_expert_down_2"][0].reshape(E, FE, P, 2, 512)
    for e in range(2):
        for k in range(KT):
            for u, w in enumerate((gate, up)):
                g = (u * KT + k) * 2 + e
                o[:, g // 6, :, g % 6] = w[e::2, k]
        for h in range(2):
            for f in range(FE):
                g = 4 * KT + (h * FE + f) * 2 + e
                o[:, g // 6, :, g % 6] = down[e::2, f, :, h]
    return out


def _pack_cols(a):
    import numpy as np
    out = np.zeros((P, NCOL), np.float32)

    def put(name, v):
        i, j = COLS[name]
        out[:, i:j] = v

    def by_channel(v):
        return v.reshape(-1, P).T

    put("c", by_channel(a["c"]))
    put("ada_b", by_channel(a["ada_b"]))
    put("norm_g", by_channel(a["norm_g"]))
    for name, key in (("pool_b", "pool_b"), ("pool_scale", "pool_scale"), ("norm_mix", "norm_mix_2"),
                      ("norm_ffn", "norm_ffn_2"), ("b_gate", "b_gate_2"), ("q_norm", "mla_q_norm"),
                      ("kv_norm", "mla_kv_norm"), ("conv_a", "conv_a_w_2"), ("conv_g", "gdn_conv_w_2"),
                      ("out_gain", "gdn_out_gain_2")):
        put(name, by_channel(a[key]))
    put("qk_gain", np.concatenate([a["nsa_qk_gain_2"][0].T] * 2, axis=0))
    put("pe", a["cmp_pe_2"][0].reshape(2, 16, P).transpose(2, 0, 1).reshape(P, 32))
    put("b_rt", np.concatenate([a["b_router_group_2"][0], a["b_router_expert_2"][0]])[None, :])
    put("a_log", a["gdn_a_log_2"][0][None, :])
    put("dt", a["gdn_dt_bias_2"][0][None, :])
    return out


def _consts():
    import numpy as np
    q = np.arange(P)
    return np.concatenate([np.eye(P), np.ones((P, P)), q[:, None] <= q[None, :],
                           np.broadcast_to(np.arange(CAP), (P, CAP))], axis=1).astype(np.float32)


def kernel(**inputs):
    import numpy as np
    import concourse.bacc as bacc
    from concourse.bass_utils import run_bass_kernel_spmd as run

    a = {k: np.asarray(v) for k, v in inputs.items()}
    arrays = {
        "stream": _pack_stream(a),
        "cols_in": _pack_cols(a),
        "consts": _consts(),
        "x_in": np.ascontiguousarray(a["x"][0].T.reshape(KT, P, S).transpose(1, 0, 2)),
    }
    nc = bacc.Bacc("TRN2", target_bir_lowering=False, num_devices=1)
    args = [nc.dram_tensor(n, v.shape, F32, kind="ExternalInput").ap() for n, v in arrays.items()]
    out = nc.dram_tensor("x_out", (P, KT, S), F32, kind="ExternalOutput").ap()
    build(nc, *args, out)
    r = run(nc, [arrays], core_ids=[0])
    y = np.asarray(r.results[0]["x_out"])
    return np.ascontiguousarray(y.transpose(1, 0, 2).reshape(D, S).T)[None]
```
